# Optimizing a Trainium2 kernel written in Bass

```python
import jax, jax.numpy as jnp
from jax import lax
import numpy as np

D_MODEL = 1024
BATCH = 1
SEQ = 256
DEPTH = 1
DEC_BATCH = 8
DEC_SEQ = 1
PAST_LEN = 2048
PAGE_SIZE = 128

N_MEM = 256
SSM_HEADS = 16
SSM_HEAD_DIM = 64
SSM_INNER = SSM_HEADS * SSM_HEAD_DIM
SSM_STATE = 128
SSM_GROUPS = 4
SSM_CONV = 4
SSM_CONV_DIM = SSM_INNER + 2 * SSM_GROUPS * SSM_STATE
SSD_CHUNK = 128
SC_WIDTH = D_MODEL
SC_CONV = 3
IN_PROJ_DIM = SSM_INNER + SSM_CONV_DIM + SSM_HEADS + 3 * SC_WIDTH + 2 * D_MODEL
XA_HEADS = 4
XA_HEAD_DIM = D_MODEL // XA_HEADS
N_EXPERTS = 32
TOP_K = 4
D_FF = D_MODEL
SWIGLU_LIMIT = 7.0
SWIGLU_ALPHA = 1.702
MOE_BLOCK = 128
EPS = 1e-6

kernel_name = 'hybrid_ssd_shortconv_memxattn_moe_step'

def rmsnorm(x, g):
    xf = x.astype(jnp.float32)
    y = xf * lax.rsqrt(jnp.mean(xf * xf, axis=-1, keepdims=True) + EPS)
    return (y * g.astype(jnp.float32)).astype(x.dtype)

def causal_dwconv(buf, u, w, bias):
    k_width = w.shape[0]
    t_len = u.shape[1]
    full = jnp.concatenate([buf.astype(u.dtype), u], axis=1)
    out = sum(full[:, k:k + t_len, :] * w[k] for k in range(k_width))
    if bias is not None:
        out = out + bias
    return out, full[:, full.shape[1] - (k_width - 1):, :]

def ssd_chunked(xs, dt, a, bs, cs):
    b, seq_len = xs.shape[:2]
    q = SSD_CHUNK
    pad = (-seq_len) % q
    if pad:
        xs = jnp.pad(xs, ((0, 0), (0, pad), (0, 0), (0, 0)))
        dt = jnp.pad(dt, ((0, 0), (0, pad), (0, 0)))
        bs = jnp.pad(bs, ((0, 0), (0, pad), (0, 0), (0, 0)))
        cs = jnp.pad(cs, ((0, 0), (0, pad), (0, 0), (0, 0)))
    n_chunks = (seq_len + pad) // q
    rep = SSM_HEADS // SSM_GROUPS
    bh = jnp.repeat(bs, rep, axis=2).reshape(b, n_chunks, q, SSM_HEADS, SSM_STATE)
    ch = jnp.repeat(cs, rep, axis=2).reshape(b, n_chunks, q, SSM_HEADS, SSM_STATE)
    xdt = (xs * dt[..., None]).reshape(b, n_chunks, q, SSM_HEADS, SSM_HEAD_DIM)
    a_cum = jnp.cumsum((dt * a).reshape(b, n_chunks, q, SSM_HEADS), axis=2)
    seg = a_cum[:, :, :, None, :] - a_cum[:, :, None, :, :]
    mask = jnp.tril(jnp.ones((q, q), dtype=bool))[None, None, :, :, None]
    decay = jnp.exp(jnp.where(mask, seg, -jnp.inf))
    scores = jnp.einsum('bclhn,bcshn->bclsh', ch, bh)
    y_diag = jnp.einsum('bclsh,bcshp->bclhp', scores * decay, xdt)
    decay_to_end = jnp.exp(a_cum[:, :, -1:, :] - a_cum)
    chunk_states = jnp.einsum('bclhn,bclh,bclhp->bchpn', bh, decay_to_end, xdt)
    chunk_decay = jnp.exp(a_cum[:, :, -1, :])

    def step(s, inp):
        st, dc = inp
        return dc[:, :, None, None] * s + st, s

    s0 = jnp.zeros((b, SSM_HEADS, SSM_HEAD_DIM, SSM_STATE), jnp.float32)
    s_final, s_in = lax.scan(step, s0, (jnp.moveaxis(chunk_states, 1, 0), jnp.moveaxis(chunk_decay, 1, 0)))
    s_in = jnp.moveaxis(s_in, 0, 1)
    y_off = jnp.einsum('bclhn,bchpn,bclh->bclhp', ch, s_in, jnp.exp(a_cum))
    y = (y_diag + y_off).reshape(b, n_chunks * q, SSM_HEADS, SSM_HEAD_DIM)[:, :seq_len]
    return y, s_final

def ssd_recurrent(xs, dt, a, bs, cs, s0):
    rep = SSM_HEADS // SSM_GROUPS

    def step(s, inp):
        xt, dtt, bt, ct = inp
        bt = jnp.repeat(bt, rep, axis=1)
        ct = jnp.repeat(ct, rep, axis=1)
        s = jnp.exp(dtt * a)[:, :, None, None] * s + jnp.einsum('bh,bhp,bhn->bhpn', dtt, xt, bt)
        return s, jnp.einsum('bhpn,bhn->bhp', s, ct)

    s_final, ys = lax.scan(step, s0, (jnp.moveaxis(xs, 1, 0), jnp.moveaxis(dt, 1, 0),
                                      jnp.moveaxis(bs, 1, 0), jnp.moveaxis(cs, 1, 0)))
    return jnp.moveaxis(ys, 0, 1), s_final

def gated_group_rmsnorm(y, z, g):
    b, t_len, _ = y.shape
    u = (y * jax.nn.silu(z.astype(jnp.float32))).reshape(b, t_len, SSM_GROUPS, SSM_INNER // SSM_GROUPS)
    u = u * lax.rsqrt(jnp.mean(u * u, axis=-1, keepdims=True) + EPS)
    return u.reshape(b, t_len, SSM_INNER) * g.astype(jnp.float32)

def mixer_block(hn, mconv_buf, sconv_buf, ssm_state, lw, prompt):
    b, t_len, _ = hn.shape
    proj = hn @ lw['w_in']
    sizes = (SSM_INNER, SSM_CONV_DIM, SSM_HEADS, SC_WIDTH, SC_WIDTH, SC_WIDTH, D_MODEL)
    cuts = [int(c) for c in np.cumsum(sizes)]
    z, xbc, dt_raw, sc_b, sc_c, sc_v, g_a, g_b = jnp.split(proj, cuts, axis=-1)
    if mconv_buf is None:
        mconv_buf = jnp.zeros((b, SSM_CONV - 1, SSM_CONV_DIM), hn.dtype)
    xbc, new_mbuf = causal_dwconv(mconv_buf, xbc, lw['w_mconv'], lw['b_mconv'])
    xbc = jax.nn.silu(xbc)
    xs, bs, cs = jnp.split(xbc, [SSM_INNER, SSM_INNER + SSM_GROUPS * SSM_STATE], axis=-1)
    xs = xs.reshape(b, t_len, SSM_HEADS, SSM_HEAD_DIM).astype(jnp.float32)
    bs = bs.reshape(b, t_len, SSM_GROUPS, SSM_STATE).astype(jnp.float32)
    cs = cs.reshape(b, t_len, SSM_GROUPS, SSM_STATE).astype(jnp.float32)
    dt = jax.nn.softplus(dt_raw.astype(jnp.float32) + lw['dt_bias'].astype(jnp.float32))
    a = -jnp.exp(lw['a_log'].astype(jnp.float32))
    if prompt:
        y, s_new = ssd_chunked(xs, dt, a, bs, cs)
    else:
        y, s_new = ssd_recurrent(xs, dt, a, bs, cs, ssm_state.astype(jnp.float32))
    y = y + lw['d_skip'].astype(jnp.float32)[:, None] * xs
    y_a = gated_group_rmsnorm(y.reshape(b, t_len, SSM_INNER), z, lw['norm_ssm']).astype(hn.dtype)
    if sconv_buf is None:
        sconv_buf = jnp.zeros((b, SC_CONV - 1, SC_WIDTH), hn.dtype)
    u, new_sbuf = causal_dwconv(sconv_buf, sc_c * sc_v, lw['w_sconv'], None)
    y_b = sc_b * u
    merged = jax.nn.sigmoid(g_a) * y_a + jax.nn.sigmoid(g_b) * y_b
    return merged @ lw['w_out'], new_mbuf, new_sbuf, s_new.astype(hn.dtype)

def mem_kv(mem, lw):
    b, m, _ = mem.shape
    mn = rmsnorm(mem, lw['norm_mem'])
    k = (mn @ lw['w_xk']).reshape(b, m, XA_HEADS, XA_HEAD_DIM)
    v = (mn @ lw['w_xv']).reshape(b, m, XA_HEADS, XA_HEAD_DIM)
    return k, v

def cross_attn(hn, k, v, w_q, w_o):
    b, t_len, _ = hn.shape
    q = (hn @ w_q).reshape(b, t_len, XA_HEADS, XA_HEAD_DIM)
    s = jnp.einsum('bthd,bmhd->bhtm', q, k.astype(q.dtype)).astype(jnp.float32) * (XA_HEAD_DIM ** -0.5)
    p = jax.nn.softmax(s, axis=-1).astype(hn.dtype)
    o = jnp.einsum('bhtm,bmhd->bthd', p, v.astype(hn.dtype)).reshape(b, t_len, D_MODEL)
    return o @ w_o

def expert_ffn(xb, w_gu, b_gu, w_dn, b_dn):
    gu = xb @ w_gu + b_gu
    gate, up = jnp.split(gu, 2, axis=-1)
    gate = jnp.minimum(gate, SWIGLU_LIMIT)
    up = jnp.clip(up, -SWIGLU_LIMIT, SWIGLU_LIMIT)
    glu = gate * jax.nn.sigmoid(SWIGLU_ALPHA * gate)
    return ((up + 1.0) * glu) @ w_dn + b_dn

def moe(hn, lw):
    b, t_len, _ = hn.shape
    x = hn.reshape(-1, D_MODEL)
    n_tok = x.shape[0]
    logits = (x @ lw['w_router']).astype(jnp.float32) + lw['b_router'].astype(jnp.float32)
    top_v, top_i = lax.top_k(logits, TOP_K)
    gates = jax.nn.softmax(top_v, axis=-1)
    n_assign = n_tok * TOP_K
    flat_e = top_i.reshape(-1).astype(jnp.int32)
    flat_g = gates.reshape(-1)
    flat_t = jnp.repeat(jnp.arange(n_tok, dtype=jnp.int32), TOP_K)
    order = jnp.argsort(flat_e, stable=True)
    se, st, sg = flat_e[order], flat_t[order], flat_g[order]
    counts = jnp.zeros((N_EXPERTS,), jnp.int32).at[flat_e].add(1)
    padded = (counts + MOE_BLOCK - 1) // MOE_BLOCK * MOE_BLOCK
    start_sorted = jnp.cumsum(counts) - counts
    pad_end = jnp.cumsum(padded)
    start_padded = pad_end - padded
    dest = start_padded[se] + jnp.arange(n_assign, dtype=jnp.int32) - start_sorted[se]
    n_blocks = -(-(n_assign + N_EXPERTS * (MOE_BLOCK - 1)) // MOE_BLOCK)
    n_rows = n_blocks * MOE_BLOCK
    row_tok = jnp.zeros((n_rows,), jnp.int32).at[dest].set(st)
    row_gate = jnp.zeros((n_rows,), jnp.float32).at[dest].set(sg)
    block_start = jnp.arange(n_blocks, dtype=jnp.int32) * MOE_BLOCK
    block_e = jnp.minimum(jnp.searchsorted(pad_end, block_start, side='right'), N_EXPERTS - 1).astype(jnp.int32)
    xs = x[row_tok].reshape(n_blocks, MOE_BLOCK, D_MODEL)

    def run_block(args):
        xb, e = args
        return expert_ffn(xb, lw['w_gate_up'][e], lw['b_gate_up'][e], lw['w_down'][e], lw['b_down'][e])

    ys = lax.map(run_block, (xs, block_e)).reshape(n_rows, D_MODEL)
    out = jnp.zeros_like(x).at[row_tok].add(ys * row_gate[:, None].astype(ys.dtype))
    return out.reshape(b, t_len, D_MODEL)

def decoder_layer(h, mem_k, mem_v, mconv_buf, sconv_buf, ssm_state, lw, prompt):
    a, new_mbuf, new_sbuf, s_new = mixer_block(rmsnorm(h, lw['norm_mix']), mconv_buf, sconv_buf, ssm_state, lw, prompt)
    h = h + a
    h = h + cross_attn(rmsnorm(h, lw['norm_xattn']), mem_k, mem_v, lw['w_xq'], lw['w_xo'])
    h = h + moe(rmsnorm(h, lw['norm_moe']), lw)
    return h, new_mbuf, new_sbuf, s_new

def setup_inputs(seed: int = 0) -> dict:
    key = jax.random.key(seed)
    ks = iter(jax.random.split(key, 40))
    f32 = jnp.float32

    def nrm(shape, scale):
        return jax.random.normal(next(ks), shape, f32) * scale

    def gain(shape):
        return 1.0 + nrm(shape, 0.02)

    dt0 = jnp.exp(jax.random.uniform(next(ks), (DEPTH, SSM_HEADS), f32, minval=np.log(1e-3), maxval=np.log(1e-1)))
    return {
        'x_prompt': nrm((BATCH, SEQ, D_MODEL), 1.0),
        'x_sample': nrm((DEC_BATCH, DEC_SEQ, D_MODEL), 1.0),
        'mem_prompt': nrm((BATCH, N_MEM, D_MODEL), 1.0),
        'state_ssm': nrm((DEPTH, DEC_BATCH, SSM_HEADS, SSM_HEAD_DIM, SSM_STATE), 0.5),
        'state_mamba_conv': nrm((DEPTH, DEC_BATCH, SSM_CONV - 1, SSM_CONV_DIM), 1.0),
        'state_short_conv': nrm((DEPTH, DEC_BATCH, SC_CONV - 1, SC_WIDTH), 1.0),
        'cache_mem_k': nrm((DEPTH, DEC_BATCH, N_MEM, XA_HEADS, XA_HEAD_DIM), 1.0),
        'cache_mem_v': nrm((DEPTH, DEC_BATCH, N_MEM, XA_HEADS, XA_HEAD_DIM), 1.0),
        'norm_mix': gain((DEPTH, D_MODEL)),
        'w_in': nrm((DEPTH, D_MODEL, IN_PROJ_DIM), D_MODEL ** -0.5),
        'w_mconv': nrm((DEPTH, SSM_CONV, SSM_CONV_DIM), SSM_CONV ** -0.5),
        'b_mconv': nrm((DEPTH, SSM_CONV_DIM), 0.02),
        'dt_bias': dt0 + jnp.log(-jnp.expm1(-dt0)),
        'a_log': jnp.log(jax.random.uniform(next(ks), (DEPTH, SSM_HEADS), f32, minval=1.0, maxval=16.0)),
        'd_skip': gain((DEPTH, SSM_HEADS)),
        'norm_ssm': gain((DEPTH, SSM_INNER)),
        'w_sconv': nrm((DEPTH, SC_CONV, SC_WIDTH), SC_CONV ** -0.5),
        'w_out': nrm((DEPTH, D_MODEL, D_MODEL), D_MODEL ** -0.5),
        'norm_xattn': gain((DEPTH, D_MODEL)),
        'norm_mem': gain((DEPTH, D_MODEL)),
        'w_xq': nrm((DEPTH, D_MODEL, D_MODEL), D_MODEL ** -0.5),
        'w_xk': nrm((DEPTH, D_MODEL, D_MODEL), D_MODEL ** -0.5),
        'w_xv': nrm((DEPTH, D_MODEL, D_MODEL), D_MODEL ** -0.5),
        'w_xo': nrm((DEPTH, D_MODEL, D_MODEL), D_MODEL ** -0.5),
        'norm_moe': gain((DEPTH, D_MODEL)),
        'w_router': nrm((DEPTH, D_MODEL, N_EXPERTS), D_MODEL ** -0.5),
        'b_router': nrm((DEPTH, N_EXPERTS), 0.01),
        'w_gate_up': nrm((DEPTH, N_EXPERTS, D_MODEL, 2 * D_FF), D_MODEL ** -0.5),
        'b_gate_up': nrm((DEPTH, N_EXPERTS, 2 * D_FF), 0.02),
        'w_down': nrm((DEPTH, N_EXPERTS, D_FF, D_MODEL), D_FF ** -0.5),
        'b_down': nrm((DEPTH, N_EXPERTS, D_MODEL), 0.02),
        'norm_final': gain((D_MODEL,)),
    }

def reference(x_prompt, x_sample, mem_prompt, state_ssm, state_mamba_conv, state_short_conv,
              cache_mem_k, cache_mem_v, norm_mix, w_in, w_mconv, b_mconv, dt_bias, a_log, d_skip,
              norm_ssm, w_sconv, w_out, norm_xattn, norm_mem, w_xq, w_xk, w_xv, w_xo, norm_moe,
              w_router, b_router, w_gate_up, b_gate_up, w_down, b_down, norm_final):
    hp, hs = x_prompt, x_sample
    ssm_p, mconv_p, sconv_p, mk_p_all, mv_p_all = [], [], [], [], []
    ssm_s, mconv_s, sconv_s = [], [], []
    for l in range(DEPTH):
        lw = {
            'norm_mix': norm_mix[l], 'w_in': w_in[l], 'w_mconv': w_mconv[l], 'b_mconv': b_mconv[l],
            'dt_bias': dt_bias[l], 'a_log': a_log[l], 'd_skip': d_skip[l], 'norm_ssm': norm_ssm[l],
            'w_sconv': w_sconv[l], 'w_out': w_out[l], 'norm_xattn': norm_xattn[l], 'norm_mem': norm_mem[l],
            'w_xq': w_xq[l], 'w_xk': w_xk[l], 'w_xv': w_xv[l], 'w_xo': w_xo[l], 'norm_moe': norm_moe[l],
            'w_router': w_router[l], 'b_router': b_router[l], 'w_gate_up': w_gate_up[l],
            'b_gate_up': b_gate_up[l], 'w_down': w_down[l], 'b_down': b_down[l],
        }
        mk_p, mv_p = mem_kv(mem_prompt, lw)
        hp, mb_p, sb_p, st_p = decoder_layer(hp, mk_p, mv_p, None, None, None, lw, True)
        hs, mb_s, sb_s, st_s = decoder_layer(hs, cache_mem_k[l], cache_mem_v[l], state_mamba_conv[l],
                                             state_short_conv[l], state_ssm[l], lw, False)
        ssm_p.append(st_p); mconv_p.append(mb_p); sconv_p.append(sb_p)
        mk_p_all.append(mk_p); mv_p_all.append(mv_p)
        ssm_s.append(st_s); mconv_s.append(mb_s); sconv_s.append(sb_s)
    y_prompt = rmsnorm(hp, norm_final)
    y_sample = rmsnorm(hs, norm_final)
    new_ssm_prompt = jnp.stack(ssm_p)
    new_mconv_prompt = jnp.stack(mconv_p)
    new_sconv_prompt = jnp.stack(sconv_p)
    mem_k_prompt = jnp.stack(mk_p_all)
    mem_v_prompt = jnp.stack(mv_p_all)
    new_ssm_sample = jnp.stack(ssm_s)
    new_mconv_sample = jnp.stack(mconv_s)
    new_sconv_sample = jnp.stack(sconv_s)
    return (y_prompt, y_sample, new_ssm_prompt, new_mconv_prompt, new_sconv_prompt, mem_k_prompt,
            mem_v_prompt, new_ssm_sample, new_mconv_sample, new_sconv_sample)


_drawn_inputs = setup_inputs


def setup_inputs(seed=0):
    import zlib

    import numpy as np

    out = dict(_drawn_inputs(seed))
    spreads = {}
    factors = {'d_skip': 3.214,
     'norm_xattn': 7.023,
     'norm_mem': 2.851,
     'b_gate_up': 6.175,
     'b_down': 20.443,
     'norm_final': 23.958,
     'norm_moe': 3.137,
     'b_router': 5.211}
    for name, (base, spread) in spreads.items():
        noise = np.random.default_rng([zlib.crc32(name.encode()), seed]).standard_normal(out[name].shape)
        drawn = base * np.exp(spread * noise) if base else spread * noise
        out[name] = __import__('jax').numpy.asarray(drawn.astype(out[name].dtype))
    for name, factor in factors.items():
        out[name] = (out[name] * factor).astype(out[name].dtype)
    return out
```

```python
from contextlib import ExitStack

import concourse.bass as bass
from concourse import mybir

F32 = mybir.dt.float32
I32 = mybir.dt.int32
ALU = mybir.AluOpType
ACT = mybir.ActivationFunctionType
AX = mybir.AxisListType

P = 128
D = 1024
KB = D // P
TP, TS = 256, 8
T = TP + TS
TILES = [(0, 128), (128, 128), (256, 8)]
H, HD, NST, G = 16, 64, 128, 4
CONV = 2048
XB = CONV // P
NM, XH = 256, 4
E, CAP, LIMIT, ALPHA = 32, 64, 7.0, 1.702
PAIRS, MAXP = E // 2, -(-T // CAP)
SLOTS, CW = 4, 512
EPS = 1e-6
A_, D_ = "act", "dve"

PLAN = [("par", 2, A_), ("mst", 1, A_), ("sst", 1, A_), ("xT", 8, A_), ("memT", 4, A_),
        ("xss", 1, A_), ("mss", 1, A_), ("dt", 1, D_), ("proj", 64, A_),
        ("mrow", 4, A_), ("srow", 2, A_), ("acum", 1, D_)]
for _c in range(2):
    PLAN += [(f"xs{_c}", 2, D_), (f"btok{_c}", 1, A_)]
PLAN += [("sin", 2, A_), ("fin", 2, A_)]
for _c in range(2):
    PLAN += [(f"ssd{_c}", 12, None)]
PLAN += [("dec", 1, D_)] + [("bcs", 16, D_)]
PLAN += [("kp", 4, A_), ("vp", 4, A_), ("kT", 4, A_), ("gn", 4, A_), ("wo", 8, D_), ("h1ss", 1, A_),
         ("q", 8, A_), ("att", 4, A_), ("pT", 4, A_), ("o", 4, A_), ("qb", 16, D_), ("sT", 1, D_),
         ("sP", 1, A_), ("so", 4, A_), ("xo", 8, D_), ("h2ss", 1, A_), ("rt", 1, D_), ("rank", 1, D_),
         ("xtok", 6, A_), ("fss", 1, A_), ("yT", 6, A_)]

JOB, WHO = {}, []
for _n, _k, _w in PLAN:
    JOB[_n] = len(WHO)
    WHO += ([A_, D_, D_] * 4) if _w is None else [_w] * _k


def emptied_before(i, who):
    return sum(1 for w in WHO[:i] if w == who)


class Steps:

    def __init__(self, eng, sem):
        self.eng, self.sem, self.n, self.off = eng, sem, 0, 0

    def __call__(self, ins):
        self.n += 1
        ins.then_inc(self.sem, 1)
        self.eng.wait_ge(self.sem, self.off + self.n)


def build(nc, a, outs):
    with ExitStack() as ctx:
        def sb(name, shape, dt=F32):
            return ctx.enter_context(nc.sbuf_tensor(name, shape, dt))

        def sem(name):
            return ctx.enter_context(nc.semaphore(name))

        bank = [ctx.enter_context(nc.psum_tensor(f"bank{i}", [P, 512], F32)) for i in range(8)]

        ring = sb("ring", [P, SLOTS, 8, CW])
        projT = sb("projT", [P, 64, T])
        conv = sb("conv", [P, XB, T])
        hT = sb("hT", [P, KB, T])
        xnT = sb("xnT", [P, KB, T])
        par = sb("par", [P, 8, P])
        flat = sb("flat", [P, 4096])
        mnT = sb("mnT", [P, KB, NM])
        ident, ones, uinc, ustr = (sb(n, [P, P]) for n in ("ident", "ones", "uinc", "ustr"))
        iota = sb("iota", [P, CAP])
        eps = sb("eps", [P, 1])
        wdt = sb("wdt", [P, KB, H])
        wrt = sb("wrt", [P, KB, E])
        dtb, alog, brt = sb("dtb", [P, H]), sb("alog", [P, H]), sb("brt", [P, E])
        dsk = sb("dsk", [P, KB])
        dts = sb("dts", [P, 6, 3, H])
        dta = sb("dta", [P, 3, H])
        small = sb("small", [P, 320])
        rinv = sb("rinv", [P, T])
        npass = sb("npass", [1, 1], I32)

        XBC, Z, GA, SCC, SCV, SCB, GB = 0, 16, 24, 32, 40, 48, 56

        stage = flat[:, 0:1024].rearrange("p (a b) -> p a b", a=8)
        xtokin = flat[:, 1024:4096].rearrange("p (a b) -> p a b", a=3)
        mrows = flat[0:11, 0:2048]
        srows = flat[0:10, 2048:3072]
        memin = projT[:, 0:8, 0:256]
        memv = [projT[:, 4 * i:4 * i + 4, 0:256] for i in range(2)]
        sqx = projT[:, 8:16, :]
        sqm = projT[:, 16:24, 0:NM]
        mstate = conv[0:24, 0:8, 0:256]
        sstate = conv[0:16, 8:12, 0:256]
        msT = sb("msT", [P, XB, 24])
        ssT = sb("ssT", [P, KB, 16])
        tmp = flat[:, 3072:3200].rearrange("p (b n) -> p b n", n=TS)
        r1 = projT[:, 0:16, :].rearrange("p a b -> p (a b)")
        r3 = projT[:, SCC:SCC + 16, :].rearrange("p a b -> p (a b)")
        xdt = r1[:, 0:2048].rearrange("p (c n) -> p c n", c=2)
        btok = r1[:, 2048:3072].rearrange("p (c n) -> p c n", c=2)
        finst = r1[:, 3072:4096].rearrange("p (h n) -> p h n", h=8)
        xdte = flat[:, 0:3072].rearrange("p (v n) -> p v n", v=3)
        sinT = flat[:, 3072:4096]
        bcum = r3[:, 0:1024].rearrange("p (u h l) -> p u h l", u=2, h=4)
        dcy = r3[:, 1024:2048].rearrange("p (u h l) -> p u h l", u=2, h=4)
        scm = r3[:, 2048:2304].rearrange("p (u l) -> p u l", u=2)
        cexp = r3[:, 2304:2816].rearrange("p (h l) -> p h l", h=4)
        eac = r3[:, 2816:3328].rearrange("p (h l) -> p h l", h=4)
        dtx = r3[:, 3328:3392].rearrange("p (h b) -> p h b", h=8)
        dec = r3[:, 3392:3456].rearrange("p (h b) -> p h b", h=8)
        yT = projT[:, GB:GB + 8, :]
        sst = r1[:, 0:2048].rearrange("p (u h n) -> p u h n", u=2, h=8)
        prod = flat[:, 0:1024].rearrange("p (h n) -> p h n", h=8)
        ktok = r3[:, 0:2048].rearrange("p (m n) -> p m n", m=2)
        vtok = r3[:, 2048:4096].rearrange("p (m n) -> p m n", m=2)
        kT = mnT
        ubr = projT[:, SCB:SCB + 8, :]
        sqg = conv[:, 0:8, :]
        merged = projT[:, Z:Z + 8, :]
        rgrp = conv[:, 8:12, :]
        qT = projT[:, Z:Z + 8, :]
        pr = flat[:, 0:2048].rearrange("p (t h m) -> p t h m", t=2, h=4)
        pT = flat[:, 2048:4096].rearrange("p (h m t) -> p h m t", h=4, m=2)
        oT = conv[:, 8:16, :]
        junk = projT[:, 0, 0:256]
        scs = projT[:, 1, 0:64]
        sP = projT[0:32, 2, 0:256]
        sPT = projT[:, 3, 0:64].rearrange("p (m c) -> p m c", m=2)
        sqh = conv[:, 0:8, :]
        moe = projT[:, :, :].rearrange("p a b -> p (a b)")
        at = [0]

        def cut(n):
            at[0] += n
            return moe[:, at[0] - n:at[0]]

        xtok = cut(3 * D).rearrange("p (t n) -> p t n", t=3)
        selT = cut(3 * P).rearrange("p (t n) -> p t n", t=3)
        selG = cut(3 * P).rearrange("p (t n) -> p t n", t=3)
        xg = cut(KB * P).rearrange("p (k n) -> p k n", k=KB)
        gate = cut(512).rearrange("p (j n) -> p j n", j=8)
        up = cut(512).rearrange("p (j n) -> p j n", j=8)
        sig = cut(512).rearrange("p (j n) -> p j n", j=8)
        act = [cut(512).rearrange("p (j n) -> p j n", j=8) for _ in range(2)]
        ypT = cut(KB * P).rearrange("p (k n) -> p k n", k=KB)
        ytok = cut(D)
        gT = cut(T)
        moeT = cut(KB * T).rearrange("p (k n) -> p k n", k=KB)
        rkp = cut(3 * (MAXP + 1) * E).rearrange("p (t n) -> p t n", t=3)
        gts = cut(3 * E).rearrange("p (t n) -> p t n", t=3)
        lg = cut(3 * E).rearrange("p (t n) -> p t n", t=3)
        msk = cut(3 * E).rearrange("p (t n) -> p t n", t=3)
        eqm = cut(3 * E).rearrange("p (t n) -> p t n", t=3)
        cum = cut(3 * E).rearrange("p (t n) -> p t n", t=3)
        zer = cut(E)
        top = cut(24).rearrange("p (t n) -> p t n", t=3)
        need = cut(8)
        yout = cut(3 * D).rearrange("p (t n) -> p t n", t=3)
        assert at[0] <= 64 * T

        def pcol(i):
            return par[:, i // P, i % P:i % P + 1]

        MW, MB_, SW, NSSM, NMIX, NXA, NMEM, NMOE, NFIN = 0, 64, 80, 104, 112, 120, 128, 136, 144
        bgu = par[:, 2:6, :].rearrange("p a b -> p (a b)")
        bdn = par[:, 6:8, :].rearrange("p a b -> p (a b)")

        bank_filled, act_emptied, dve_emptied = sem("bank_filled"), sem("act_emptied"), sem("dve_emptied")
        act_step, dve_step, pool_step = sem("act_step"), sem("dve_step"), sem("pool_step")
        slot_full = [sem(f"slot_full{i}") for i in range(SLOTS)]
        params_in, x_in, mem_in, small_in, conv_in = (sem(n) for n in (
            "params_in", "x_in", "mem_in", "small_in", "conv_in"))
        state_in = [sem(f"state_in{u}") for u in range(2)]
        state_out = [sem(f"state_out{u}") for u in range(2)]
        names = ("consts_set", "x_squared", "mem_squared", "x_rms", "mem_rms", "x_normed", "mem_normed",
                 "dt_abs", "dt_exp", "dt_one", "dt_log", "a_exp", "dt_ready", "convolved", "conv_silu",
                 "gated_conv", "gb_sigmoid", "ubr_ready", "raw_used", "cv_ready", "acum_read",
                 "dw_exp", "xdte_ready", "seg_ready", "dcy_ready", "eac_ready", "m_ready", "ce_ready",
                 "dec_exp", "dec_ready", "state_new", "z_silu", "ga_sigmoid", "u_ready", "u_squared",
                 "grp_rms", "merged_ready", "h1_ready", "h_squared", "h_rms", "xn_ready",
                 "att_max", "att_exp", "probs_ready", "s_neg", "s_exp", "s_probs", "h2_ready",
                 "lg_ready", "lg_exp", "mask_ready", "rank_ready", "passes_ready",
                 "rows_out", "kv_out", "fin_out", "y_out", "copy_out",
                 "chunk_done", "bias_gate", "sig_ready", "h_act", "gu_read", "dn_read",
                 "sel_ready", "xg_full", "xg_ready", "selg_ready", "misc_full", "misc_read", "yp_ready",
                 "moe_summed", "final_normed", "state_free", "scratch_free", "sin_ready")
        S = {n: sem(n) for n in names}

        def filled(eng, name, k=0):
            i = JOB[name] + k
            eng.wait_ge(bank_filled, i + 1)
            return bank[i % 8]

        def emptied(eng, name, k=0):
            i = JOB[name] + k
            eng.wait_ge(act_emptied if WHO[i] == A_ else dve_emptied, emptied_before(i + 1, WHO[i]))

        def free_bank(pe, name, k=0):
            i = JOB[name] + k
            if i >= 8:
                w = WHO[i - 8]
                pe.wait_ge(act_emptied if w == A_ else dve_emptied, emptied_before(i - 7, w))
            return bank[i % 8]

        block = ctx.enter_context(nc.Block())

        def wcols(w, c0):
            return w[0].rearrange("(k p) n -> p k n", p=P)[:, :, c0:c0 + CW]

        proj_cols = [1024, 1536, 2048, 2560, 0, 512, 6160, 6672, 4112, 4624, 5136, 5648,
                     3088, 3600, 7184, 7696]
        chunks = [(wcols(a["w_in"], c), ("proj", 4 * i + 3)) for i, c in enumerate(proj_cols)]
        for w, j in (("w_xk", "kp"), ("w_xv", "vp")):
            chunks += [(wcols(a[w], 0), (j, 1)), (wcols(a[w], 512), (j, 3))]
        chunks += [(wcols(a["w_out"], 0), ("wo", 3)), (wcols(a["w_out"], 512), ("wo", 7))]
        chunks += [(wcols(a["w_xq"], 0), ("q", 3)), (wcols(a["w_xq"], 512), ("q", 7))]
        for w, j, per in (("cache_mem_k", "qb", 4), ("cache_mem_v", "so", 1)):
            src = a[w][0].rearrange("b (m p) h d -> p b m (h d)", p=P)
            chunks += [(src[:, 2 * i:2 * i + 2], (j, per * i + per - 1)) for i in range(4)]
        chunks += [(wcols(a["w_xo"], 0), ("xo", 3)), (wcols(a["w_xo"], 512), ("xo", 7))]
        NCH = len(chunks)
        CH = {"w_xk": 16, "w_xv": 18, "w_out": 20, "w_xq": 22, "k": 24, "v": 28, "w_xo": 32}
        assert NCH == 34

        def slot(i):
            return ring[:, i % SLOTS]

        def chunk_in(eng, i):
            eng.wait_ge(slot_full[i % SLOTS], 16 * (i // SLOTS + 1))
            return slot(i)

        wgu = a["w_gate_up"][0].rearrange("e (k p) n -> e p k n", p=P)
        wdn = a["w_down"][0].rearrange("e (k p) n -> e p k n", p=P)

        def moe_chunk(pair, j):
            if j < 8:
                return wgu[bass.ds(pair * 2 + j // 4, 1), :, :, (j % 4) * CW:(j % 4 + 1) * CW].rearrange(
                    "e p k n -> (e p) k n")
            return wdn[bass.ds(pair * 2 + (j - 8) // 2, 1), :, :, (j % 2) * CW:(j % 2 + 1) * CW].rearrange(
                "e p k n -> (e p) k n")

        @block.sync
        def _(sp):
            sp.dma_start(xtokin[:, 0:2, :], a["x_prompt"][0].rearrange("(t p) n -> p t n", p=P)).then_inc(x_in, 16)
            sp.dma_start(xtokin[0:TS, 2, :], a["x_sample"].rearrange("b s n -> (b s) n")).then_inc(x_in, 16)
            for i, (src, _) in enumerate(chunks):
                if i >= SLOTS:
                    name, k = chunks[i - SLOTS][1]
                    if name == "qb":
                        emptied(sp, name, k)
                    else:
                        filled(sp, name, k)
                if 24 <= i < 32:
                    dst = slot(i).rearrange("p (b m n) c -> p b m (n c)", b=2, m=2)
                else:
                    dst = slot(i)
                sp.dma_start(dst, src).then_inc(slot_full[i % SLOTS], 16)
            for j in range(SLOTS):
                filled(sp, *chunks[NCH - SLOTS + j][1])
                sp.dma_start(slot(NCH + j), moe_chunk(0, j)).then_inc(slot_full[(NCH + j) % SLOTS], 16)
            sp.wait_ge(S["passes_ready"], 1)
            n = sp.value_load(npass[0:1, 0:1], min_val=0, max_val=MAXP - 1)

            def rest(it, pair):
                for j in range(SLOTS, 12):
                    sp.wait_ge(S["chunk_done"], it * 12 + (j - 3))
                    sp.dma_start(slot(NCH + j), moe_chunk(pair, j)).then_inc(slot_full[(NCH + j) % SLOTS], 16)

            with sp.Fori(0, n * PAIRS + (PAIRS - 1)) as it:
                rest(it, it % PAIRS)
                nxt = (it + 1) % PAIRS
                for j in range(SLOTS):
                    sp.wait_ge(S["chunk_done"], it * 12 + (9 + j))
                    sp.dma_start(slot(NCH + j), moe_chunk(nxt, j)).then_inc(slot_full[(NCH + j) % SLOTS], 16)
            for j in range(SLOTS, 12):
                sp.wait_ge(S["chunk_done"], n * (12 * PAIRS) + (12 * (PAIRS - 1) + j - 3))
                e = E - 2 + (j // 4 if j < 8 else (j - 8) // 2)
                src = wgu[e] if j < 8 else wdn[e]
                c = (j % 4 if j < 8 else j % 2) * CW
                sp.dma_start(slot(NCH + j), src[:, :, c:c + CW]).then_inc(slot_full[(NCH + j) % SLOTS], 16)
            emptied(sp, "yT", 3)
            sp.dma_start(outs[0][0].rearrange("(t p) n -> p t n", p=P), yout[:, 0:2, :]).then_inc(S["y_out"], 16)
            emptied(sp, "yT", 5)
            sp.dma_start(outs[1].rearrange("b s n -> (b s) n"), yout[0:TS, 2, :]).then_inc(S["y_out"], 16)
            sp.wait_ge(S["y_out"], 32)

        @block.gpsimd
        def _(pool):
            st = Steps(pool, pool_step)
            for m in (ident, ones, uinc, ustr):
                st(pool.memset(m[:], 0.0 if m is ident else 1.0))
            st(pool.affine_select(out=ident[:], in_=ident[:], compare_op=ALU.not_equal, fill=1.0, base=0,
                                  pattern=[[-1, P]], channel_multiplier=1))
            for m, op in ((uinc, ALU.is_ge), (ustr, ALU.is_gt)):
                st(pool.affine_select(out=m[:], in_=m[:], compare_op=op, fill=0.0, base=0,
                                      pattern=[[1, P]], channel_multiplier=-1))
            pool.iota(iota[:], pattern=[[1, CAP]], base=0, channel_multiplier=0,
                      allow_small_or_imprecise_dtypes=True).then_inc(S["consts_set"], 1)
            pool.dma_start(outs[8][0, :, 0:2, :], a["state_mamba_conv"][0, :, 1:3, :]).then_inc(S["copy_out"], 16)
            pool.dma_start(outs[9][0, :, 0:1, :], a["state_short_conv"][0, :, 1:2, :]).then_inc(S["copy_out"], 16)
            emptied(pool, "srow", 1)
            pool.dma_start(outs[3][0, 0], mrows[0:3, :]).then_inc(S["rows_out"], 16)
            pool.dma_start(outs[4][0, 0], srows[0:2, :]).then_inc(S["rows_out"], 16)
            pool.dma_start(outs[8][0, :, 2, :], mrows[3:11, :]).then_inc(S["rows_out"], 16)
            pool.dma_start(outs[9][0, :, 1, :], srows[2:10, :]).then_inc(S["rows_out"], 16)
            emptied(pool, "fin", 1)
            pool.dma_start(outs[2][0, 0].rearrange("(x y) p n -> (y p) x n", y=2), finst).then_inc(S["fin_out"], 16)
            sin = a["state_ssm"][0].rearrange("b (x y) p n -> b (y p) x n", y=2)
            sout = outs[7][0].rearrange("b (x y) p n -> b (y p) x n", y=2)
            pool.wait_ge(S["state_free"], 1)
            for b in range(TS + 2):
                if b >= 2:
                    pool.wait_ge(S["state_new"], b - 1)
                    pool.dma_start(sout[b - 2], sst[:, b % 2]).then_inc(state_out[b % 2], 16)
                    pool.wait_ge(state_out[b % 2], 16 * (b // 2))
                if b < TS:
                    if b >= 2:
                        emptied(pool, "bcs", 2 * b - 3)
                    pool.dma_start(sst[:, b % 2], sin[b]).then_inc(state_in[b % 2], 16)
            emptied(pool, "kp", 3)
            pool.dma_start(outs[5][0, 0].rearrange("(m p) h d -> p m (h d)", p=P), ktok).then_inc(S["kv_out"], 16)
            emptied(pool, "vp", 3)
            pool.dma_start(outs[6][0, 0].rearrange("(m p) h d -> p m (h d)", p=P), vtok).then_inc(S["kv_out"], 16)
            pool.wait_ge(S["kv_out"], 32)
            pool.wait_ge(S["fin_out"], 16)
            pool.wait_ge(S["rows_out"], 64)
            pool.wait_ge(S["copy_out"], 32)

        @block.scalar
        def _(s):
            st = Steps(s, act_step)

            def copy(out, in_, scale=1.0):
                return s.activation(out, in_, ACT.Copy, scale=scale)

            def done(ins):
                return ins.then_inc(act_emptied, 1)

            rows = [(0, 0, "w_mconv", 64), (0, 64, "b_mconv", 16), (0, 80, "w_sconv", 24), (0, 104, "norm_ssm", 8),
                    (0, 112, "norm_mix", 8), (0, 120, "norm_xattn", 8), (1, 0, "norm_mem", 8),
                    (1, 8, "norm_moe", 8), (1, 16, "norm_final", 8)]
            for t, r, name, n in rows:
                src = a[name]
                if len(src.shape) == 3:
                    src = src.rearrange("l k (b f) -> (l k b) f", f=P)
                elif len(src.shape) == 2:
                    src = src.rearrange("l (b f) -> (l b) f", f=P)
                else:
                    src = src.rearrange("(b f) -> b f", f=P)
                s.dma_start(stage[r:r + n, t, :], src).then_inc(params_in, 16)
            s.dma_start(stage[:, 2:6, :], a["b_gate_up"][0].rearrange("(a e) (b f) -> (e b) a f", a=4, f=P))\
                .then_inc(params_in, 16)
            s.dma_start(stage[:, 6:8, :], a["b_down"][0].rearrange("(a e) (b f) -> (e b) a f", a=2, f=P))\
                .then_inc(params_in, 16)
            s.dma_start(mstate, a["state_mamba_conv"][0].rearrange("b k (c f) -> (b k) c f", f=256)).then_inc(conv_in, 16)
            s.dma_start(sstate, a["state_short_conv"][0].rearrange("b k (c f) -> (b k) c f", f=256)).then_inc(conv_in, 16)
            for t in range(2):
                s.dma_start(memv[t], a["mem_prompt"][0, t * P:(t + 1) * P, :].rearrange("p (a n) -> p a n", a=4))\
                    .then_inc(mem_in, 16)
            s.dma_start(wdt[:], a["w_in"][0].rearrange("(k p) n -> p k n", p=P)[:, :, 3072:3088]).then_inc(small_in, 16)
            s.dma_start(wrt[:], a["w_router"][0].rearrange("(k p) n -> p k n", p=P)).then_inc(small_in, 16)
            s.dma_start(dtb[:], a["dt_bias"][0].partition_broadcast(P)).then_inc(small_in, 16)
            s.dma_start(alog[:], a["a_log"][0].partition_broadcast(P)).then_inc(small_in, 16)
            s.dma_start(brt[:], a["b_router"][0].partition_broadcast(P)).then_inc(small_in, 16)
            for y in range(2):
                s.dma_start(dsk[64 * y:64 * y + 64, :],
                            a["d_skip"][0].rearrange("(x y) -> y x", y=2)[y].partition_broadcast(64),
                            allow_slow_non_contiguous=True).then_inc(small_in, 16)

            for k in range(2):
                b = filled(s, "par", k)
                if k == 0:
                    st(copy(par[:, 0, :], b[:, 0:P]))
                    st(copy(par[:, 1, 0:24], b[:, P:P + 24]))
                    done(copy(par[:, 2:4, :], b[:, 2 * P:4 * P].rearrange("p (a n) -> p a n", a=2)))
                else:
                    done(copy(par[:, 4:8, :], b[:, :].rearrange("p (a n) -> p a n", a=4)))
            b = filled(s, "mst")
            done(copy(msT[:], b[:, 0:384].rearrange("p (b c) -> p b c", b=XB)))
            b = filled(s, "sst")
            done(copy(ssT[:], b[:, 0:128].rearrange("p (b c) -> p b c", b=8)))
            for k in range(8):
                b = filled(s, "xT", k)
                done(copy(hT[:, k, :], b[:, 0:T]))
            for k in range(4):
                b = filled(s, "memT", k)
                done(copy(mnT[:, 2 * k:2 * k + 2, :], b[:, :].rearrange("p (a n) -> p a n", a=2)))
            emptied(s, "memT", 3)
            s.activation(sqx, hT[:], ACT.Square).then_inc(S["x_squared"], 1)
            s.activation(sqm, mnT[:], ACT.Square).then_inc(S["mem_squared"], 1)

            def root(name, out, n, div=D):
                b = filled(s, name)
                done(s.activation(out, b[:, 0:n], ACT.Sqrt, bias=eps[:, 0:1], scale=1.0 / div))

            s.wait_ge(S["consts_set"], 2)
            root("xss", rinv[:], T)
            root("mss", small[:, 0:NM], NM)
            s.wait_ge(S["dt_abs"], 1)
            s.activation(dts[:, 1], dts[:, 1], ACT.Exp, scale=-1.0).then_inc(S["dt_exp"], 1)
            s.wait_ge(small_in, 112)
            s.activation(alog[:], alog[:], ACT.Exp).then_inc(S["a_exp"], 1)
            s.wait_ge(S["dt_one"], 1)
            s.activation(dts[:, 3], dts[:, 2], ACT.Ln).then_inc(S["dt_log"], 1)

            def proj_blocks(n0, groups):
                base = JOB["proj"] + n0
                with s.Fori(0, groups) as g:
                    for j in range(8):
                        s.wait_ge(bank_filled, g * 8 + (base + j + 1))
                        copy(projT[:, bass.ds(g * 8 + (n0 + j), 1), :].rearrange("p a n -> p (a n)"),
                             bank[(base + j) % 8][:, 0:T]).then_inc(act_emptied, 1)

            s.wait_ge(S["x_normed"], 8)
            s.wait_ge(S["mem_normed"], 8)
            proj_blocks(0, 2)
            proj_blocks(16, 2)
            emptied(s, "proj", 31)
            s.wait_ge(S["convolved"], 1)
            s.activation(conv[:], conv[:], ACT.Silu).then_inc(S["conv_silu"], 1)
            s.activation(projT[:, Z:Z + 8, :], projT[:, Z:Z + 8, :], ACT.Silu).then_inc(S["z_silu"], 1)
            s.activation(projT[:, GA:GA + 8, :], projT[:, GA:GA + 8, :], ACT.Sigmoid).then_inc(S["ga_sigmoid"], 1)
            proj_blocks(32, 4)
            emptied(s, "proj", 63)
            s.activation(projT[:, GB:GB + 8, :], projT[:, GB:GB + 8, :], ACT.Sigmoid).then_inc(S["gb_sigmoid"], 1)
            for k in range(4):
                b = filled(s, "mrow", k)
                done(copy(mrows[:, 512 * k:512 * k + 512], b[0:11, :]))
            for k in range(2):
                b = filled(s, "srow", k)
                done(copy(srows[:, 512 * k:512 * k + 512], b[0:10, :]))
            s.wait_ge(S["acum_read"], 1)
            s.activation(small[:, 64:112], small[:, 64:112], ACT.Exp).then_inc(S["dw_exp"], 1)
            for c in range(2):
                b = filled(s, f"btok{c}")
                done(copy(btok[:, c, :], b[:, :]))
            for k in range(2):
                b = filled(s, "sin", k)
                done(copy(sinT[:, 512 * k:512 * k + 512], b[:, :]))
            for k in range(2):
                b = filled(s, "fin", k)
                done(copy(finst[:, 4 * k:4 * k + 4, :], b[:, :].rearrange("p (h n) -> p h n", h=4)))
            for c in range(2):
                for g in range(G):
                    n = G * c + g
                    b = filled(s, f"ssd{c}", 3 * g)
                    if n == 0:
                        s.wait_ge(S["ubr_ready"], 1)
                    done(copy(bcum[:, n % 2], b[:, :].rearrange("p (h l) -> p h l", h=4)))
                    if c == 1:
                        emptied(s, f"ssd{c}", 3 * g)
                        if g >= 1:
                            s.wait_ge(S["ce_ready"], g)
                        s.activation(eac, bcum[:, n % 2], ACT.Exp).then_inc(S["eac_ready"], 1)
                    s.wait_ge(S["seg_ready"], n + 1)
                    s.activation(dcy[:, n % 2], dcy[:, n % 2], ACT.Exp).then_inc(S["dcy_ready"], 1)
            emptied(s, "dec")
            s.activation(dec, dec, ACT.Exp).then_inc(S["dec_ready"], 1)
            s.wait_ge(S["scratch_free"], 1)
            for name, dst in (("kp", ktok), ("vp", vtok)):
                for nh in range(2):
                    for mt in range(2):
                        b = filled(s, name, 2 * nh + mt)
                        done(copy(dst[:, mt, nh * 512:nh * 512 + 512], b[:, :]))
            for k in range(4):
                b = filled(s, "kT", k)
                done(copy(kT[:, 2 * k:2 * k + 2, :], b[:, :].rearrange("p (a n) -> p a n", a=2)))
            s.wait_ge(S["u_ready"], 1)
            s.activation(sqg, yT, ACT.Square).then_inc(S["u_squared"], 1)
            for g in range(G):
                b = filled(s, "gn", g)
                done(s.activation(rgrp[:, g, :], b[:, 0:T], ACT.Sqrt, bias=eps[:, 0:1], scale=1.0 / 256))

            def square_h():
                s.activation(sqh, hT[:], ACT.Square).then_inc(S["h_squared"], 1)

            emptied(s, "wo", 7)
            square_h()
            root("h1ss", rinv[:], T)
            for k in range(8):
                b = filled(s, "q", k)
                done(copy(qT[:, k, :], b[:, 0:T], 1.0 / 16))
            for t in range(2):
                for hh in range(2):
                    n = 2 * t + hh
                    b = filled(s, "att", n)
                    s.wait_ge(S["att_max"], n + 1)
                    for h in range(2):
                        j = 8 * t + 2 * hh + h
                        ins = s.activation(pr[:, t, 2 * hh + h, :], b[:, h * 256:h * 256 + 256], ACT.Exp,
                                           bias=small[:, j:j + 1], accum_out=small[:, 16 + j:17 + j])
                        if h == 0:
                            st(ins)
                    done(ins)
            for h in range(4):
                b = filled(s, "pT", h)
                done(copy(pT[:, h], b[:, :].rearrange("p (m t) -> p m t", m=2)))
            for k in range(4):
                b = filled(s, "o", k)
                done(copy(oT[:, 2 * k:2 * k + 2, 0:TP], b[:, :].rearrange("p (a t) -> p a t", a=2)))
            emptied(s, "sT")
            s.activation(sP, sP, ACT.Exp, bias=small[0:32, 32:33], accum_out=small[0:32, 33:34]).then_inc(S["s_exp"], 1)
            b = filled(s, "sP")
            done(copy(sPT, b[:, 0:64].rearrange("p (m c) -> p m c", m=2)))
            for i in range(4):
                b = filled(s, "so", i)
                done(copy(oT[:, :, TP + 2 * i:TP + 2 * i + 2].rearrange("p k b -> p b k"),
                          b[:, 0:16].rearrange("p (b k) -> p b k", b=2)))
            emptied(s, "xo", 7)
            square_h()
            root("h2ss", rinv[:], T)
            s.wait_ge(S["lg_ready"], 1)
            s.activation(gts, gts, ACT.Exp).then_inc(S["lg_exp"], 1)
            for t, (_, n) in enumerate(TILES):
                for k in range(2):
                    b = filled(s, "xtok", 2 * t + k)
                    done(copy(xtok[0:n, t, 512 * k:512 * k + 512], b[0:n, :]))

            def gathered(n):
                s.wait_ge(S["xg_full"], n)
                for k in range(2):
                    copy(xg[:, 4 * k:4 * k + 4, :], bank[3 + k][:, :].rearrange("p (a n) -> p a n", a=4))\
                        .then_inc(S["xg_ready"], 1)

            for k in range(2):
                s.activation(small[:, 300 + k:301 + k], eps[:], ACT.Copy).then_inc(S["xg_ready"], 1)
            gathered(1)
            s.wait_ge(S["passes_ready"], 1)
            n = s.value_load(npass[0:1, 0:1], min_val=0, max_val=MAXP - 1)
            with s.Fori(0, n * PAIRS + PAIRS) as it:
                for e in range(2):
                    s.wait_ge(S["bias_gate"], it * 2 + (e + 1))
                    s.activation(sig, gate, ACT.Sigmoid, scale=ALPHA).then_inc(S["sig_ready"], 1)
                gathered(it + 2)
            s.wait_ge(S["moe_summed"], 1)
            square_h()
            root("fss", rinv[:], T)
            for t, (_, n) in enumerate(TILES):
                for k in range(2):
                    b = filled(s, "yT", 2 * t + k)
                    done(copy(yout[0:n, t, 512 * k:512 * k + 512], b[0:n, :]))

        @block.vector
        def _(v):
            st = Steps(v, dve_step)

            def done(ins):
                return ins.then_inc(dve_emptied, 1)

            def bc(x, n):
                return x.unsqueeze(2).to_broadcast([x.shape[0], x.shape[1], n])

            st(v.memset(small[:], 0.0))
            st(v.memset(dts[:], 0.0))
            v.memset(eps[:], EPS).then_inc(S["consts_set"], 1)

            def norm(name, dst, src, r, n, gain, out):
                emptied(v, name)
                st(v.reciprocal(r, r))
                for k in range(KB):
                    v.scalar_tensor_tensor(out=dst[:, k, 0:n], in0=src[:, k, 0:n], scalar=pcol(gain + k), in1=r,
                                           op0=ALU.mult, op1=ALU.mult).then_inc(S[out], 1)

            norm("xss", xnT, hT, rinv[:], T, NMIX, "x_normed")
            norm("mss", mnT, mnT, small[:, 0:NM], NM, NMEM, "mem_normed")
            v.wait_ge(S["mem_normed"], 8)

            v.wait_ge(small_in, 112)
            b = filled(v, "dt")
            st(v.tensor_tensor(out=dts[:, 0, 0:2], in0=b[:, 0:32].rearrange("p (t h) -> p t h", t=2),
                               in1=dtb[:].unsqueeze(1).to_broadcast([P, 2, H]), op=ALU.add))
            done(v.tensor_tensor(out=dts[0:TS, 0, 2], in0=b[0:TS, 32:48], in1=dtb[0:TS, :], op=ALU.add))
            emptied(v, "dt")
            v.scalar_tensor_tensor(out=dts[:, 1], in0=dts[:, 0], scalar=-1.0, in1=dts[:, 0], op0=ALU.mult, op1=ALU.max).then_inc(S["dt_abs"], 1)
            v.wait_ge(S["dt_exp"], 1)
            v.tensor_scalar(dts[:, 2], dts[:, 1], 1.0, None, ALU.add).then_inc(S["dt_one"], 1)
            v.wait_ge(S["dt_one"], 1)
            st(v.tensor_scalar(dts[:, 4], dts[:, 2], -1.0, None, ALU.add))
            st(v.tensor_scalar(dts[:, 5], dts[:, 4], 0.0, None, ALU.is_equal))
            st(v.tensor_tensor(out=dts[:, 4], in0=dts[:, 4], in1=dts[:, 5], op=ALU.add))
            st(v.reciprocal(dts[:, 4], dts[:, 4]))
            v.wait_ge(S["dt_log"], 1)
            st(v.tensor_tensor(out=dts[:, 3], in0=dts[:, 3], in1=dts[:, 5], op=ALU.add))
            st(v.tensor_tensor(out=dts[:, 3], in0=dts[:, 3], in1=dts[:, 4], op=ALU.mult))
            st(v.tensor_tensor(out=dts[:, 3], in0=dts[:, 3], in1=dts[:, 1], op=ALU.mult))
            st(v.scalar_tensor_tensor(out=dts[:, 0], in0=dts[:, 0], scalar=0.0, in1=dts[:, 3],
                                      op0=ALU.max, op1=ALU.add))
            v.wait_ge(S["a_exp"], 1)
            v.scalar_tensor_tensor(out=dta[:], in0=dts[:, 0], scalar=-1.0,
                                   in1=alog[:].unsqueeze(1).to_broadcast([P, 3, H]),
                                   op0=ALU.mult, op1=ALU.mult).then_inc(S["dt_ready"], 1)

            def blk_of(buf, i, c0, c1):
                return buf[:, bass.ds(i, 1), c0:c1].rearrange("p a n -> p (a n)")

            def weight(i):
                return par[:, 0, bass.ds(i, 1)]

            emptied(v, "par", 0)
            n0, before = st.n, emptied_before(JOB["proj"], A_)
            with v.Fori(0, XB) as blk:
                st.n, st.off = n0, blk * 4
                v.wait_ge(act_emptied, blk + (before + 1))
                st(v.tensor_scalar(blk_of(conv, blk, 0, T), blk_of(projT, blk, 0, T),
                                   weight(blk + 48), weight(blk + MB_), ALU.mult, ALU.add))
                for d in range(1, 4):
                    st(v.scalar_tensor_tensor(out=blk_of(conv, blk, d, TP), in0=blk_of(projT, blk, 0, TP - d),
                                              scalar=weight(blk + 16 * (3 - d)), in1=blk_of(conv, blk, d, TP),
                                              op0=ALU.mult, op1=ALU.add))
            st.n, st.off = n0 + 4 * XB, 0
            emptied(v, "mst")
            old = msT[:].rearrange("p b (s k) -> p b s k", k=3)
            for k in range(3):
                st(v.tensor_tensor(out=tmp, in0=old[:, :, :, k], in1=bc(par[:, 0, 16 * k:16 * k + 16], TS),
                                   op=ALU.mult))
                ins = v.tensor_tensor(out=conv[:, :, TP:T], in0=conv[:, :, TP:T], in1=tmp, op=ALU.add)
                if k < 2:
                    st(ins)
            ins.then_inc(S["convolved"], 1)

            emptied(v, "proj", 47)
            v.tensor_tensor(out=projT[:, SCC:SCC + 8, :], in0=projT[:, SCC:SCC + 8, :],
                            in1=projT[:, SCV:SCV + 8, :], op=ALU.mult).then_inc(S["cv_ready"], 1)
            v.wait_ge(S["cv_ready"], 1)
            n0 = st.n
            with v.Fori(0, KB) as blk:
                st.n, st.off = n0, blk * 3
                st(v.tensor_scalar(blk_of(projT, blk + SCV, 0, T), blk_of(projT, blk + SCC, 0, T),
                                   weight(blk + (SW + 16)), None, ALU.mult))
                for d in range(1, 3):
                    st(v.scalar_tensor_tensor(out=blk_of(projT, blk + SCV, d, TP), in0=blk_of(projT, blk + SCC, 0, TP - d),
                                              scalar=weight(blk + (SW + 8 * (2 - d))), in1=blk_of(projT, blk + SCV, d, TP),
                                              op0=ALU.mult, op1=ALU.add))
            st.n, st.off = n0 + 3 * KB, 0
            u = projT[:, SCV:SCV + 8, :]
            emptied(v, "sst")
            old = ssT[:].rearrange("p b (s k) -> p b s k", k=2)
            v.wait_ge(S["convolved"], 1)
            for k in range(2):
                st(v.tensor_tensor(out=tmp[:, 0:8], in0=old[:, :, :, k],
                                   in1=bc(par[:, 0, SW + 8 * k:SW + 8 * k + 8], TS), op=ALU.mult))
                st(v.tensor_tensor(out=u[:, :, TP:T], in0=u[:, :, TP:T], in1=tmp[:, 0:8], op=ALU.add))
            emptied(v, "proj", 63)
            st(v.tensor_tensor(out=ubr, in0=ubr, in1=u, op=ALU.mult))
            v.wait_ge(S["gb_sigmoid"], 1)
            v.tensor_tensor(out=ubr, in0=ubr, in1=projT[:, GB:GB + 8, :], op=ALU.mult).then_inc(S["ubr_ready"], 1)
            v.wait_ge(S["ubr_ready"], 1)

            b = filled(v, "acum")
            done(v.tensor_copy(small[:, 0:64], b[:, 0:64]))
            emptied(v, "acum")
            st(v.tensor_tensor(out=small[:, 64:80], in0=small[:, 32:48], in1=small[:, 0:16], op=ALU.subtract))
            st(v.tensor_tensor(out=small[:, 80:96], in0=small[:, 64:80], in1=small[:, 48:64], op=ALU.add))
            v.tensor_tensor(out=small[:, 96:112], in0=small[:, 48:64], in1=small[:, 16:32],
                            op=ALU.subtract).then_inc(S["acum_read"], 1)

            def heads(x, n):
                return x.rearrange("p (h n) -> p h n", h=n)

            v.wait_ge(S["rows_out"], 64)
            for c in range(2):
                for k in range(2):
                    b = filled(v, f"xs{c}", k)
                    done(v.tensor_tensor(out=heads(xdt[:, c, 512 * k:512 * k + 512], 8), in0=heads(b[:, :], 8),
                                         in1=bc(dts[:, 0, c, 8 * k:8 * k + 8], HD), op=ALU.mult))
                emptied(v, f"xs{c}", 1)
                v.wait_ge(S["dw_exp"], 1)
                for i in ((0, 1), (2,))[c]:
                    v.tensor_tensor(out=heads(xdte[:, i], H), in0=heads(xdt[:, c], H),
                                    in1=bc(small[:, 64 + 16 * i:80 + 16 * i], HD), op=ALU.mult)\
                        .then_inc(S["xdte_ready"], 1)
            for c in range(2):
                cols = slice(c * P, c * P + P)
                for g in range(G):
                    n = G * c + g
                    b = filled(v, f"ssd{c}", 3 * g + 1)
                    done(v.tensor_tensor(out=scm[:, n % 2], in0=b[:, 0:P], in1=uinc[:], op=ALU.mult))
                    emptied(v, f"ssd{c}", 3 * g)
                    st(v.tensor_tensor(out=dcy[:, n % 2], in0=bcum[:, n % 2],
                                       in1=bc(small[:, 16 * c + 4 * g:16 * c + 4 * g + 4], P), op=ALU.subtract))
                    v.tensor_scalar(dcy[:, n % 2], dcy[:, n % 2], 0.0, None, ALU.min).then_inc(S["seg_ready"], 1)
                    if c == 1:
                        v.wait_ge(S["eac_ready"], g + 1)
                        v.tensor_tensor(out=cexp, in0=eac, in1=conv[:, 12 + g, cols].unsqueeze(1).to_broadcast([P, 4, P]),
                                        op=ALU.mult).then_inc(S["ce_ready"], 1)
                    v.wait_ge(S["dcy_ready"], n + 1)
                    emptied(v, f"ssd{c}", 3 * g + 1)
                    v.tensor_tensor(out=dcy[:, n % 2], in0=dcy[:, n % 2],
                                    in1=scm[:, n % 2].unsqueeze(1).to_broadcast([P, 4, P]),
                                    op=ALU.mult).then_inc(S["m_ready"], 1)
                    b = filled(v, f"ssd{c}", 3 * g + 2)
                    for i in range(2):
                        ins = v.scalar_tensor_tensor(out=yT[:, 2 * g + i, cols], in0=conv[:, 2 * g + i, cols],
                                                     scalar=dsk[:, 2 * g + i:2 * g + i + 1],
                                                     in1=b[:, i * P:i * P + P], op0=ALU.mult, op1=ALU.add)
                    done(ins)
            emptied(v, "ssd1", 11)
            st(v.memset(tmp[:, 0:8], 0.0))
            v.memset(tmp[:, 8:16], 0.0).then_inc(S["state_free"], 1)

            xs_s = conv[:, 0:8, TP:T]
            b = filled(v, "dec")
            st(v.tensor_tensor(out=dtx, in0=xs_s, in1=b[:, 0:64].rearrange("p (h s) -> p h s", h=8), op=ALU.mult))
            done(v.tensor_copy(dec, b[:, 64:128].rearrange("p (h s) -> p h s", h=8)))
            v.wait_ge(S["dec_ready"], 1)

            def by_group(x):
                return x.rearrange("p (g y) n -> p g y n", y=2)

            def rows_of(b):
                return b[:, :].rearrange("p (g n) -> p g n", g=G).unsqueeze(2).to_broadcast([P, G, 2, P])

            for i in range(TS):
                s_ = sst[:, i % 2]
                v.wait_ge(state_in[i % 2], 16 * (i // 2 + 1))
                st(v.tensor_tensor(out=s_, in0=s_, in1=bc(dec[:, :, i], P), op=ALU.mult))
                b = filled(v, "bcs", 2 * i)
                done(v.tensor_tensor(out=by_group(prod), in0=rows_of(b), in1=by_group(bc(dtx[:, :, i], P)), op=ALU.mult))
                emptied(v, "bcs", 2 * i)
                v.tensor_tensor(out=s_, in0=s_, in1=prod, op=ALU.add).then_inc(S["state_new"], 1)
                v.wait_ge(S["state_new"], i + 1)
                b = filled(v, "bcs", 2 * i + 1)
                done(v.tensor_tensor(out=by_group(prod), in0=rows_of(b), in1=by_group(s_), op=ALU.mult))
                emptied(v, "bcs", 2 * i + 1)
                st(v.tensor_reduce(yT[:, :, TP + i], prod, AX.X, ALU.add))
            st(v.tensor_tensor(out=dtx, in0=xs_s, in1=bc(dsk[:, :], TS), op=ALU.mult))
            v.tensor_tensor(out=yT[:, :, TP:T], in0=yT[:, :, TP:T], in1=dtx, op=ALU.add).then_inc(S["scratch_free"], 1)
            v.wait_ge(S["scratch_free"], 1)
            v.wait_ge(S["z_silu"], 1)
            v.tensor_tensor(out=yT, in0=yT, in1=projT[:, Z:Z + 8, :], op=ALU.mult).then_inc(S["u_ready"], 1)
            v.wait_ge(S["u_ready"], 1)
            emptied(v, "gn", 3)
            st(v.reciprocal(rgrp, rgrp))
            for k in range(KB):
                st(v.scalar_tensor_tensor(out=yT[:, k, :], in0=yT[:, k, :], scalar=pcol(NSSM + k),
                                          in1=rgrp[:, k // 2, :], op0=ALU.mult, op1=ALU.mult))
            v.wait_ge(S["ga_sigmoid"], 1)
            st(v.tensor_tensor(out=merged, in0=yT, in1=projT[:, GA:GA + 8, :], op=ALU.mult))
            v.tensor_tensor(out=merged, in0=merged, in1=ubr, op=ALU.add).then_inc(S["merged_ready"], 1)

            def add_to_h(name):
                for k in range(KB):
                    b = filled(v, name, k)
                    done(v.tensor_tensor(out=hT[:, k, :], in0=b[:, 0:T], in1=hT[:, k, :], op=ALU.add))
                emptied(v, name, 7)

            add_to_h("wo")
            norm("h1ss", xnT, hT, rinv[:], T, NXA, "xn_ready")
            for n in range(4):
                t, hh = n // 2, n % 2
                j = 8 * t + 2 * hh
                b = filled(v, "att", n)
                v.tensor_reduce(small[:, j:j + 2], b[:, :].rearrange("p (h m) -> p h m", h=2), AX.X, ALU.max,
                                negate=True).then_inc(S["att_max"], 1)
            for t in range(2):
                emptied(v, "att", 2 * t + 1)
                r = small[:, 16 + 8 * t:20 + 8 * t]
                st(v.reciprocal(r, r))
                v.tensor_tensor(out=pr[:, t], in0=pr[:, t], in1=bc(r, 256), op=ALU.mult).then_inc(S["probs_ready"], 1)
            for u in range(2):
                v.wait_ge(state_out[u], 16 * (TS // 2))
            for i in range(TS):
                keys = chunk_in(v, CH["k"] + i // 2).rearrange("p (b m n) c -> p b m (n c)", b=2, m=2)
                for hh in range(2):
                    b = filled(v, "qb", 2 * i + hh)
                    for h in range(2):
                        for m in range(2):
                            c = m * 32 + i * 4 + 2 * hh + h
                            ins = v.tensor_tensor_reduce(junk, keys[:, i % 2, m, (2 * hh + h) * 256:(2 * hh + h + 1) * 256],
                                                         b[:, h * 256:h * 256 + 256], 1.0, 0.0, ALU.mult, ALU.add,
                                                         scs[:, c:c + 1])
                            if h + m < 2:
                                st(ins)
                    done(ins)
                    emptied(v, "qb", 2 * i + hh)
            b = filled(v, "sT")
            st(v.tensor_reduce(small[0:32, 32:33], b[0:32, 0:256], AX.X, ALU.max, negate=True))
            done(v.tensor_copy(sP, b[0:32, 0:256]))
            v.wait_ge(S["s_exp"], 1)
            st(v.reciprocal(small[0:32, 33:34], small[0:32, 33:34]))
            v.tensor_scalar(sP, sP, small[0:32, 33:34], None, ALU.mult).then_inc(S["s_probs"], 1)
            add_to_h("xo")
            norm("h2ss", xnT, hT, rinv[:], T, NMOE, "xn_ready")

            v.wait_ge(S["kv_out"], 32)
            v.wait_ge(S["fin_out"], 16)
            st(v.memset(gts, 0.0))
            st(v.memset(eqm, 0.0))
            st(v.memset(msk, 0.0))
            st(v.memset(zer, 0.0))
            b = filled(v, "rt")
            for t, (_, n) in enumerate(TILES):
                ins = v.tensor_tensor(out=lg[0:n, t], in0=b[0:n, t * E:t * E + E], in1=brt[0:n, :], op=ALU.add)
            done(ins)
            emptied(v, "rt")
            for t, (_, n) in enumerate(TILES):
                l, tp = lg[0:n, t], top[0:n, t]
                st(v.max(tp, l))
                st(v.tensor_scalar(gts[0:n, t], l, tp[:, 0:1], None, ALU.subtract))
            v.memset(top[:, 2, 4:8], 0.0).then_inc(S["lg_ready"], 1)
            v.wait_ge(S["lg_ready"], 1)
            for t, (_, n) in enumerate(TILES):
                l, tp, nd = lg[0:n, t], top[0:n, t], need[0:n, t:t + 1]
                st(v.tensor_scalar(msk[0:n, t], l, tp[:, 3:4], None, ALU.is_gt))
                st(v.tensor_scalar(eqm[0:n, t], l, tp[:, 3:4], None, ALU.is_equal))
                st(v.tensor_reduce(nd, msk[0:n, t], AX.X, ALU.add))
                st(v.tensor_scalar(nd, nd, -1.0, 4.0, ALU.mult, ALU.add))
                st(v.tensor_tensor_scan(cum[0:n, t], eqm[0:n, t], zer[0:n, :], 0.0, ALU.add, ALU.add))
                st(v.tensor_scalar(cum[0:n, t], cum[0:n, t], nd, None, ALU.is_le))
                st(v.tensor_tensor(out=eqm[0:n, t], in0=eqm[0:n, t], in1=cum[0:n, t], op=ALU.mult))
                ins = v.tensor_tensor(out=msk[0:n, t], in0=msk[0:n, t], in1=eqm[0:n, t], op=ALU.add)
                if t < 2:
                    st(ins)
            ins.then_inc(S["mask_ready"], 1)
            v.wait_ge(S["mask_ready"], 1)
            v.wait_ge(S["lg_exp"], 1)
            st(v.tensor_tensor(out=gts, in0=gts, in1=msk, op=ALU.mult))
            for t, (_, n) in enumerate(TILES):
                nd = need[0:n, 4 + t:5 + t]
                st(v.tensor_reduce(nd, gts[0:n, t], AX.X, ALU.add))
                st(v.reciprocal(nd, nd))
                st(v.tensor_scalar(gts[0:n, t], gts[0:n, t], nd, None, ALU.mult))
            b = filled(v, "rank")
            for t, (_, n) in enumerate(TILES):
                st(v.scalar_tensor_tensor(out=eqm[0:n, t], in0=b[0:n, t * E:t * E + E], scalar=1.0, in1=msk[0:n, t],
                                          op0=ALU.add, op1=ALU.mult))
            done(v.tensor_reduce(small[0:1, 0:1], b[0:1, 3 * E:4 * E], AX.X, ALU.max))
            for p in range(MAXP + 1):
                st(v.tensor_scalar(rkp[:, :, p * E:p * E + E], eqm, -1.0 - CAP * p, None, ALU.add))
            emptied(v, "rank")
            st(v.tensor_scalar(small[0:1, 1:2], small[0:1, 0:1], float(CAP), None, ALU.is_gt))
            for p in range(2, MAXP):
                st(v.scalar_tensor_tensor(out=small[0:1, 1:2], in0=small[0:1, 0:1], scalar=float(CAP * p),
                                          in1=small[0:1, 1:2], op0=ALU.is_gt, op1=ALU.add))
            v.tensor_copy(npass[0:1, 0:1], small[0:1, 1:2]).then_inc(S["passes_ready"], 1)

            def select(it, gated):
                dst = selG if gated else selT
                for t, (_, n) in enumerate(TILES):
                    for j in range(2):
                        g = gts[0:n, t, bass.ds((it % PAIRS) * 2 + j, 1)] if gated else None
                        ins = v.tensor_scalar(dst[0:n, t, j * CAP:j * CAP + CAP], iota[0:n, :],
                                              rkp[0:n, t, bass.ds(it * 2 + j, 1)], g,
                                              ALU.is_equal, ALU.mult if gated else ALU.bypass)
                ins.then_inc(S["selg_ready" if gated else "sel_ready"], 1)

            for k, name in enumerate(("gu_read", "gu_read", "dn_read", "misc_read", "misc_read")):
                v.memset(moeT[:, 2 * k:2 * k + 2] if k < 4 else zer, 0.0).then_inc(S[name], 1)
            v.wait_ge(S["consts_set"], 2)
            select(0, False)
            for name, k in (("gu_read", 2), ("dn_read", 1), ("misc_read", 2)):
                v.wait_ge(S[name], k)
            v.wait_ge(S["passes_ready"], 1)
            n = v.value_load(npass[0:1, 0:1], min_val=0, max_val=MAXP - 1)
            n0 = st.n

            def eight(b):
                return b[:, :].rearrange("p (j n) -> p j n", j=8)

            with v.Fori(0, n * PAIRS + PAIRS) as it:
                st.n, st.off = n0, it * 6
                pair = it % PAIRS
                for e in range(2):
                    v.wait_ge(S["chunk_done"], it * 12 + (4 * e + 2))
                    v.tensor_tensor(out=gate, in0=eight(bank[0]), in1=bc(bgu[:, bass.ds(pair * 32 + 16 * e, 8)], CAP),
                                    op=ALU.add).then_inc(S["gu_read"], 1)
                    v.wait_ge(S["gu_read"], it * 4 + (2 * e + 3))
                    v.tensor_scalar(gate, gate, LIMIT, None, ALU.min).then_inc(S["bias_gate"], 1)
                    v.wait_ge(S["chunk_done"], it * 12 + (4 * e + 4))
                    v.tensor_tensor(out=up, in0=eight(bank[1]), in1=bc(bgu[:, bass.ds(pair * 32 + (16 * e + 8), 8)], CAP),
                                    op=ALU.add).then_inc(S["gu_read"], 1)
                    v.wait_ge(S["gu_read"], it * 4 + (2 * e + 4))
                    st(v.tensor_scalar(up, up, LIMIT, -LIMIT, ALU.min, ALU.max))
                    v.wait_ge(S["bias_gate"], it * 2 + (e + 1))
                    st(v.scalar_tensor_tensor(out=up, in0=up, scalar=1.0, in1=gate, op0=ALU.add, op1=ALU.mult))
                    v.wait_ge(S["sig_ready"], it * 2 + (e + 1))
                    v.tensor_tensor(out=act[e], in0=up, in1=sig, op=ALU.mult).then_inc(S["h_act"], 1)
                    if e == 0:
                        v.wait_ge(S["xg_full"], it + 1)
                        select(it + 1, False)
                        select(it, True)
                for e in range(2):
                    v.wait_ge(S["chunk_done"], it * 12 + (10 + 2 * e))
                    v.tensor_tensor(out=ypT[:, :, e * CAP:e * CAP + CAP], in0=eight(bank[2]),
                                    in1=bc(bdn[:, bass.ds(pair * 16 + 8 * e, 8)], CAP), op=ALU.add)\
                        .then_inc(S["dn_read"], 1)
                for k in range(12):
                    b = bank[6 + k % 2]
                    v.wait_ge(S["misc_full"], it * 12 + (k + 1))
                    if k == 0:
                        ins = v.tensor_copy(gT[:, 0:P], b[:, 0:P])
                    elif k == 1:
                        ins = v.tensor_copy(gT[:, P:T], b[:, 0:T - P])
                    elif k < 4:
                        ins = v.tensor_copy(ytok[:, (k - 2) * 512:(k - 1) * 512], b[:, :])
                    else:
                        ins = v.tensor_tensor(out=moeT[:, k - 4, :], in0=b[:, 0:T], in1=moeT[:, k - 4, :], op=ALU.add)
                    ins.then_inc(S["misc_read"], 1)
                st(v.memset(zer, 0.0))
                st(v.memset(zer, 0.0))
            v.wait_ge(S["misc_read"], n * (12 * PAIRS) + (12 * PAIRS + 2))
            v.tensor_tensor(out=hT[:], in0=hT[:], in1=moeT, op=ALU.add).then_inc(S["moe_summed"], 1)
            v.wait_ge(S["moe_summed"], 1)
            norm("fss", xnT, hT, rinv[:], T, NFIN, "final_normed")

        @block.tensor
        def _(pe):
            last = [None]

            def mm(out, lhsT, rhs, start=True, stop=True):
                last[0] = pe.matmul(out, lhsT, rhs, start=start, stop=stop)
                return last[0]

            def close():
                last[0].then_inc(bank_filled, 1)

            def turn(out, in_):
                k = in_.shape[0]
                last[0] = pe.transpose(out, in_, ident[0:k, 0:k])

            pe.wait_ge(S["consts_set"], 2)
            pe.wait_ge(params_in, 16 * 11)
            for k in range(2):
                b = free_bank(pe, "par", k)
                for i in range(4):
                    if k == 0 and i == 1:
                        turn(b[:, i * P:i * P + 24], stage[0:24, i, :])
                    else:
                        turn(b[:, i * P:i * P + P], stage[:, 4 * k + i, :])
                close()
            pe.wait_ge(conv_in, 32)
            b = free_bank(pe, "mst")
            for i in range(XB):
                turn(b[:, i * 24:i * 24 + 24], mstate[:, i // 2, (i % 2) * P:(i % 2) * P + P])
            close()
            b = free_bank(pe, "sst")
            for i in range(KB):
                turn(b[:, i * 16:i * 16 + 16], sstate[:, i // 2, (i % 2) * P:(i % 2) * P + P])
            close()
            pe.wait_ge(x_in, 32)
            for k in range(KB):
                b = free_bank(pe, "xT", k)
                for t, (c, n) in enumerate(TILES):
                    turn(b[:, c:c + n], xtokin[0:n, t, k * P:k * P + P])
                close()
            pe.wait_ge(mem_in, 32)
            for k in range(4):
                b = free_bank(pe, "memT", k)
                for i in range(2):
                    for t in range(2):
                        turn(b[:, i * 256 + t * P:i * 256 + t * P + P], memv[t][:, k, i * P:i * P + P])
                close()

            def sum_squares(name, sq, n):
                b = free_bank(pe, name)
                for k in range(KB):
                    mm(b[:, 0:n], ones[:], sq[:, k, 0:n], k == 0, k == KB - 1)
                close()

            pe.wait_ge(S["x_squared"], 1)
            sum_squares("xss", sqx, T)
            pe.wait_ge(S["mem_squared"], 1)
            sum_squares("mss", sqm, NM)
            pe.wait_ge(S["x_normed"], 8)
            pe.wait_ge(small_in, 112)
            b = free_bank(pe, "dt")
            for t, (c, n) in enumerate(TILES):
                for k in range(KB):
                    mm(b[0:n, t * H:t * H + H], xnT[:, k, c:c + n], wdt[:, k, :], k == 0, k == KB - 1)
            close()
            base = JOB["proj"]
            before = emptied_before(base, A_)
            with pe.Fori(0, 4) as it:
                for j in range(16):
                    if j % 4 == 0:
                        pe.wait_ge(slot_full[j // 4], it * 16 + 16)
                    if base + j - 8 == JOB["dt"]:
                        emptied(pe, "dt")
                    pe.wait_ge(act_emptied, it * 16 + (emptied_before(base + j - 7, A_) if j < 8 else before + j - 7))
                    for k in range(KB):
                        mm(bank[(base + j) % 8][:, 0:T], ring[:, j // 4, k, (j % 4) * P:(j % 4) * P + P], xnT[:, k, :],
                           k == 0, k == KB - 1)
                    close()

            def project(name, chunk, rhs):
                n = rhs.shape[2]
                for j in range(KB):
                    if j % 4 == 0:
                        w = chunk_in(pe, chunk + j // 4)
                    b = free_bank(pe, name, j)
                    for k in range(KB):
                        mm(b[:, 0:n], w[:, k, (j % 4) * P:(j % 4) * P + P], rhs[:, k, :], k == 0, k == KB - 1)
                    close()

            emptied(pe, "proj", 63)
            for k in range(4):
                b = free_bank(pe, "mrow", k)
                for i in range(4):
                    turn(b[0:11, i * P:i * P + P], projT[:, 4 * k + i, T - 11:T])
                close()
            pe.wait_ge(S["cv_ready"], 1)
            for k in range(2):
                b = free_bank(pe, "srow", k)
                for i in range(4):
                    turn(b[0:10, i * P:i * P + P], projT[:, SCC + 4 * k + i, T - 10:T])
                close()
            pe.wait_ge(S["dt_ready"], 1)
            b = free_bank(pe, "acum")
            for c in range(2):
                mm(b[:, c * H:c * H + H], uinc[:], dta[:, c, :])
                mm(b[:, 32 + c * H:32 + c * H + H], ones[:], dta[:, c, :])
            close()
            pe.wait_ge(S["conv_silu"], 1)
            for c in range(2):
                cols = slice(c * P, c * P + P)
                for k in range(2):
                    b = free_bank(pe, f"xs{c}", k)
                    for i in range(4):
                        turn(b[:, i * P:i * P + P], conv[:, 4 * k + i, cols])
                    close()
                b = free_bank(pe, f"btok{c}")
                for i in range(4):
                    turn(b[:, i * P:i * P + P], conv[:, 8 + i, cols])
                close()
            emptied(pe, "btok1")
            pe.wait_ge(S["xdte_ready"], 3)
            for k in range(2):
                b = free_bank(pe, "sin", k)
                for i in range(2):
                    g = 2 * k + i
                    mm(b[:, i * 256:i * 256 + 256], btok[:, 0, g * P:g * P + P], xdte[:, 0, g * 256:g * 256 + 256])
                close()
            for k in range(2):
                b = free_bank(pe, "fin", k)
                for i in range(4):
                    h = 4 * k + i
                    for c in range(2):
                        mm(b[:, i * P:i * P + P], xdte[:, 1 + c, h * P:h * P + P],
                           btok[:, c, (h // 2) * P:(h // 2) * P + P], c == 0, c == 1)
                close()
            emptied(pe, "sin", 1)
            for c in range(2):
                cols = slice(c * P, c * P + P)
                for g in range(G):
                    b = free_bank(pe, f"ssd{c}", 3 * g)
                    for i in range(4):
                        mm(b[:, i * P:i * P + P], dta[:, c, 4 * g + i:4 * g + i + 1].to_broadcast([P, P]), uinc[:])
                    close()
                    b = free_bank(pe, f"ssd{c}", 3 * g + 1)
                    mm(b[:, 0:P], conv[:, 8 + g, cols], conv[:, 12 + g, cols])
                    close()
                    b = free_bank(pe, f"ssd{c}", 3 * g + 2)
                    n = G * c + g
                    pe.wait_ge(S["m_ready"], n + 1)
                    if c == 1:
                        pe.wait_ge(S["ce_ready"], g + 1)
                    for i in range(4):
                        h = 4 * g + i
                        out = b[64 * (i % 2):64 * (i % 2) + 64, (i // 2) * P:(i // 2) * P + P]
                        mm(out, xdt[:, c, h * HD:h * HD + HD], dcy[:, n % 2, i, :], True, c == 0)
                        if c == 1:
                            mm(out, sinT[:, h * HD:h * HD + HD], cexp[:, i, :], False, True)
                    close()
            b = free_bank(pe, "dec")
            for i in range(KB):
                for j, src in enumerate((dts[0:TS, 0, 2], dta[0:TS, 2])):
                    for y in range(2):
                        mm(b[HD * y:HD * y + HD, 64 * j + 8 * i:64 * j + 8 * i + 8],
                           src[:, 2 * i + y:2 * i + y + 1].to_broadcast([TS, HD]), ident[0:TS, 0:TS])
            close()
            for i in range(TS):
                for j in range(2):
                    b = free_bank(pe, "bcs", 2 * i + j)
                    for g in range(G):
                        mm(b[:, g * P:g * P + P], conv[:, 8 + 4 * j + g, TP + i:TP + i + 1].to_broadcast([P, P]), ident[:])
                    close()
            for name, chunk in (("kp", CH["w_xk"]), ("vp", CH["w_xv"])):
                for nh in range(2):
                    w = chunk_in(pe, chunk + nh)
                    for mt in range(2):
                        b = free_bank(pe, name, 2 * nh + mt)
                        for k in range(KB):
                            mm(b[:, :], mnT[:, k, mt * P:mt * P + P], w[:, k, :], k == 0, k == KB - 1)
                        close()
            emptied(pe, "kp", 3)
            for k in range(4):
                b = free_bank(pe, "kT", k)
                for i in range(2):
                    for mt in range(2):
                        turn(b[:, i * 256 + mt * P:i * 256 + mt * P + P],
                             ktok[:, mt, (2 * k + i) * P:(2 * k + i + 1) * P])
                close()
            pe.wait_ge(S["u_squared"], 1)
            for g in range(G):
                b = free_bank(pe, "gn", g)
                for k in range(2):
                    mm(b[:, 0:T], ones[:], sqg[:, 2 * g + k, :], k == 0, k == 1)
                close()
            pe.wait_ge(S["merged_ready"], 1)
            project("wo", CH["w_out"], merged)
            pe.wait_ge(S["h_squared"], 1)
            sum_squares("h1ss", sqh, T)
            pe.wait_ge(S["xn_ready"], 8)
            project("q", CH["w_xq"], xnT)
            emptied(pe, "q", 7)
            emptied(pe, "kT", 3)
            for t in range(2):
                for hh in range(2):
                    b = free_bank(pe, "att", 2 * t + hh)
                    for i in range(2):
                        h = 2 * hh + i
                        for k in range(2):
                            mm(b[:, i * 256:i * 256 + 256], qT[:, 2 * h + k, t * P:t * P + P], kT[:, 2 * h + k, :],
                               k == 0, k == 1)
                    close()
            pe.wait_ge(S["probs_ready"], 2)
            for h in range(4):
                b = free_bank(pe, "pT", h)
                for mt in range(2):
                    for t in range(2):
                        turn(b[:, mt * 256 + t * P:mt * 256 + t * P + P], pr[:, t, h, mt * P:mt * P + P])
                close()
            emptied(pe, "vp", 3)
            emptied(pe, "pT", 3)
            for k in range(4):
                b = free_bank(pe, "o", k)
                for i in range(2):
                    for mt in range(2):
                        mm(b[:, i * 256:i * 256 + 256], vtok[:, mt, (2 * k + i) * P:(2 * k + i + 1) * P],
                           pT[:, k, mt, :], mt == 0, mt == 1)
                close()
            for i in range(TS):
                for hh in range(2):
                    b = free_bank(pe, "qb", 2 * i + hh)
                    for k in range(4):
                        mm(b[:, k * P:k * P + P], qT[:, 4 * hh + k, TP + i:TP + i + 1].to_broadcast([P, P]), ident[:])
                    close()
            emptied(pe, "qb", 15)
            b = free_bank(pe, "sT")
            for m in range(2):
                turn(b[0:32, m * P:m * P + P], scs[:, m * 32:m * 32 + 32])
            close()
            pe.wait_ge(S["s_probs"], 1)
            b = free_bank(pe, "sP")
            for m in range(2):
                turn(b[:, m * 32:m * 32 + 32], sP[:, m * P:m * P + P])
            close()
            emptied(pe, "sP")
            for i in range(4):
                vals = chunk_in(pe, CH["v"] + i).rearrange("p (b m n) c -> p b m (n c)", b=2, m=2)
                b = free_bank(pe, "so", i)
                for s_ in range(2):
                    for k in range(KB):
                        for m in range(2):
                            c = (2 * i + s_) * 4 + k // 2
                            mm(b[:, s_ * 8 + k:s_ * 8 + k + 1], vals[:, s_, m, k * P:k * P + P], sPT[:, m, c:c + 1],
                               m == 0, m == 1)
                close()
            emptied(pe, "so", 3)
            project("xo", CH["w_xo"], oT)
            pe.wait_ge(S["h_squared"], 2)
            sum_squares("h2ss", sqh, T)
            pe.wait_ge(S["xn_ready"], 16)
            b = free_bank(pe, "rt")
            for t, (c, n) in enumerate(TILES):
                for k in range(KB):
                    mm(b[0:n, t * E:t * E + E], xnT[:, k, c:c + n], wrt[:, k, :], k == 0, k == KB - 1)
            close()
            pe.wait_ge(S["mask_ready"], 1)
            b = free_bank(pe, "rank")
            for t, (_, n) in enumerate(TILES):
                for u in range(t):
                    mm(b[0:n, t * E:t * E + E], ones[:, 0:n], msk[:, u], u == 0, False)
                mm(b[0:n, t * E:t * E + E], ustr[0:n, 0:n], msk[0:n, t], t == 0, True)
            for t, (_, n) in enumerate(TILES):
                mm(b[:, 3 * E:4 * E], ones[0:n, :], msk[0:n, t], t == 0, t == 2)
            close()
            for t, (c, n) in enumerate(TILES):
                for k in range(2):
                    b = free_bank(pe, "xtok", 2 * t + k)
                    for i in range(4):
                        turn(b[0:n, i * P:i * P + P], xnT[:, 4 * k + i, c:c + n])
                    close()
            emptied(pe, "xtok", 5)
            emptied(pe, "rank")

            def gather(n):
                pe.wait_ge(S["sel_ready"], n)
                pe.wait_ge(S["xg_ready"], n * 2)
                for k in range(KB):
                    for t, (_, r) in enumerate(TILES):
                        mm(bank[3 + k // 4][:, (k % 4) * P:(k % 4) * P + P], xtok[0:r, t, k * P:k * P + P],
                           selT[0:r, t, :], t == 0, t == 2)
                last[0].then_inc(S["xg_full"], 1)

            gather(1)
            pe.wait_ge(S["passes_ready"], 1)
            n = pe.value_load(npass[0:1, 0:1], min_val=0, max_val=MAXP - 1)
            with pe.Fori(0, n * PAIRS + PAIRS) as it:
                pe.wait_ge(S["xg_ready"], it * 2 + 4)
                for j in range(12):
                    c = NCH + j
                    w = slot(c)
                    pe.wait_ge(slot_full[c % SLOTS], it * 48 + 16 * (c // SLOTS + 1))
                    if j < 8:
                        e, half, b = j // 4, j % 2, bank[(j % 4) // 2]
                        if half == 0:
                            pe.wait_ge(S["gu_read"], it * 4 + (j // 2 + 1))
                        rhs = xg[:, :, e * CAP:e * CAP + CAP]
                    else:
                        e, half, b = (j - 8) // 2, j % 2, bank[2]
                        if half == 0:
                            pe.wait_ge(S["h_act"], it * 2 + (e + 1))
                            pe.wait_ge(S["dn_read"], it * 2 + (e + 1))
                        rhs = act[e]
                    for i in range(4):
                        c0 = (4 * half + i) * CAP
                        for k in range(KB):
                            mm(b[:, c0:c0 + CAP], w[:, k, i * P:i * P + P], rhs[:, k, :], k == 0, k == KB - 1)
                    last[0].then_inc(S["chunk_done"], 1)
                gather(it + 2)

                def misc(k):
                    pe.wait_ge(S["misc_read"], it * 12 + (k + 1))
                    return bank[6 + k % 2]

                pe.wait_ge(S["selg_ready"], it + 1)
                b = misc(0)
                turn(b[:, 0:P], selG[:, 0, :])
                last[0].then_inc(S["misc_full"], 1)
                b = misc(1)
                turn(b[:, 0:P], selG[:, 1, :])
                turn(b[:, P:P + TS], selG[0:TS, 2, :])
                last[0].then_inc(S["misc_full"], 1)
                pe.wait_ge(S["dn_read"], it * 2 + 3)
                for k in range(2):
                    b = misc(2 + k)
                    for i in range(4):
                        turn(b[:, i * P:i * P + P], ypT[:, 4 * k + i, :])
                    last[0].then_inc(S["misc_full"], 1)
                pe.wait_ge(S["misc_read"], it * 12 + 6)
                for k in range(KB):
                    b = misc(4 + k)
                    mm(b[:, 0:T], ytok[:, k * P:k * P + P], gT)
                    last[0].then_inc(S["misc_full"], 1)
            pe.wait_ge(S["h_squared"], 3)
            sum_squares("fss", sqh, T)
            pe.wait_ge(S["final_normed"], 8)
            for t, (c, n) in enumerate(TILES):
                for k in range(2):
                    b = free_bank(pe, "yT", 2 * t + k)
                    for i in range(4):
                        turn(b[0:n, i * P:i * P + P], xnT[:, 4 * k + i, c:c + n])
                    close()


_INS = ["x_prompt", "x_sample", "mem_prompt", "state_ssm", "state_mamba_conv", "state_short_conv",
        "cache_mem_k", "cache_mem_v", "norm_mix", "w_in", "w_mconv", "b_mconv", "dt_bias", "a_log", "d_skip",
        "norm_ssm", "w_sconv", "w_out", "norm_xattn", "norm_mem", "w_xq", "w_xk", "w_xv", "w_xo", "norm_moe",
        "w_router", "b_router", "w_gate_up", "b_gate_up", "w_down", "b_down", "norm_final"]
_OUTS = [(1, 256, 1024), (8, 1, 1024), (1, 1, 16, 64, 128), (1, 1, 3, 2048), (1, 1, 2, 1024),
         (1, 1, 256, 4, 256), (1, 1, 256, 4, 256), (1, 8, 16, 64, 128), (1, 8, 3, 2048), (1, 8, 2, 1024)]


def kernel(**inputs):
    import numpy as _np
    import concourse.bacc as _bacc
    from concourse import mybir as _mybir
    from concourse.bass_utils import run_bass_kernel_spmd as _run

    nc = _bacc.Bacc("TRN2", target_bir_lowering=False, num_devices=1)
    arrays, args = {}, {}
    for name in _INS:
        x = _np.ascontiguousarray(inputs[name])
        arrays[f"in_{name}"] = x
        args[name] = nc.dram_tensor(f"in_{name}", x.shape, _mybir.dt.from_np(x.dtype), kind="ExternalInput").ap()
    outs = [nc.dram_tensor(f"out_{i}", shape, _mybir.dt.float32, kind="ExternalOutput").ap()
            for i, shape in enumerate(_OUTS)]
    build(nc, args, outs)
    r = _run(nc, [arrays], core_ids=[0])
    return tuple(r.results[0][f"out_{i}"] for i in range(len(_OUTS)))
```

```python
from contextlib import ExitStack

import concourse.bass as bass
from concourse import mybir

F32 = mybir.dt.float32
I32 = mybir.dt.int32
ALU = mybir.AluOpType
ACT = mybir.ActivationFunctionType
AX = mybir.AxisListType

P = 128
D = 1024
KB = D // P
TP, TS = 256, 8
T = TP + TS
TILES = [(0, 128), (128, 128), (256, 8)]
H, HD, NST, G = 16, 64, 128, 4
CONV = 2048
XB = CONV // P
NM, XH = 256, 4
E, CAP, LIMIT, ALPHA = 32, 64, 7.0, 1.702
PAIRS, MAXP = E // 2, -(-T // CAP)
SLOTS, CW = 4, 512
EPS = 1e-6
A_, D_ = "act", "dve"

PLAN = [("par", 2, A_), ("mst", 1, A_), ("sst", 1, A_), ("xT", 8, A_), ("memT", 4, A_),
        ("xss", 1, A_), ("mss", 1, A_), ("dt", 1, D_), ("proj", 64, A_),
        ("mrow", 4, A_), ("srow", 2, A_), ("acum", 1, D_)]
for _c in range(2):
    PLAN += [(f"xs{_c}", 2, D_), (f"btok{_c}", 1, A_)]
PLAN += [("sin", 2, A_), ("fin", 2, A_)]
for _c in range(2):
    PLAN += [(f"ssd{_c}", 12, None)]
PLAN += [("dec", 1, D_)] + [("bcs", 16, D_)]
PLAN += [("kp", 4, A_), ("vp", 4, A_), ("kT", 4, A_), ("gn", 4, A_), ("wo", 8, D_), ("h1ss", 1, A_),
         ("q", 8, A_), ("att", 4, A_), ("pT", 4, A_), ("o", 4, A_), ("qb", 16, D_), ("sT", 1, D_),
         ("sP", 1, A_), ("so", 4, A_), ("xo", 8, D_), ("h2ss", 1, A_), ("rt", 1, D_), ("rank", 1, D_),
         ("xtok", 6, A_), ("gtT", 1, D_), ("bd", 8, D_), ("fss", 1, A_), ("yT", 6, A_)]

JOB, WHO = {}, []
for _n, _k, _w in PLAN:
    JOB[_n] = len(WHO)
    WHO += ([A_, D_, D_] * 4) if _w is None else [_w] * _k


def emptied_before(i, who):
    return sum(1 for w in WHO[:i] if w == who)


class Steps:

    def __init__(self, eng, sem):
        self.eng, self.sem, self.n, self.off = eng, sem, 0, 0

    def __call__(self, ins):
        self.n += 1
        ins.then_inc(self.sem, 1)
        self.eng.wait_ge(self.sem, self.off + self.n)


def build(nc, a, outs):
    with ExitStack() as ctx:
        def sb(name, shape, dt=F32):
            return ctx.enter_context(nc.sbuf_tensor(name, shape, dt))

        def sem(name):
            return ctx.enter_context(nc.semaphore(name))

        bank = [ctx.enter_context(nc.psum_tensor(f"bank{i}", [P, 512], F32)) for i in range(8)]

        ring = sb("ring", [P, SLOTS, 8, CW])
        projT = sb("projT", [P, 64, T])
        conv = sb("conv", [P, XB, T])
        hT = sb("hT", [P, KB, T])
        xnT = sb("xnT", [P, KB, T])
        par = sb("par", [P, 6, P])
        bdn = sb("bdn", [E, D])
        flat = sb("flat", [P, 4096])
        mnT = sb("mnT", [P, KB, NM])
        ident, ones, uinc, ustr = (sb(n, [P, P]) for n in ("ident", "ones", "uinc", "ustr"))
        iota = sb("iota", [P, CAP])
        eps = sb("eps", [P, 1])
        wdt = sb("wdt", [P, KB, H])
        wrt = sb("wrt", [P, KB, E])
        dtb, alog, brt = sb("dtb", [P, H]), sb("alog", [P, H]), sb("brt", [P, E])
        dsk = sb("dsk", [P, KB])
        dts = sb("dts", [P, 6, 3, H])
        dta = sb("dta", [P, 3, H])
        small = sb("small", [P, 320])
        rinv = sb("rinv", [P, T])
        npass = sb("npass", [1, 1], I32)

        XBC, Z, GA, SCC, SCV, SCB, GB = 0, 16, 24, 32, 40, 48, 56

        stage = flat[:, 0:1024].rearrange("p (a b) -> p a b", a=8)
        xtokin = flat[:, 1024:4096].rearrange("p (a b) -> p a b", a=3)
        mrows = flat[0:11, 0:2048]
        srows = flat[0:10, 2048:3072]
        memin = projT[:, 0:8, 0:256]
        memv = [projT[:, 4 * i:4 * i + 4, 0:256] for i in range(2)]
        sqx = projT[:, 8:16, :]
        sqm = projT[:, 16:24, 0:NM]
        mstate = conv[0:24, 0:8, 0:256]
        sstate = conv[0:16, 8:12, 0:256]
        msT = sb("msT", [P, XB, 24])
        ssT = sb("ssT", [P, KB, 16])
        tmp = flat[:, 3072:3200].rearrange("p (b n) -> p b n", n=TS)
        r1 = projT[:, 0:16, :].rearrange("p a b -> p (a b)")
        r3 = projT[:, SCC:SCC + 16, :].rearrange("p a b -> p (a b)")
        xdt = r1[:, 0:2048].rearrange("p (c n) -> p c n", c=2)
        btok = r1[:, 2048:3072].rearrange("p (c n) -> p c n", c=2)
        finst = r1[:, 3072:4096].rearrange("p (h n) -> p h n", h=8)
        xdte = flat[:, 0:3072].rearrange("p (v n) -> p v n", v=3)
        sinT = flat[:, 3072:4096]
        bcum = r3[:, 0:1024].rearrange("p (u h l) -> p u h l", u=2, h=4)
        dcy = r3[:, 1024:2048].rearrange("p (u h l) -> p u h l", u=2, h=4)
        scm = r3[:, 2048:2304].rearrange("p (u l) -> p u l", u=2)
        cexp = r3[:, 2304:2816].rearrange("p (h l) -> p h l", h=4)
        eac = r3[:, 2816:3328].rearrange("p (h l) -> p h l", h=4)
        dtx = r3[:, 3328:3392].rearrange("p (h b) -> p h b", h=8)
        dec = r3[:, 3392:3456].rearrange("p (h b) -> p h b", h=8)
        yT = projT[:, GB:GB + 8, :]
        sst = r1[:, 0:2048].rearrange("p (u h n) -> p u h n", u=2, h=8)
        prod = flat[:, 0:1024].rearrange("p (h n) -> p h n", h=8)
        ktok = r3[:, 0:2048].rearrange("p (m n) -> p m n", m=2)
        vtok = r3[:, 2048:4096].rearrange("p (m n) -> p m n", m=2)
        kT = mnT
        ubr = projT[:, SCB:SCB + 8, :]
        sqg = conv[:, 0:8, :]
        merged = projT[:, Z:Z + 8, :]
        rgrp = conv[:, 8:12, :]
        qT = projT[:, Z:Z + 8, :]
        pr = flat[:, 0:2048].rearrange("p (t h m) -> p t h m", t=2, h=4)
        pT = flat[:, 2048:4096].rearrange("p (h m t) -> p h m t", h=4, m=2)
        oT = conv[:, 8:16, :]
        junk = projT[:, 0, 0:256]
        scs = projT[:, 1, 0:64]
        sP = projT[0:32, 2, 0:256]
        sPT = projT[:, 3, 0:64].rearrange("p (m c) -> p m c", m=2)
        sqh = conv[:, 0:8, :]
        moe = projT[:, :, :].rearrange("p a b -> p (a b)")
        at = [0]

        def cut(n):
            at[0] += n
            return moe[:, at[0] - n:at[0]]

        xtok = cut(3 * D).rearrange("p (t n) -> p t n", t=3)
        selT = cut(3 * P).rearrange("p (t n) -> p t n", t=3)
        selG = cut(3 * P).rearrange("p (t n) -> p t n", t=3)
        xg = cut(KB * P).rearrange("p (k n) -> p k n", k=KB)
        gus = cut(4 * 512).rearrange("p (s n) -> p s n", s=4)
        gate, up, sig, act = (cut(KB * P).rearrange("p (k n) -> p k n", k=KB) for _ in range(4))
        ytok = cut(D)
        gtT = cut(T)[0:E, :]
        gT = cut(T)
        moeT = cut(KB * T).rearrange("p (k n) -> p k n", k=KB)
        rkp = cut(3 * (MAXP + 1) * E).rearrange("p (t n) -> p t n", t=3)
        gts = cut(3 * E).rearrange("p (t n) -> p t n", t=3)
        lg = cut(3 * E).rearrange("p (t n) -> p t n", t=3)
        msk = cut(3 * E).rearrange("p (t n) -> p t n", t=3)
        eqm = cut(3 * E).rearrange("p (t n) -> p t n", t=3)
        cum = cut(3 * E).rearrange("p (t n) -> p t n", t=3)
        zer = cut(E)
        top = cut(24).rearrange("p (t n) -> p t n", t=3)
        need = cut(8)
        yout = xtok
        assert at[0] <= 64 * T

        def pcol(i):
            return par[:, i // P, i % P:i % P + 1]

        MW, MB_, SW, NSSM, NMIX, NXA, NMEM, NMOE, NFIN = 0, 64, 80, 104, 112, 120, 128, 136, 144
        bgu = par[:, 2:6, :].rearrange("p a b -> p (a b)")
        bgu = bgu.rearrange("p (e j) -> p e j", j=16)

        bank_filled, act_emptied, dve_emptied = sem("bank_filled"), sem("act_emptied"), sem("dve_emptied")
        act_step, dve_step, pool_step = sem("act_step"), sem("dve_step"), sem("pool_step")
        slot_full = [sem(f"slot_full{i}") for i in range(SLOTS)]
        moe_full = [sem(f"moe_full{i}") for i in range(6)]
        params_in, x_in, mem_in, small_in, conv_in = (sem(n) for n in (
            "params_in", "x_in", "mem_in", "small_in", "conv_in"))
        state_in = [sem(f"state_in{u}") for u in range(2)]
        state_out = [sem(f"state_out{u}") for u in range(2)]
        names = ("consts_set", "x_squared", "mem_squared", "x_rms", "mem_rms", "x_normed", "mem_normed",
                 "dt_abs", "dt_exp", "dt_one", "dt_log", "a_exp", "dt_ready", "convolved", "conv_silu",
                 "gated_conv", "gb_sigmoid", "ubr_ready", "raw_used", "cv_ready", "acum_read",
                 "dw_exp", "xdte_ready", "seg_ready", "dcy_ready", "eac_ready", "m_ready", "ce_ready",
                 "dec_exp", "dec_ready", "state_new", "z_silu", "ga_sigmoid", "u_ready", "u_squared",
                 "grp_rms", "merged_ready", "h1_ready", "h_squared", "h_rms", "xn_ready",
                 "att_max", "att_exp", "probs_ready", "s_neg", "s_exp", "s_probs", "h2_ready",
                 "lg_ready", "lg_exp", "mask_ready", "rank_ready", "passes_ready",
                 "rows_out", "kv_out", "fin_out", "y_out", "copy_out",
                 "stage_done", "gu_copied", "turned", "turned_read", "bias_gate", "sig_ready", "h_act",
                 "sel_ready", "xy_full", "xy_copied", "selg_ready", "misc_full", "misc_read",
                 "moe_summed", "final_normed", "state_free", "scratch_free", "sin_ready")
        S = {n: sem(n) for n in names}

        def filled(eng, name, k=0):
            i = JOB[name] + k
            eng.wait_ge(bank_filled, i + 1)
            return bank[i % 8]

        def emptied(eng, name, k=0):
            i = JOB[name] + k
            eng.wait_ge(act_emptied if WHO[i] == A_ else dve_emptied, emptied_before(i + 1, WHO[i]))

        def free_bank(pe, name, k=0):
            i = JOB[name] + k
            if i >= 8:
                w = WHO[i - 8]
                pe.wait_ge(act_emptied if w == A_ else dve_emptied, emptied_before(i - 7, w))
            return bank[i % 8]

        block = ctx.enter_context(nc.Block())

        def wcols(w, c0):
            return w[0].rearrange("(k p) n -> p k n", p=P)[:, :, c0:c0 + CW]

        proj_cols = [1024, 1536, 2048, 2560, 0, 512, 6160, 6672, 4112, 4624, 5136, 5648,
                     3088, 3600, 7184, 7696]
        chunks = [(wcols(a["w_in"], c), ("proj", 4 * i + 3)) for i, c in enumerate(proj_cols)]
        for w, j in (("w_xk", "kp"), ("w_xv", "vp")):
            chunks += [(wcols(a[w], 0), (j, 1)), (wcols(a[w], 512), (j, 3))]
        chunks += [(wcols(a["w_out"], 0), ("wo", 3)), (wcols(a["w_out"], 512), ("wo", 7))]
        chunks += [(wcols(a["w_xq"], 0), ("q", 3)), (wcols(a["w_xq"], 512), ("q", 7))]
        for w, j, per in (("cache_mem_k", "qb", 4), ("cache_mem_v", "so", 1)):
            src = a[w][0].rearrange("b (m p) h d -> p b m (h d)", p=P)
            chunks += [(src[:, 2 * i:2 * i + 2], (j, per * i + per - 1)) for i in range(4)]
        chunks += [(wcols(a["w_xo"], 0), ("xo", 3)), (wcols(a["w_xo"], 512), ("xo", 7))]
        NCH = len(chunks)
        CH = {"w_xk": 16, "w_xv": 18, "w_out": 20, "w_xq": 22, "k": 24, "v": 28, "w_xo": 32}
        assert NCH == 34

        def slot(i):
            return ring[:, i % SLOTS]

        def chunk_in(eng, i):
            eng.wait_ge(slot_full[i % SLOTS], 16 * (i // SLOTS + 1))
            return slot(i)

        wgu = a["w_gate_up"][0].rearrange("e (k p) n -> e p k n", p=P)
        wdn = a["w_down"][0].rearrange("e (k p) n -> e p k n", p=P)

        mslot = [ring[:, i] for i in range(SLOTS)] + [
            flat[:, 0:4096].rearrange("p (k n) -> p k n", k=8),
            conv[:].rearrange("p a b -> p (a b)")[:, 0:4096].rearrange("p (k n) -> p k n", k=8)]

        def moe_chunk(pair, j):
            w, c = (wgu, j // 2 * CW) if j < 8 else (wdn, (j // 2 - 4) * CW)
            return w[bass.ds(pair * 2 + j % 2, 1), :, :, c:c + CW].rearrange("e p k n -> (e p) k n")

        @block.sync
        def _(sp):
            sp.dma_start(xtokin[:, 0:2, :], a["x_prompt"][0].rearrange("(t p) n -> p t n", p=P)).then_inc(x_in, 16)
            sp.dma_start(xtokin[0:TS, 2, :], a["x_sample"].rearrange("b s n -> (b s) n")).then_inc(x_in, 16)
            for i, (src, _) in enumerate(chunks):
                if i >= SLOTS:
                    name, k = chunks[i - SLOTS][1]
                    if name == "qb":
                        emptied(sp, name, k)
                    else:
                        filled(sp, name, k)
                if 24 <= i < 32:
                    dst = slot(i).rearrange("p (b m n) c -> p b m (n c)", b=2, m=2)
                else:
                    dst = slot(i)
                sp.dma_start(dst, src).then_inc(slot_full[i % SLOTS], 16)
            for j, name, k in ((2, "so", 2), (3, "so", 3), (4, "o", 3), (0, "xo", 3), (1, "xo", 7), (5, "h2ss", 0)):
                filled(sp, name, k)
                sp.dma_start(mslot[j], moe_chunk(0, j)).then_inc(moe_full[j], 16)
            sp.wait_ge(S["passes_ready"], 1)
            n = sp.value_load(npass[0:1, 0:1], min_val=0, max_val=MAXP - 1)
            with sp.Fori(0, n * PAIRS + (PAIRS - 1)) as it:
                for j in range(6, 18):
                    if j % 2 == 0:
                        sp.wait_ge(S["stage_done"], it * 6 + (j // 2 - 2))
                    pair = it % PAIRS if j < 12 else (it + 1) % PAIRS
                    sp.dma_start(mslot[j % 6], moe_chunk(pair, j % 12)).then_inc(moe_full[j % 6], 16)
            for j in range(6, 12):
                if j % 2 == 0:
                    sp.wait_ge(S["stage_done"], n * (6 * PAIRS) + (6 * (PAIRS - 1) + j // 2 - 2))
                src, c = (wgu, j // 2 * CW) if j < 8 else (wdn, (j // 2 - 4) * CW)
                sp.dma_start(mslot[j % 6], src[E - 2 + j % 2, :, :, c:c + CW]).then_inc(moe_full[j % 6], 16)
            emptied(sp, "yT", 3)
            sp.dma_start(outs[0][0].rearrange("(t p) n -> p t n", p=P), yout[:, 0:2, :]).then_inc(S["y_out"], 16)
            emptied(sp, "yT", 5)
            sp.dma_start(outs[1].rearrange("b s n -> (b s) n"), yout[0:TS, 2, :]).then_inc(S["y_out"], 16)
            sp.wait_ge(S["y_out"], 32)

        @block.gpsimd
        def _(pool):
            st = Steps(pool, pool_step)
            for m in (ident, ones, uinc, ustr):
                st(pool.memset(m[:], 0.0 if m is ident else 1.0))
            st(pool.affine_select(out=ident[:], in_=ident[:], compare_op=ALU.not_equal, fill=1.0, base=0,
                                  pattern=[[-1, P]], channel_multiplier=1))
            for m, op in ((uinc, ALU.is_ge), (ustr, ALU.is_gt)):
                st(pool.affine_select(out=m[:], in_=m[:], compare_op=op, fill=0.0, base=0,
                                      pattern=[[1, P]], channel_multiplier=-1))
            pool.iota(iota[:], pattern=[[1, CAP]], base=0, channel_multiplier=0,
                      allow_small_or_imprecise_dtypes=True).then_inc(S["consts_set"], 1)
            pool.dma_start(outs[8][0, :, 0:2, :], a["state_mamba_conv"][0, :, 1:3, :]).then_inc(S["copy_out"], 16)
            pool.dma_start(outs[9][0, :, 0:1, :], a["state_short_conv"][0, :, 1:2, :]).then_inc(S["copy_out"], 16)
            emptied(pool, "srow", 1)
            pool.dma_start(outs[3][0, 0], mrows[0:3, :]).then_inc(S["rows_out"], 16)
            pool.dma_start(outs[4][0, 0], srows[0:2, :]).then_inc(S["rows_out"], 16)
            pool.dma_start(outs[8][0, :, 2, :], mrows[3:11, :]).then_inc(S["rows_out"], 16)
            pool.dma_start(outs[9][0, :, 1, :], srows[2:10, :]).then_inc(S["rows_out"], 16)
            emptied(pool, "fin", 1)
            pool.dma_start(outs[2][0, 0].rearrange("(x y) p n -> (y p) x n", y=2), finst).then_inc(S["fin_out"], 16)
            sin = a["state_ssm"][0].rearrange("b (x y) p n -> b (y p) x n", y=2)
            sout = outs[7][0].rearrange("b (x y) p n -> b (y p) x n", y=2)
            pool.wait_ge(S["state_free"], 1)
            for b in range(TS + 2):
                if b >= 2:
                    pool.wait_ge(S["state_new"], b - 1)
                    pool.dma_start(sout[b - 2], sst[:, b % 2]).then_inc(state_out[b % 2], 16)
                    pool.wait_ge(state_out[b % 2], 16 * (b // 2))
                if b < TS:
                    if b >= 2:
                        emptied(pool, "bcs", 2 * b - 3)
                    pool.dma_start(sst[:, b % 2], sin[b]).then_inc(state_in[b % 2], 16)
            emptied(pool, "kp", 3)
            pool.dma_start(outs[5][0, 0].rearrange("(m p) h d -> p m (h d)", p=P), ktok).then_inc(S["kv_out"], 16)
            emptied(pool, "vp", 3)
            pool.dma_start(outs[6][0, 0].rearrange("(m p) h d -> p m (h d)", p=P), vtok).then_inc(S["kv_out"], 16)
            pool.wait_ge(S["kv_out"], 32)
            pool.wait_ge(S["fin_out"], 16)
            pool.wait_ge(S["rows_out"], 64)
            pool.wait_ge(S["copy_out"], 32)

        @block.scalar
        def _(s):
            st = Steps(s, act_step)

            def copy(out, in_, scale=1.0):
                return s.activation(out, in_, ACT.Copy, scale=scale)

            def done(ins):
                return ins.then_inc(act_emptied, 1)

            rows = [(0, 0, "w_mconv", 64), (0, 64, "b_mconv", 16), (0, 80, "w_sconv", 24), (0, 104, "norm_ssm", 8),
                    (0, 112, "norm_mix", 8), (0, 120, "norm_xattn", 8), (1, 0, "norm_mem", 8),
                    (1, 8, "norm_moe", 8), (1, 16, "norm_final", 8)]
            for t, r, name, n in rows:
                src = a[name]
                if len(src.shape) == 3:
                    src = src.rearrange("l k (b f) -> (l k b) f", f=P)
                elif len(src.shape) == 2:
                    src = src.rearrange("l (b f) -> (l b) f", f=P)
                else:
                    src = src.rearrange("(b f) -> b f", f=P)
                s.dma_start(stage[r:r + n, t, :], src).then_inc(params_in, 16)
            s.dma_start(stage[:, 2:6, :], a["b_gate_up"][0].rearrange("(a e) (b f) -> (e b) a f", a=4, f=P))\
                .then_inc(params_in, 16)
            s.dma_start(bdn[:], a["b_down"][0]).then_inc(params_in, 16)
            s.dma_start(mstate, a["state_mamba_conv"][0].rearrange("b k (c f) -> (b k) c f", f=256)).then_inc(conv_in, 16)
            s.dma_start(sstate, a["state_short_conv"][0].rearrange("b k (c f) -> (b k) c f", f=256)).then_inc(conv_in, 16)
            for t in range(2):
                s.dma_start(memv[t], a["mem_prompt"][0, t * P:(t + 1) * P, :].rearrange("p (a n) -> p a n", a=4))\
                    .then_inc(mem_in, 16)
            s.dma_start(wdt[:], a["w_in"][0].rearrange("(k p) n -> p k n", p=P)[:, :, 3072:3088]).then_inc(small_in, 16)
            s.dma_start(wrt[:], a["w_router"][0].rearrange("(k p) n -> p k n", p=P)).then_inc(small_in, 16)
            s.dma_start(dtb[:], a["dt_bias"][0].partition_broadcast(P)).then_inc(small_in, 16)
            s.dma_start(alog[:], a["a_log"][0].partition_broadcast(P)).then_inc(small_in, 16)
            s.dma_start(brt[:], a["b_router"][0].partition_broadcast(P)).then_inc(small_in, 16)
            for y in range(2):
                s.dma_start(dsk[64 * y:64 * y + 64, :],
                            a["d_skip"][0].rearrange("(x y) -> y x", y=2)[y].partition_broadcast(64),
                            allow_slow_non_contiguous=True).then_inc(small_in, 16)

            for k in range(2):
                b = filled(s, "par", k)
                if k == 0:
                    st(copy(par[:, 0, :], b[:, 0:P]))
                    st(copy(par[:, 1, 0:24], b[:, P:P + 24]))
                    done(copy(par[:, 2:4, :], b[:, 2 * P:4 * P].rearrange("p (a n) -> p a n", a=2)))
                else:
                    done(copy(par[:, 4:6, :], b[:, 0:2 * P].rearrange("p (a n) -> p a n", a=2)))
            b = filled(s, "mst")
            done(copy(msT[:], b[:, 0:384].rearrange("p (b c) -> p b c", b=XB)))
            b = filled(s, "sst")
            done(copy(ssT[:], b[:, 0:128].rearrange("p (b c) -> p b c", b=8)))
            for k in range(8):
                b = filled(s, "xT", k)
                done(copy(hT[:, k, :], b[:, 0:T]))
            for k in range(4):
                b = filled(s, "memT", k)
                done(copy(mnT[:, 2 * k:2 * k + 2, :], b[:, :].rearrange("p (a n) -> p a n", a=2)))
            emptied(s, "memT", 3)
            s.activation(sqx, hT[:], ACT.Square).then_inc(S["x_squared"], 1)
            s.activation(sqm, mnT[:], ACT.Square).then_inc(S["mem_squared"], 1)

            def root(name, out, n, div=D):
                b = filled(s, name)
                done(s.activation(out, b[:, 0:n], ACT.Sqrt, bias=eps[:, 0:1], scale=1.0 / div))

            s.wait_ge(S["consts_set"], 2)
            root("xss", rinv[:], T)
            root("mss", small[:, 0:NM], NM)
            s.wait_ge(S["dt_abs"], 1)
            s.activation(dts[:, 1], dts[:, 1], ACT.Exp, scale=-1.0).then_inc(S["dt_exp"], 1)
            s.wait_ge(small_in, 112)
            s.activation(alog[:], alog[:], ACT.Exp).then_inc(S["a_exp"], 1)
            s.wait_ge(S["dt_one"], 1)
            s.activation(dts[:, 3], dts[:, 2], ACT.Ln).then_inc(S["dt_log"], 1)

            def proj_blocks(n0, groups):
                base = JOB["proj"] + n0
                with s.Fori(0, groups) as g:
                    for j in range(8):
                        s.wait_ge(bank_filled, g * 8 + (base + j + 1))
                        copy(projT[:, bass.ds(g * 8 + (n0 + j), 1), :].rearrange("p a n -> p (a n)"),
                             bank[(base + j) % 8][:, 0:T]).then_inc(act_emptied, 1)

            s.wait_ge(S["x_normed"], 8)
            s.wait_ge(S["mem_normed"], 8)
            proj_blocks(0, 2)
            proj_blocks(16, 2)
            emptied(s, "proj", 31)
            s.wait_ge(S["convolved"], 1)
            s.activation(conv[:], conv[:], ACT.Silu).then_inc(S["conv_silu"], 1)
            s.activation(projT[:, Z:Z + 8, :], projT[:, Z:Z + 8, :], ACT.Silu).then_inc(S["z_silu"], 1)
            s.activation(projT[:, GA:GA + 8, :], projT[:, GA:GA + 8, :], ACT.Sigmoid).then_inc(S["ga_sigmoid"], 1)
            proj_blocks(32, 4)
            emptied(s, "proj", 63)
            s.activation(projT[:, GB:GB + 8, :], projT[:, GB:GB + 8, :], ACT.Sigmoid).then_inc(S["gb_sigmoid"], 1)
            for k in range(4):
                b = filled(s, "mrow", k)
                done(copy(mrows[:, 512 * k:512 * k + 512], b[0:11, :]))
            for k in range(2):
                b = filled(s, "srow", k)
                done(copy(srows[:, 512 * k:512 * k + 512], b[0:10, :]))
            s.wait_ge(S["acum_read"], 1)
            s.activation(small[:, 64:112], small[:, 64:112], ACT.Exp).then_inc(S["dw_exp"], 1)
            for c in range(2):
                b = filled(s, f"btok{c}")
                done(copy(btok[:, c, :], b[:, :]))
            for k in range(2):
                b = filled(s, "sin", k)
                done(copy(sinT[:, 512 * k:512 * k + 512], b[:, :]))
            for k in range(2):
                b = filled(s, "fin", k)
                done(copy(finst[:, 4 * k:4 * k + 4, :], b[:, :].rearrange("p (h n) -> p h n", h=4)))
            for c in range(2):
                for g in range(G):
                    n = G * c + g
                    b = filled(s, f"ssd{c}", 3 * g)
                    if n == 0:
                        s.wait_ge(S["ubr_ready"], 1)
                    done(copy(bcum[:, n % 2], b[:, :].rearrange("p (h l) -> p h l", h=4)))
                    if c == 1:
                        emptied(s, f"ssd{c}", 3 * g)
                        if g >= 1:
                            s.wait_ge(S["ce_ready"], g)
                        s.activation(eac, bcum[:, n % 2], ACT.Exp).then_inc(S["eac_ready"], 1)
                    s.wait_ge(S["seg_ready"], n + 1)
                    s.activation(dcy[:, n % 2], dcy[:, n % 2], ACT.Exp).then_inc(S["dcy_ready"], 1)
            emptied(s, "dec")
            s.activation(dec, dec, ACT.Exp).then_inc(S["dec_ready"], 1)
            s.wait_ge(S["scratch_free"], 1)
            for name, dst in (("kp", ktok), ("vp", vtok)):
                for nh in range(2):
                    for mt in range(2):
                        b = filled(s, name, 2 * nh + mt)
                        done(copy(dst[:, mt, nh * 512:nh * 512 + 512], b[:, :]))
            for k in range(4):
                b = filled(s, "kT", k)
                done(copy(kT[:, 2 * k:2 * k + 2, :], b[:, :].rearrange("p (a n) -> p a n", a=2)))
            s.wait_ge(S["u_ready"], 1)
            s.activation(sqg, yT, ACT.Square).then_inc(S["u_squared"], 1)
            for g in range(G):
                b = filled(s, "gn", g)
                done(s.activation(rgrp[:, g, :], b[:, 0:T], ACT.Sqrt, bias=eps[:, 0:1], scale=1.0 / 256))

            def square_h():
                s.activation(sqh, hT[:], ACT.Square).then_inc(S["h_squared"], 1)

            emptied(s, "wo", 7)
            square_h()
            root("h1ss", rinv[:], T)
            for k in range(8):
                b = filled(s, "q", k)
                done(copy(qT[:, k, :], b[:, 0:T], 1.0 / 16))
            for t in range(2):
                for hh in range(2):
                    n = 2 * t + hh
                    b = filled(s, "att", n)
                    s.wait_ge(S["att_max"], n + 1)
                    for h in range(2):
                        j = 8 * t + 2 * hh + h
                        ins = s.activation(pr[:, t, 2 * hh + h, :], b[:, h * 256:h * 256 + 256], ACT.Exp,
                                           bias=small[:, j:j + 1], accum_out=small[:, 16 + j:17 + j])
                        if h == 0:
                            st(ins)
                    done(ins)
            for h in range(4):
                b = filled(s, "pT", h)
                done(copy(pT[:, h], b[:, :].rearrange("p (m t) -> p m t", m=2)))
            for k in range(4):
                b = filled(s, "o", k)
                done(copy(oT[:, 2 * k:2 * k + 2, 0:TP], b[:, :].rearrange("p (a t) -> p a t", a=2)))
            emptied(s, "sT")
            s.activation(sP, sP, ACT.Exp, bias=small[0:32, 32:33], accum_out=small[0:32, 33:34]).then_inc(S["s_exp"], 1)
            b = filled(s, "sP")
            done(copy(sPT, b[:, 0:64].rearrange("p (m c) -> p m c", m=2)))
            for i in range(4):
                b = filled(s, "so", i)
                done(copy(oT[:, :, TP + 2 * i:TP + 2 * i + 2].rearrange("p k b -> p b k"),
                          b[:, 0:16].rearrange("p (b k) -> p b k", b=2)))
            emptied(s, "xo", 7)
            square_h()
            root("h2ss", rinv[:], T)
            s.wait_ge(S["lg_ready"], 1)
            s.activation(gts, gts, ACT.Exp).then_inc(S["lg_exp"], 1)
            for t, (_, n) in enumerate(TILES):
                for k in range(2):
                    b = filled(s, "xtok", 2 * t + k)
                    done(copy(xtok[0:n, t, 512 * k:512 * k + 512], b[0:n, :]))

            for k, name in enumerate(("gu_copied", "gu_copied")):
                s.activation(small[:, 300 + k:301 + k], eps[:], ACT.Copy).then_inc(S[name], 1)

            def gathered(n):
                for k in range(2):
                    s.wait_ge(S["xy_full"], n + (k + 1))
                    copy(xg[:, 4 * k:4 * k + 4, :], bank[4 + k][:, :].rearrange("p (a n) -> p a n", a=4))\
                        .then_inc(S["xy_copied"], 1)

            gathered(0)
            s.wait_ge(S["passes_ready"], 1)
            n = s.value_load(npass[0:1, 0:1], min_val=0, max_val=MAXP - 1)
            with s.Fori(0, n * PAIRS + PAIRS) as it:
                for k in range(4):
                    s.wait_ge(S["stage_done"], it * 6 + (k + 1))
                    copy(gus[:, k], bank[k % 2][:, :]).then_inc(S["gu_copied"], 1)
                    if k in (1, 2):
                        h = k - 1
                        s.wait_ge(S["bias_gate"], it * 2 + (h + 1))
                        s.activation(sig[:, 4 * h:4 * h + 4], gate[:, 4 * h:4 * h + 4], ACT.Sigmoid, scale=ALPHA)\
                            .then_inc(S["sig_ready"], 1)
                gathered(it * 2 + 2)
                for k in range(2):
                    s.wait_ge(S["stage_done"], it * 6 + (k + 5))
                    copy(ytok[:, 512 * k:512 * k + 512], bank[4 + k][:, :]).then_inc(S["xy_copied"], 1)
            s.wait_ge(S["moe_summed"], 1)
            square_h()
            root("fss", rinv[:], T)
            for t, (_, n) in enumerate(TILES):
                for k in range(2):
                    b = filled(s, "yT", 2 * t + k)
                    done(copy(yout[0:n, t, 512 * k:512 * k + 512], b[0:n, :]))

        @block.vector
        def _(v):
            st = Steps(v, dve_step)

            def done(ins):
                return ins.then_inc(dve_emptied, 1)

            def bc(x, n):
                return x.unsqueeze(2).to_broadcast([x.shape[0], x.shape[1], n])

            st(v.memset(small[:], 0.0))
            st(v.memset(dts[:], 0.0))
            v.memset(eps[:], EPS).then_inc(S["consts_set"], 1)

            def norm(name, dst, src, r, n, gain, out):
                emptied(v, name)
                st(v.reciprocal(r, r))
                for k in range(KB):
                    v.scalar_tensor_tensor(out=dst[:, k, 0:n], in0=src[:, k, 0:n], scalar=pcol(gain + k), in1=r,
                                           op0=ALU.mult, op1=ALU.mult).then_inc(S[out], 1)

            norm("xss", xnT, hT, rinv[:], T, NMIX, "x_normed")
            norm("mss", mnT, mnT, small[:, 0:NM], NM, NMEM, "mem_normed")
            v.wait_ge(S["mem_normed"], 8)

            v.wait_ge(small_in, 112)
            b = filled(v, "dt")
            st(v.tensor_tensor(out=dts[:, 0, 0:2], in0=b[:, 0:32].rearrange("p (t h) -> p t h", t=2),
                               in1=dtb[:].unsqueeze(1).to_broadcast([P, 2, H]), op=ALU.add))
            done(v.tensor_tensor(out=dts[0:TS, 0, 2], in0=b[0:TS, 32:48], in1=dtb[0:TS, :], op=ALU.add))
            emptied(v, "dt")
            v.scalar_tensor_tensor(out=dts[:, 1], in0=dts[:, 0], scalar=-1.0, in1=dts[:, 0], op0=ALU.mult, op1=ALU.max).then_inc(S["dt_abs"], 1)
            v.wait_ge(S["dt_exp"], 1)
            v.tensor_scalar(dts[:, 2], dts[:, 1], 1.0, None, ALU.add).then_inc(S["dt_one"], 1)
            v.wait_ge(S["dt_one"], 1)
            st(v.tensor_scalar(dts[:, 4], dts[:, 2], -1.0, None, ALU.add))
            st(v.tensor_scalar(dts[:, 5], dts[:, 4], 0.0, None, ALU.is_equal))
            st(v.tensor_tensor(out=dts[:, 4], in0=dts[:, 4], in1=dts[:, 5], op=ALU.add))
            st(v.reciprocal(dts[:, 4], dts[:, 4]))
            v.wait_ge(S["dt_log"], 1)
            st(v.tensor_tensor(out=dts[:, 3], in0=dts[:, 3], in1=dts[:, 5], op=ALU.add))
            st(v.tensor_tensor(out=dts[:, 3], in0=dts[:, 3], in1=dts[:, 4], op=ALU.mult))
            st(v.tensor_tensor(out=dts[:, 3], in0=dts[:, 3], in1=dts[:, 1], op=ALU.mult))
            st(v.scalar_tensor_tensor(out=dts[:, 0], in0=dts[:, 0], scalar=0.0, in1=dts[:, 3],
                                      op0=ALU.max, op1=ALU.add))
            v.wait_ge(S["a_exp"], 1)
            v.scalar_tensor_tensor(out=dta[:], in0=dts[:, 0], scalar=-1.0,
                                   in1=alog[:].unsqueeze(1).to_broadcast([P, 3, H]),
                                   op0=ALU.mult, op1=ALU.mult).then_inc(S["dt_ready"], 1)

            def blk_of(buf, i, c0, c1):
                return buf[:, bass.ds(i, 1), c0:c1].rearrange("p a n -> p (a n)")

            def weight(i):
                return par[:, 0, bass.ds(i, 1)]

            emptied(v, "par", 0)
            n0, before = st.n, emptied_before(JOB["proj"], A_)
            with v.Fori(0, XB) as blk:
                st.n, st.off = n0, blk * 4
                v.wait_ge(act_emptied, blk + (before + 1))
                st(v.tensor_scalar(blk_of(conv, blk, 0, T), blk_of(projT, blk, 0, T),
                                   weight(blk + 48), weight(blk + MB_), ALU.mult, ALU.add))
                for d in range(1, 4):
                    st(v.scalar_tensor_tensor(out=blk_of(conv, blk, d, TP), in0=blk_of(projT, blk, 0, TP - d),
                                              scalar=weight(blk + 16 * (3 - d)), in1=blk_of(conv, blk, d, TP),
                                              op0=ALU.mult, op1=ALU.add))
            st.n, st.off = n0 + 4 * XB, 0
            emptied(v, "mst")
            old = msT[:].rearrange("p b (s k) -> p b s k", k=3)
            for k in range(3):
                st(v.tensor_tensor(out=tmp, in0=old[:, :, :, k], in1=bc(par[:, 0, 16 * k:16 * k + 16], TS),
                                   op=ALU.mult))
                ins = v.tensor_tensor(out=conv[:, :, TP:T], in0=conv[:, :, TP:T], in1=tmp, op=ALU.add)
                if k < 2:
                    st(ins)
            ins.then_inc(S["convolved"], 1)

            emptied(v, "proj", 47)
            v.tensor_tensor(out=projT[:, SCC:SCC + 8, :], in0=projT[:, SCC:SCC + 8, :],
                            in1=projT[:, SCV:SCV + 8, :], op=ALU.mult).then_inc(S["cv_ready"], 1)
            v.wait_ge(S["cv_ready"], 1)
            n0 = st.n
            with v.Fori(0, KB) as blk:
                st.n, st.off = n0, blk * 3
                st(v.tensor_scalar(blk_of(projT, blk + SCV, 0, T), blk_of(projT, blk + SCC, 0, T),
                                   weight(blk + (SW + 16)), None, ALU.mult))
                for d in range(1, 3):
                    st(v.scalar_tensor_tensor(out=blk_of(projT, blk + SCV, d, TP), in0=blk_of(projT, blk + SCC, 0, TP - d),
                                              scalar=weight(blk + (SW + 8 * (2 - d))), in1=blk_of(projT, blk + SCV, d, TP),
                                              op0=ALU.mult, op1=ALU.add))
            st.n, st.off = n0 + 3 * KB, 0
            u = projT[:, SCV:SCV + 8, :]
            emptied(v, "sst")
            old = ssT[:].rearrange("p b (s k) -> p b s k", k=2)
            v.wait_ge(S["convolved"], 1)
            for k in range(2):
                st(v.tensor_tensor(out=tmp[:, 0:8], in0=old[:, :, :, k],
                                   in1=bc(par[:, 0, SW + 8 * k:SW + 8 * k + 8], TS), op=ALU.mult))
                st(v.tensor_tensor(out=u[:, :, TP:T], in0=u[:, :, TP:T], in1=tmp[:, 0:8], op=ALU.add))
            emptied(v, "proj", 63)
            st(v.tensor_tensor(out=ubr, in0=ubr, in1=u, op=ALU.mult))
            v.wait_ge(S["gb_sigmoid"], 1)
            v.tensor_tensor(out=ubr, in0=ubr, in1=projT[:, GB:GB + 8, :], op=ALU.mult).then_inc(S["ubr_ready"], 1)
            v.wait_ge(S["ubr_ready"], 1)

            b = filled(v, "acum")
            done(v.tensor_copy(small[:, 0:64], b[:, 0:64]))
            emptied(v, "acum")
            st(v.tensor_tensor(out=small[:, 64:80], in0=small[:, 32:48], in1=small[:, 0:16], op=ALU.subtract))
            st(v.tensor_tensor(out=small[:, 80:96], in0=small[:, 64:80], in1=small[:, 48:64], op=ALU.add))
            v.tensor_tensor(out=small[:, 96:112], in0=small[:, 48:64], in1=small[:, 16:32],
                            op=ALU.subtract).then_inc(S["acum_read"], 1)

            def heads(x, n):
                return x.rearrange("p (h n) -> p h n", h=n)

            v.wait_ge(S["rows_out"], 64)
            for c in range(2):
                for k in range(2):
                    b = filled(v, f"xs{c}", k)
                    done(v.tensor_tensor(out=heads(xdt[:, c, 512 * k:512 * k + 512], 8), in0=heads(b[:, :], 8),
                                         in1=bc(dts[:, 0, c, 8 * k:8 * k + 8], HD), op=ALU.mult))
                emptied(v, f"xs{c}", 1)
                v.wait_ge(S["dw_exp"], 1)
                for i in ((0, 1), (2,))[c]:
                    v.tensor_tensor(out=heads(xdte[:, i], H), in0=heads(xdt[:, c], H),
                                    in1=bc(small[:, 64 + 16 * i:80 + 16 * i], HD), op=ALU.mult)\
                        .then_inc(S["xdte_ready"], 1)
            for c in range(2):
                cols = slice(c * P, c * P + P)
                for g in range(G):
                    n = G * c + g
                    b = filled(v, f"ssd{c}", 3 * g + 1)
                    done(v.tensor_tensor(out=scm[:, n % 2], in0=b[:, 0:P], in1=uinc[:], op=ALU.mult))
                    emptied(v, f"ssd{c}", 3 * g)
                    st(v.tensor_tensor(out=dcy[:, n % 2], in0=bcum[:, n % 2],
                                       in1=bc(small[:, 16 * c + 4 * g:16 * c + 4 * g + 4], P), op=ALU.subtract))
                    v.tensor_scalar(dcy[:, n % 2], dcy[:, n % 2], 0.0, None, ALU.min).then_inc(S["seg_ready"], 1)
                    if c == 1:
                        v.wait_ge(S["eac_ready"], g + 1)
                        v.tensor_tensor(out=cexp, in0=eac, in1=conv[:, 12 + g, cols].unsqueeze(1).to_broadcast([P, 4, P]),
                                        op=ALU.mult).then_inc(S["ce_ready"], 1)
                    v.wait_ge(S["dcy_ready"], n + 1)
                    emptied(v, f"ssd{c}", 3 * g + 1)
                    v.tensor_tensor(out=dcy[:, n % 2], in0=dcy[:, n % 2],
                                    in1=scm[:, n % 2].unsqueeze(1).to_broadcast([P, 4, P]),
                                    op=ALU.mult).then_inc(S["m_ready"], 1)
                    b = filled(v, f"ssd{c}", 3 * g + 2)
                    for i in range(2):
                        ins = v.scalar_tensor_tensor(out=yT[:, 2 * g + i, cols], in0=conv[:, 2 * g + i, cols],
                                                     scalar=dsk[:, 2 * g + i:2 * g + i + 1],
                                                     in1=b[:, i * P:i * P + P], op0=ALU.mult, op1=ALU.add)
                    done(ins)
            emptied(v, "ssd1", 11)
            st(v.memset(tmp[:, 0:8], 0.0))
            v.memset(tmp[:, 8:16], 0.0).then_inc(S["state_free"], 1)

            xs_s = conv[:, 0:8, TP:T]
            b = filled(v, "dec")
            st(v.tensor_tensor(out=dtx, in0=xs_s, in1=b[:, 0:64].rearrange("p (h s) -> p h s", h=8), op=ALU.mult))
            done(v.tensor_copy(dec, b[:, 64:128].rearrange("p (h s) -> p h s", h=8)))
            v.wait_ge(S["dec_ready"], 1)

            def by_group(x):
                return x.rearrange("p (g y) n -> p g y n", y=2)

            def rows_of(b):
                return b[:, :].rearrange("p (g n) -> p g n", g=G).unsqueeze(2).to_broadcast([P, G, 2, P])

            for i in range(TS):
                s_ = sst[:, i % 2]
                v.wait_ge(state_in[i % 2], 16 * (i // 2 + 1))
                st(v.tensor_tensor(out=s_, in0=s_, in1=bc(dec[:, :, i], P), op=ALU.mult))
                b = filled(v, "bcs", 2 * i)
                done(v.tensor_tensor(out=by_group(prod), in0=rows_of(b), in1=by_group(bc(dtx[:, :, i], P)), op=ALU.mult))
                emptied(v, "bcs", 2 * i)
                v.tensor_tensor(out=s_, in0=s_, in1=prod, op=ALU.add).then_inc(S["state_new"], 1)
                v.wait_ge(S["state_new"], i + 1)
                b = filled(v, "bcs", 2 * i + 1)
                done(v.tensor_tensor(out=by_group(prod), in0=rows_of(b), in1=by_group(s_), op=ALU.mult))
                emptied(v, "bcs", 2 * i + 1)
                st(v.tensor_reduce(yT[:, :, TP + i], prod, AX.X, ALU.add))
            st(v.tensor_tensor(out=dtx, in0=xs_s, in1=bc(dsk[:, :], TS), op=ALU.mult))
            v.tensor_tensor(out=yT[:, :, TP:T], in0=yT[:, :, TP:T], in1=dtx, op=ALU.add).then_inc(S["scratch_free"], 1)
            v.wait_ge(S["scratch_free"], 1)
            v.wait_ge(S["z_silu"], 1)
            v.tensor_tensor(out=yT, in0=yT, in1=projT[:, Z:Z + 8, :], op=ALU.mult).then_inc(S["u_ready"], 1)
            v.wait_ge(S["u_ready"], 1)
            emptied(v, "gn", 3)
            st(v.reciprocal(rgrp, rgrp))
            for k in range(KB):
                st(v.scalar_tensor_tensor(out=yT[:, k, :], in0=yT[:, k, :], scalar=pcol(NSSM + k),
                                          in1=rgrp[:, k // 2, :], op0=ALU.mult, op1=ALU.mult))
            v.wait_ge(S["ga_sigmoid"], 1)
            st(v.tensor_tensor(out=merged, in0=yT, in1=projT[:, GA:GA + 8, :], op=ALU.mult))
            v.tensor_tensor(out=merged, in0=merged, in1=ubr, op=ALU.add).then_inc(S["merged_ready"], 1)

            def add_to_h(name):
                for k in range(KB):
                    b = filled(v, name, k)
                    done(v.tensor_tensor(out=hT[:, k, :], in0=b[:, 0:T], in1=hT[:, k, :], op=ALU.add))
                emptied(v, name, 7)

            add_to_h("wo")
            norm("h1ss", xnT, hT, rinv[:], T, NXA, "xn_ready")
            for n in range(4):
                t, hh = n // 2, n % 2
                j = 8 * t + 2 * hh
                b = filled(v, "att", n)
                v.tensor_reduce(small[:, j:j + 2], b[:, :].rearrange("p (h m) -> p h m", h=2), AX.X, ALU.max,
                                negate=True).then_inc(S["att_max"], 1)
            for t in range(2):
                emptied(v, "att", 2 * t + 1)
                r = small[:, 16 + 8 * t:20 + 8 * t]
                st(v.reciprocal(r, r))
                v.tensor_tensor(out=pr[:, t], in0=pr[:, t], in1=bc(r, 256), op=ALU.mult).then_inc(S["probs_ready"], 1)
            for u in range(2):
                v.wait_ge(state_out[u], 16 * (TS // 2))
            for i in range(TS):
                keys = chunk_in(v, CH["k"] + i // 2).rearrange("p (b m n) c -> p b m (n c)", b=2, m=2)
                for hh in range(2):
                    b = filled(v, "qb", 2 * i + hh)
                    for h in range(2):
                        for m in range(2):
                            c = m * 32 + i * 4 + 2 * hh + h
                            ins = v.tensor_tensor_reduce(junk, keys[:, i % 2, m, (2 * hh + h) * 256:(2 * hh + h + 1) * 256],
                                                         b[:, h * 256:h * 256 + 256], 1.0, 0.0, ALU.mult, ALU.add,
                                                         scs[:, c:c + 1])
                            if h + m < 2:
                                st(ins)
                    done(ins)
                    emptied(v, "qb", 2 * i + hh)
            b = filled(v, "sT")
            st(v.tensor_reduce(small[0:32, 32:33], b[0:32, 0:256], AX.X, ALU.max, negate=True))
            done(v.tensor_copy(sP, b[0:32, 0:256]))
            v.wait_ge(S["s_exp"], 1)
            st(v.reciprocal(small[0:32, 33:34], small[0:32, 33:34]))
            v.tensor_scalar(sP, sP, small[0:32, 33:34], None, ALU.mult).then_inc(S["s_probs"], 1)
            add_to_h("xo")
            norm("h2ss", xnT, hT, rinv[:], T, NMOE, "xn_ready")

            v.wait_ge(S["kv_out"], 32)
            v.wait_ge(S["fin_out"], 16)
            st(v.memset(gts, 0.0))
            st(v.memset(eqm, 0.0))
            st(v.memset(msk, 0.0))
            st(v.memset(zer, 0.0))
            b = filled(v, "rt")
            for t, (_, n) in enumerate(TILES):
                ins = v.tensor_tensor(out=lg[0:n, t], in0=b[0:n, t * E:t * E + E], in1=brt[0:n, :], op=ALU.add)
            done(ins)
            emptied(v, "rt")
            for t, (_, n) in enumerate(TILES):
                l, tp = lg[0:n, t], top[0:n, t]
                st(v.max(tp, l))
                st(v.tensor_scalar(gts[0:n, t], l, tp[:, 0:1], None, ALU.subtract))
            v.memset(top[:, 2, 4:8], 0.0).then_inc(S["lg_ready"], 1)
            v.wait_ge(S["lg_ready"], 1)
            for t, (_, n) in enumerate(TILES):
                l, tp, nd = lg[0:n, t], top[0:n, t], need[0:n, t:t + 1]
                st(v.tensor_scalar(msk[0:n, t], l, tp[:, 3:4], None, ALU.is_gt))
                st(v.tensor_scalar(eqm[0:n, t], l, tp[:, 3:4], None, ALU.is_equal))
                st(v.tensor_reduce(nd, msk[0:n, t], AX.X, ALU.add))
                st(v.tensor_scalar(nd, nd, -1.0, 4.0, ALU.mult, ALU.add))
                st(v.tensor_tensor_scan(cum[0:n, t], eqm[0:n, t], zer[0:n, :], 0.0, ALU.add, ALU.add))
                st(v.tensor_scalar(cum[0:n, t], cum[0:n, t], nd, None, ALU.is_le))
                st(v.tensor_tensor(out=eqm[0:n, t], in0=eqm[0:n, t], in1=cum[0:n, t], op=ALU.mult))
                ins = v.tensor_tensor(out=msk[0:n, t], in0=msk[0:n, t], in1=eqm[0:n, t], op=ALU.add)
                if t < 2:
                    st(ins)
            ins.then_inc(S["mask_ready"], 1)
            v.wait_ge(S["mask_ready"], 1)
            v.wait_ge(S["lg_exp"], 1)
            st(v.tensor_tensor(out=gts, in0=gts, in1=msk, op=ALU.mult))
            for t, (_, n) in enumerate(TILES):
                nd = need[0:n, 4 + t:5 + t]
                st(v.tensor_reduce(nd, gts[0:n, t], AX.X, ALU.add))
                st(v.reciprocal(nd, nd))
                st(v.tensor_scalar(gts[0:n, t], gts[0:n, t], nd, None, ALU.mult))
            b = filled(v, "rank")
            for t, (_, n) in enumerate(TILES):
                st(v.scalar_tensor_tensor(out=eqm[0:n, t], in0=b[0:n, t * E:t * E + E], scalar=1.0, in1=msk[0:n, t],
                                          op0=ALU.add, op1=ALU.mult))
            done(v.tensor_reduce(small[0:1, 0:1], b[0:1, 3 * E:4 * E], AX.X, ALU.max))
            for p in range(MAXP + 1):
                st(v.tensor_scalar(rkp[:, :, p * E:p * E + E], eqm, -1.0 - CAP * p, None, ALU.add))
            emptied(v, "rank")
            st(v.tensor_scalar(small[0:1, 1:2], small[0:1, 0:1], float(CAP), None, ALU.is_gt))
            for p in range(2, MAXP):
                st(v.scalar_tensor_tensor(out=small[0:1, 1:2], in0=small[0:1, 0:1], scalar=float(CAP * p),
                                          in1=small[0:1, 1:2], op0=ALU.is_gt, op1=ALU.add))
            v.tensor_copy(npass[0:1, 0:1], small[0:1, 1:2]).then_inc(S["passes_ready"], 1)

            def select(it, gated):
                dst = selG if gated else selT
                for t, (_, n) in enumerate(TILES):
                    for j in range(2):
                        g = gts[0:n, t, bass.ds((it % PAIRS) * 2 + j, 1)] if gated else None
                        ins = v.tensor_scalar(dst[0:n, t, j * CAP:j * CAP + CAP], iota[0:n, :],
                                              rkp[0:n, t, bass.ds(it * 2 + j, 1)], g,
                                              ALU.is_equal, ALU.mult if gated else ALU.bypass)
                ins.then_inc(S["selg_ready" if gated else "sel_ready"], 1)

            b = filled(v, "gtT")
            done(v.tensor_copy(gtT, b[0:E, 0:T]))
            for k in range(KB):
                b = filled(v, "bd", k)
                done(v.tensor_copy(moeT[:, k, :], b[:, 0:T]))
            for k, name in enumerate(("turned_read", "turned_read", "misc_read", "misc_read")):
                v.memset(small[:, 304 + k:305 + k], 0.0).then_inc(S[name], 1)
            v.wait_ge(S["consts_set"], 2)
            select(0, False)
            v.wait_ge(S["turned_read"], 2)
            v.wait_ge(S["misc_read"], 2)
            emptied(v, "bd", 7)
            v.wait_ge(S["passes_ready"], 1)
            n = v.value_load(npass[0:1, 0:1], min_val=0, max_val=MAXP - 1)
            n0 = st.n

            def biased(dst, h, pair, off, k):
                v.wait_ge(S["turned"], it * 4 + (k + 1))
                v.tensor_tensor(out=dst[:, 4 * h:4 * h + 4, :].rearrange("p b (e c) -> p b e c", e=2),
                                in0=bank[2 + k % 2][:, :].rearrange("p (b e c) -> p b e c", b=4, e=2),
                                in1=bgu[:, bass.ds(pair * 2, 2), off + 4 * h:off + 4 * h + 4]
                                .rearrange("p e b -> p b e").unsqueeze(3).to_broadcast([P, 4, 2, CAP]),
                                op=ALU.add).then_inc(S["turned_read"], 1)
                v.wait_ge(S["turned_read"], it * 4 + (k + 3))
                return dst[:, 4 * h:4 * h + 4]

            with v.Fori(0, n * PAIRS + PAIRS) as it:
                st.n, st.off = n0, it * 4
                pair = it % PAIRS
                for h in range(2):
                    x = biased(gate, h, pair, 0, h)
                    v.tensor_scalar(x, x, LIMIT, None, ALU.min).then_inc(S["bias_gate"], 1)
                v.wait_ge(S["xy_full"], it * 2 + 2)
                select(it + 1, False)
                select(it, True)
                for h in range(2):
                    x = biased(up, h, pair, 8, 2 + h)
                    st(v.tensor_scalar(x, x, LIMIT, -LIMIT, ALU.min, ALU.max))
                    v.wait_ge(S["bias_gate"], it * 2 + (h + 1))
                    st(v.scalar_tensor_tensor(out=x, in0=x, scalar=1.0, in1=gate[:, 4 * h:4 * h + 4],
                                              op0=ALU.add, op1=ALU.mult))
                    v.wait_ge(S["sig_ready"], it * 2 + (h + 1))
                    v.tensor_tensor(out=act[:, 4 * h:4 * h + 4], in0=x, in1=sig[:, 4 * h:4 * h + 4],
                                    op=ALU.mult).then_inc(S["h_act"], 1)
                for k in range(10):
                    b = bank[6 + k % 2]
                    v.wait_ge(S["misc_full"], it * 10 + (k + 1))
                    if k == 0:
                        ins = v.tensor_copy(gT[:, 0:P], b[:, 0:P])
                    elif k == 1:
                        ins = v.tensor_copy(gT[:, P:T], b[:, 0:T - P])
                    else:
                        ins = v.tensor_tensor(out=moeT[:, k - 2, :], in0=b[:, 0:T], in1=moeT[:, k - 2, :], op=ALU.add)
                    ins.then_inc(S["misc_read"], 1)
            v.wait_ge(S["misc_read"], n * (10 * PAIRS) + (10 * PAIRS + 2))
            v.tensor_tensor(out=hT[:], in0=hT[:], in1=moeT, op=ALU.add).then_inc(S["moe_summed"], 1)
            v.wait_ge(S["moe_summed"], 1)
            norm("fss", xnT, hT, rinv[:], T, NFIN, "final_normed")

        @block.tensor
        def _(pe):
            last = [None]

            def mm(out, lhsT, rhs, start=True, stop=True):
                last[0] = pe.matmul(out, lhsT, rhs, start=start, stop=stop)
                return last[0]

            def close():
                last[0].then_inc(bank_filled, 1)

            def turn(out, in_):
                k = in_.shape[0]
                last[0] = pe.transpose(out, in_, ident[0:k, 0:k])

            pe.wait_ge(S["consts_set"], 2)
            pe.wait_ge(params_in, 16 * 11)
            for k in range(2):
                b = free_bank(pe, "par", k)
                for i in range(4 - 2 * k):
                    if k == 0 and i == 1:
                        turn(b[:, i * P:i * P + 24], stage[0:24, i, :])
                    else:
                        turn(b[:, i * P:i * P + P], stage[:, 4 * k + i, :])
                close()
            pe.wait_ge(conv_in, 32)
            b = free_bank(pe, "mst")
            for i in range(XB):
                turn(b[:, i * 24:i * 24 + 24], mstate[:, i // 2, (i % 2) * P:(i % 2) * P + P])
            close()
            b = free_bank(pe, "sst")
            for i in range(KB):
                turn(b[:, i * 16:i * 16 + 16], sstate[:, i // 2, (i % 2) * P:(i % 2) * P + P])
            close()
            pe.wait_ge(x_in, 32)
            for k in range(KB):
                b = free_bank(pe, "xT", k)
                for t, (c, n) in enumerate(TILES):
                    turn(b[:, c:c + n], xtokin[0:n, t, k * P:k * P + P])
                close()
            pe.wait_ge(mem_in, 32)
            for k in range(4):
                b = free_bank(pe, "memT", k)
                for i in range(2):
                    for t in range(2):
                        turn(b[:, i * 256 + t * P:i * 256 + t * P + P], memv[t][:, k, i * P:i * P + P])
                close()

            def sum_squares(name, sq, n):
                b = free_bank(pe, name)
                for k in range(KB):
                    mm(b[:, 0:n], ones[:], sq[:, k, 0:n], k == 0, k == KB - 1)
                close()

            pe.wait_ge(S["x_squared"], 1)
            sum_squares("xss", sqx, T)
            pe.wait_ge(S["mem_squared"], 1)
            sum_squares("mss", sqm, NM)
            pe.wait_ge(S["x_normed"], 8)
            pe.wait_ge(small_in, 112)
            b = free_bank(pe, "dt")
            for t, (c, n) in enumerate(TILES):
                for k in range(KB):
                    mm(b[0:n, t * H:t * H + H], xnT[:, k, c:c + n], wdt[:, k, :], k == 0, k == KB - 1)
            close()
            base = JOB["proj"]
            before = emptied_before(base, A_)
            with pe.Fori(0, 4) as it:
                for j in range(16):
                    if j % 4 == 0:
                        pe.wait_ge(slot_full[j // 4], it * 16 + 16)
                    if base + j - 8 == JOB["dt"]:
                        emptied(pe, "dt")
                    pe.wait_ge(act_emptied, it * 16 + (emptied_before(base + j - 7, A_) if j < 8 else before + j - 7))
                    for k in range(KB):
                        mm(bank[(base + j) % 8][:, 0:T], ring[:, j // 4, k, (j % 4) * P:(j % 4) * P + P], xnT[:, k, :],
                           k == 0, k == KB - 1)
                    close()

            def project(name, chunk, rhs):
                n = rhs.shape[2]
                for j in range(KB):
                    if j % 4 == 0:
                        w = chunk_in(pe, chunk + j // 4)
                    b = free_bank(pe, name, j)
                    for k in range(KB):
                        mm(b[:, 0:n], w[:, k, (j % 4) * P:(j % 4) * P + P], rhs[:, k, :], k == 0, k == KB - 1)
                    close()

            emptied(pe, "proj", 63)
            for k in range(4):
                b = free_bank(pe, "mrow", k)
                for i in range(4):
                    turn(b[0:11, i * P:i * P + P], projT[:, 4 * k + i, T - 11:T])
                close()
            pe.wait_ge(S["cv_ready"], 1)
            for k in range(2):
                b = free_bank(pe, "srow", k)
                for i in range(4):
                    turn(b[0:10, i * P:i * P + P], projT[:, SCC + 4 * k + i, T - 10:T])
                close()
            pe.wait_ge(S["dt_ready"], 1)
            b = free_bank(pe, "acum")
            for c in range(2):
                mm(b[:, c * H:c * H + H], uinc[:], dta[:, c, :])
                mm(b[:, 32 + c * H:32 + c * H + H], ones[:], dta[:, c, :])
            close()
            pe.wait_ge(S["conv_silu"], 1)
            for c in range(2):
                cols = slice(c * P, c * P + P)
                for k in range(2):
                    b = free_bank(pe, f"xs{c}", k)
                    for i in range(4):
                        turn(b[:, i * P:i * P + P], conv[:, 4 * k + i, cols])
                    close()
                b = free_bank(pe, f"btok{c}")
                for i in range(4):
                    turn(b[:, i * P:i * P + P], conv[:, 8 + i, cols])
                close()
            emptied(pe, "btok1")
            pe.wait_ge(S["xdte_ready"], 3)
            for k in range(2):
                b = free_bank(pe, "sin", k)
                for i in range(2):
                    g = 2 * k + i
                    mm(b[:, i * 256:i * 256 + 256], btok[:, 0, g * P:g * P + P], xdte[:, 0, g * 256:g * 256 + 256])
                close()
            for k in range(2):
                b = free_bank(pe, "fin", k)
                for i in range(4):
                    h = 4 * k + i
                    for c in range(2):
                        mm(b[:, i * P:i * P + P], xdte[:, 1 + c, h * P:h * P + P],
                           btok[:, c, (h // 2) * P:(h // 2) * P + P], c == 0, c == 1)
                close()
            emptied(pe, "sin", 1)
            for c in range(2):
                cols = slice(c * P, c * P + P)
                for g in range(G):
                    b = free_bank(pe, f"ssd{c}", 3 * g)
                    for i in range(4):
                        mm(b[:, i * P:i * P + P], dta[:, c, 4 * g + i:4 * g + i + 1].to_broadcast([P, P]), uinc[:])
                    close()
                    b = free_bank(pe, f"ssd{c}", 3 * g + 1)
                    mm(b[:, 0:P], conv[:, 8 + g, cols], conv[:, 12 + g, cols])
                    close()
                    b = free_bank(pe, f"ssd{c}", 3 * g + 2)
                    n = G * c + g
                    pe.wait_ge(S["m_ready"], n + 1)
                    if c == 1:
                        pe.wait_ge(S["ce_ready"], g + 1)
                    for i in range(4):
                        h = 4 * g + i
                        out = b[64 * (i % 2):64 * (i % 2) + 64, (i // 2) * P:(i // 2) * P + P]
                        mm(out, xdt[:, c, h * HD:h * HD + HD], dcy[:, n % 2, i, :], True, c == 0)
                        if c == 1:
                            mm(out, sinT[:, h * HD:h * HD + HD], cexp[:, i, :], False, True)
                    close()
            b = free_bank(pe, "dec")
            for i in range(KB):
                for j, src in enumerate((dts[0:TS, 0, 2], dta[0:TS, 2])):
                    for y in range(2):
                        mm(b[HD * y:HD * y + HD, 64 * j + 8 * i:64 * j + 8 * i + 8],
                           src[:, 2 * i + y:2 * i + y + 1].to_broadcast([TS, HD]), ident[0:TS, 0:TS])
            close()
            for i in range(TS):
                for j in range(2):
                    b = free_bank(pe, "bcs", 2 * i + j)
                    for g in range(G):
                        mm(b[:, g * P:g * P + P], conv[:, 8 + 4 * j + g, TP + i:TP + i + 1].to_broadcast([P, P]), ident[:])
                    close()
            for name, chunk in (("kp", CH["w_xk"]), ("vp", CH["w_xv"])):
                for nh in range(2):
                    w = chunk_in(pe, chunk + nh)
                    for mt in range(2):
                        b = free_bank(pe, name, 2 * nh + mt)
                        for k in range(KB):
                            mm(b[:, :], mnT[:, k, mt * P:mt * P + P], w[:, k, :], k == 0, k == KB - 1)
                        close()
            emptied(pe, "kp", 3)
            for k in range(4):
                b = free_bank(pe, "kT", k)
                for i in range(2):
                    for mt in range(2):
                        turn(b[:, i * 256 + mt * P:i * 256 + mt * P + P],
                             ktok[:, mt, (2 * k + i) * P:(2 * k + i + 1) * P])
                close()
            pe.wait_ge(S["u_squared"], 1)
            for g in range(G):
                b = free_bank(pe, "gn", g)
                for k in range(2):
                    mm(b[:, 0:T], ones[:], sqg[:, 2 * g + k, :], k == 0, k == 1)
                close()
            pe.wait_ge(S["merged_ready"], 1)
            project("wo", CH["w_out"], merged)
            pe.wait_ge(S["h_squared"], 1)
            sum_squares("h1ss", sqh, T)
            pe.wait_ge(S["xn_ready"], 8)
            project("q", CH["w_xq"], xnT)
            emptied(pe, "q", 7)
            emptied(pe, "kT", 3)
            for t in range(2):
                for hh in range(2):
                    b = free_bank(pe, "att", 2 * t + hh)
                    for i in range(2):
                        h = 2 * hh + i
                        for k in range(2):
                            mm(b[:, i * 256:i * 256 + 256], qT[:, 2 * h + k, t * P:t * P + P], kT[:, 2 * h + k, :],
                               k == 0, k == 1)
                    close()
            pe.wait_ge(S["probs_ready"], 2)
            for h in range(4):
                b = free_bank(pe, "pT", h)
                for mt in range(2):
                    for t in range(2):
                        turn(b[:, mt * 256 + t * P:mt * 256 + t * P + P], pr[:, t, h, mt * P:mt * P + P])
                close()
            emptied(pe, "vp", 3)
            emptied(pe, "pT", 3)
            for k in range(4):
                b = free_bank(pe, "o", k)
                for i in range(2):
                    for mt in range(2):
                        mm(b[:, i * 256:i * 256 + 256], vtok[:, mt, (2 * k + i) * P:(2 * k + i + 1) * P],
                           pT[:, k, mt, :], mt == 0, mt == 1)
                close()
            for i in range(TS):
                for hh in range(2):
                    b = free_bank(pe, "qb", 2 * i + hh)
                    for k in range(4):
                        mm(b[:, k * P:k * P + P], qT[:, 4 * hh + k, TP + i:TP + i + 1].to_broadcast([P, P]), ident[:])
                    close()
            emptied(pe, "qb", 15)
            b = free_bank(pe, "sT")
            for m in range(2):
                turn(b[0:32, m * P:m * P + P], scs[:, m * 32:m * 32 + 32])
            close()
            pe.wait_ge(S["s_probs"], 1)
            b = free_bank(pe, "sP")
            for m in range(2):
                turn(b[:, m * 32:m * 32 + 32], sP[:, m * P:m * P + P])
            close()
            emptied(pe, "sP")
            for i in range(4):
                vals = chunk_in(pe, CH["v"] + i).rearrange("p (b m n) c -> p b m (n c)", b=2, m=2)
                b = free_bank(pe, "so", i)
                for s_ in range(2):
                    for k in range(KB):
                        for m in range(2):
                            c = (2 * i + s_) * 4 + k // 2
                            mm(b[:, s_ * 8 + k:s_ * 8 + k + 1], vals[:, s_, m, k * P:k * P + P], sPT[:, m, c:c + 1],
                               m == 0, m == 1)
                close()
            emptied(pe, "so", 3)
            project("xo", CH["w_xo"], oT)
            pe.wait_ge(S["h_squared"], 2)
            sum_squares("h2ss", sqh, T)
            pe.wait_ge(S["xn_ready"], 16)
            b = free_bank(pe, "rt")
            for t, (c, n) in enumerate(TILES):
                for k in range(KB):
                    mm(b[0:n, t * E:t * E + E], xnT[:, k, c:c + n], wrt[:, k, :], k == 0, k == KB - 1)
            close()
            pe.wait_ge(S["mask_ready"], 1)
            b = free_bank(pe, "rank")
            for t, (_, n) in enumerate(TILES):
                for u in range(t):
                    mm(b[0:n, t * E:t * E + E], ones[:, 0:n], msk[:, u], u == 0, False)
                mm(b[0:n, t * E:t * E + E], ustr[0:n, 0:n], msk[0:n, t], t == 0, True)
            for t, (_, n) in enumerate(TILES):
                mm(b[:, 3 * E:4 * E], ones[0:n, :], msk[0:n, t], t == 0, t == 2)
            close()
            for t, (c, n) in enumerate(TILES):
                for k in range(2):
                    b = free_bank(pe, "xtok", 2 * t + k)
                    for i in range(4):
                        turn(b[0:n, i * P:i * P + P], xnT[:, 4 * k + i, c:c + n])
                    close()
            emptied(pe, "xtok", 5)
            emptied(pe, "rank")

            b = free_bank(pe, "gtT")
            for t, (c, n) in enumerate(TILES):
                turn(b[0:E, c:c + n], gts[0:n, t, :])
            close()
            emptied(pe, "gtT")
            for k in range(KB):
                b = free_bank(pe, "bd", k)
                mm(b[:, 0:T], bdn[:, k * P:k * P + P], gtT)
                close()
            emptied(pe, "bd", 7)

            def gather(n, m=None):
                pe.wait_ge(S["sel_ready"], n)
                for h in range(2):
                    if m is not None:
                        pe.wait_ge(S["xy_copied"], m + (h + 1))
                    for k in range(4 * h, 4 * h + 4):
                        for t, (_, r) in enumerate(TILES):
                            mm(bank[4 + h][:, (k % 4) * P:(k % 4) * P + P], xtok[0:r, t, k * P:k * P + P],
                               selT[0:r, t, :], t == 0, t == 2)
                    last[0].then_inc(S["xy_full"], 1)

            gather(1)
            pe.wait_ge(S["passes_ready"], 1)
            n = pe.value_load(npass[0:1, 0:1], min_val=0, max_val=MAXP - 1)
            with pe.Fori(0, n * PAIRS + PAIRS) as it:

                def stream(stage, b, stationary, halves=False):
                    for e in range(2):
                        j = 2 * stage + e
                        pe.wait_ge(moe_full[j % 6], it * 32 + 16 * (j // 6 + 1))
                    for k in range(KB):
                        if halves and k % 4 == 0:
                            pe.wait_ge(S["h_act"], it * 2 + (k // 4 + 1))
                        for e in range(2):
                            mm(b[64 * e:64 * e + 64, :], stationary[:, k, 64 * e:64 * e + 64],
                               mslot[(2 * stage + e) % 6][:, k, :], k == 0, k == KB - 1)
                    last[0].then_inc(S["stage_done"], 1)

                def turn_half(k):
                    pe.wait_ge(S["gu_copied"], it * 4 + (k + 3))
                    pe.wait_ge(S["turned_read"], it * 4 + (k + 1))
                    for i in range(4):
                        turn(bank[2 + k % 2][:, i * P:i * P + P], gus[:, k, i * P:i * P + P])
                    last[0].then_inc(S["turned"], 1)

                def misc(k):
                    pe.wait_ge(S["misc_read"], it * 10 + (k + 1))
                    return bank[6 + k % 2]

                pe.wait_ge(S["xy_copied"], it * 4 + 2)
                for k in range(4):
                    pe.wait_ge(S["gu_copied"], it * 4 + (k + 1))
                    stream(k, bank[k % 2], xg)
                    if k:
                        turn_half(k - 1)
                gather(it + 2, it * 4)
                turn_half(3)
                pe.wait_ge(S["selg_ready"], it + 1)
                b = misc(0)
                turn(b[:, 0:P], selG[:, 0, :])
                last[0].then_inc(S["misc_full"], 1)
                b = misc(1)
                turn(b[:, 0:P], selG[:, 1, :])
                turn(b[:, P:P + TS], selG[0:TS, 2, :])
                last[0].then_inc(S["misc_full"], 1)
                for k in range(2):
                    pe.wait_ge(S["xy_copied"], it * 4 + (k + 3))
                    stream(4 + k, bank[4 + k], act, halves=True)
                pe.wait_ge(S["misc_read"], it * 10 + 4)
                for k in range(KB):
                    if k % 4 == 0:
                        pe.wait_ge(S["xy_copied"], it * 4 + (5 + k // 4))
                    b = misc(2 + k)
                    mm(b[:, 0:T], ytok[:, k * P:k * P + P], gT)
                    last[0].then_inc(S["misc_full"], 1)
            pe.wait_ge(S["h_squared"], 3)
            sum_squares("fss", sqh, T)
            pe.wait_ge(S["final_normed"], 8)
            for t, (c, n) in enumerate(TILES):
                for k in range(2):
                    b = free_bank(pe, "yT", 2 * t + k)
                    for i in range(4):
                        turn(b[0:n, i * P:i * P + P], xnT[:, 4 * k + i, c:c + n])
                    close()


_INS = ["x_prompt", "x_sample", "mem_prompt", "state_ssm", "state_mamba_conv", "state_short_conv",
        "cache_mem_k", "cache_mem_v", "norm_mix", "w_in", "w_mconv", "b_mconv", "dt_bias", "a_log", "d_skip",
        "norm_ssm", "w_sconv", "w_out", "norm_xattn", "norm_mem", "w_xq", "w_xk", "w_xv", "w_xo", "norm_moe",
        "w_router", "b_router", "w_gate_up", "b_gate_up", "w_down", "b_down", "norm_final"]
_OUTS = [(1, 256, 1024), (8, 1, 1024), (1, 1, 16, 64, 128), (1, 1, 3, 2048), (1, 1, 2, 1024),
         (1, 1, 256, 4, 256), (1, 1, 256, 4, 256), (1, 8, 16, 64, 128), (1, 8, 3, 2048), (1, 8, 2, 1024)]


def kernel(**inputs):
    import numpy as _np
    import concourse.bacc as _bacc
    from concourse import mybir as _mybir
    from concourse.bass_utils import run_bass_kernel_spmd as _run

    nc = _bacc.Bacc("TRN2", target_bir_lowering=False, num_devices=1)
    arrays, args = {}, {}
    for name in _INS:
        x = _np.ascontiguousarray(inputs[name])
        arrays[f"in_{name}"] = x
        args[name] = nc.dram_tensor(f"in_{name}", x.shape, _mybir.dt.from_np(x.dtype), kind="ExternalInput").ap()
    outs = [nc.dram_tensor(f"out_{i}", shape, _mybir.dt.float32, kind="ExternalOutput").ap()
            for i, shape in enumerate(_OUTS)]
    build(nc, args, outs)
    r = _run(nc, [arrays], core_ids=[0])
    return tuple(r.results[0][f"out_{i}"] for i in range(len(_OUTS)))
```

```python
from contextlib import ExitStack

import concourse.bass as bass
from concourse import mybir

F32 = mybir.dt.float32
I32 = mybir.dt.int32
ALU = mybir.AluOpType
ACT = mybir.ActivationFunctionType
AX = mybir.AxisListType

P = 128
D = 1024
KB = D // P
TP, TS = 256, 8
T = TP + TS
TILES = [(0, 128), (128, 128), (256, 8)]
H, HD, NST, G = 16, 64, 128, 4
CONV = 2048
XB = CONV // P
NM, XH = 256, 4
E, CAP, LIMIT, ALPHA = 32, 64, 7.0, 1.702
PAIRS, MAXP = E // 2, -(-T // CAP)
SLOTS, CW = 4, 512
EPS = 1e-6
A_, D_ = "act", "dve"

PLAN = [("xT", 8, A_), ("xss", 1, A_), ("par0", 1, A_), ("mst", 1, A_), ("sst", 1, A_), ("memT", 4, A_),
        ("dt", 1, D_), ("mss", 1, A_), ("par1", 2, A_), ("proj", 64, A_),
        ("mrow", 4, A_), ("srow", 2, A_), ("acum", 1, D_)]
for _c in range(2):
    PLAN += [(f"xs{_c}", 2, D_), (f"btok{_c}", 1, A_)]
PLAN += [("vp", 2, A_), ("sin", 2, A_), ("fin", 2, A_)]
for _n in range(2 * G + 2):
    if _n < 2 * G:
        PLAN += [("bc", 1, A_), ("sc", 1, D_)]
    if _n == 1:
        PLAN += [("vp", 1, A_)]
    if _n >= 2:
        PLAN += [("y", 1, D_)]
PLAN += [("dec", 1, D_)]
FILL = {1: "vp", 2: "kp", 4: "kp", 5: "kp", 6: "kp"}
for _n in range(TS):
    PLAN += [("bcs", 2, D_)]
    if _n in FILL:
        PLAN += [(FILL[_n], 1, A_)]
PLAN += [("kT", 4, A_), ("gn", 4, A_), ("wo", 8, D_), ("h1ss", 1, A_), ("q", 8, A_), ("att", 4, A_),
         ("qb", 8, D_), ("pT", 4, A_), ("qb", 8, D_), ("o", 2, A_), ("sT", 1, D_), ("o", 2, A_), ("sP", 1, A_),
         ("so", 4, A_), ("sx", 4, A_), ("xo", 8, D_), ("h2ss", 1, A_), ("rt", 1, D_), ("xtok", 6, A_),
         ("rank", 1, D_), ("gtT", 1, D_), ("bd", 8, D_), ("fss", 1, A_), ("yT", 6, A_)]

JOB, WHO, _seen = {}, [], {}
for _n, _k, _w in PLAN:
    for _ in range(_k):
        JOB[_n, _seen.get(_n, 0)] = len(WHO)
        _seen[_n] = _seen.get(_n, 0) + 1
        WHO.append(_w)


def emptied_before(i, who):
    return sum(1 for w in WHO[:i] if w == who)


class Steps:

    def __init__(self, eng, sem):
        self.eng, self.sem, self.n, self.off = eng, sem, 0, 0

    def __call__(self, ins):
        self.n += 1
        ins.then_inc(self.sem, 1)
        self.eng.wait_ge(self.sem, self.off + self.n)


def build(nc, a, outs):
    with ExitStack() as ctx:
        def sb(name, shape, dt=F32):
            return ctx.enter_context(nc.sbuf_tensor(name, shape, dt))

        def sem(name):
            return ctx.enter_context(nc.semaphore(name))

        bank = [ctx.enter_context(nc.psum_tensor(f"bank{i}", [P, 512], F32)) for i in range(8)]

        ring = sb("ring", [P, SLOTS, 8, CW])
        projT = sb("projT", [P, 64, T])
        conv = sb("conv", [P, XB, T])
        hT = sb("hT", [P, KB, T])
        xnT = sb("xnT", [P, KB, T])
        par = sb("par", [P, 6, P])
        bdn = sb("bdn", [E, D])
        flat = sb("flat", [P, 4096])
        mnT = sb("mnT", [P, KB, NM])
        ident, ones, uinc, ustr = (sb(n, [P, P]) for n in ("ident", "ones", "uinc", "ustr"))
        iota = sb("iota", [P, CAP])
        eps = sb("eps", [P, 1])
        wdt = sb("wdt", [P, KB, H])
        wrt = sb("wrt", [P, KB, E])
        dtb, alog, brt = sb("dtb", [P, H]), sb("alog", [P, H]), sb("brt", [P, E])
        dsk = sb("dsk", [P, KB])
        dts = sb("dts", [P, 6, 3, H])
        dta = sb("dta", [P, 3, H])
        small = sb("small", [P, 320])
        rinv = sb("rinv", [P, T])
        npass = sb("npass", [1, 1], I32)

        XBC, Z, GA, SCC, SCV, SCB, GB = 0, 16, 24, 32, 40, 48, 56

        stage = flat[:, 0:1024].rearrange("p (a b) -> p a b", a=8)
        xtokin = flat[:, 1024:4096].rearrange("p (a b) -> p a b", a=3)
        mrows = flat[0:11, 0:2048]
        srows = flat[0:10, 2048:3072]
        memin = projT[:, 0:8, 0:256]
        memv = [projT[:, 4 * i:4 * i + 4, 0:256] for i in range(2)]
        sqx = projT[:, 8:16, :]
        sqm = projT[:, 16:24, 0:NM]
        mstate = conv[0:24, 0:8, 0:256]
        sstate = conv[0:16, 8:12, 0:256]
        msT = sb("msT", [P, XB, 24])
        ssT = sb("ssT", [P, KB, 16])
        tmp = flat[:, 3072:3200].rearrange("p (b n) -> p b n", n=TS)
        r1 = projT[:, 0:16, :].rearrange("p a b -> p (a b)")
        r3 = projT[:, SCC:SCC + 16, :].rearrange("p a b -> p (a b)")
        xdt = r1[:, 0:2048].rearrange("p (c n) -> p c n", c=2)
        btok = r1[:, 2048:3072].rearrange("p (c n) -> p c n", c=2)
        finst = r1[:, 3072:4096].rearrange("p (h n) -> p h n", h=8)
        xdte = flat[:, 0:3072].rearrange("p (v n) -> p v n", v=3)
        sinT = flat[:, 3072:4096]
        dcy = r3[:, 0:1536].rearrange("p (u h l) -> p u h l", u=3, h=4)
        scm = msT[:].rearrange("p b c -> p (b c)").rearrange("p (u l) -> p u l", u=3)
        cexp = flat[:, 0:1024].rearrange("p (u h l) -> p u h l", u=2, h=4)
        dtx = r3[:, 4096:4160].rearrange("p (h b) -> p h b", h=8)
        dec = r3[:, 4160:4224].rearrange("p (h b) -> p h b", h=8)
        yT = projT[:, GB:GB + 8, :]
        sst = r1[:, 0:2048].rearrange("p (u h n) -> p u h n", u=2, h=8)
        prod = r3[:, 0:1024].rearrange("p (h n) -> p h n", h=8)
        ktok = flat[:, 0:2048].rearrange("p (m n) -> p m n", m=2)
        vtok = r3[:, 2048:4096].rearrange("p (m n) -> p m n", m=2)
        kT = mnT
        ubr = projT[:, SCB:SCB + 8, :]
        sqg = conv[:, 0:8, :]
        merged = projT[:, Z:Z + 8, :]
        rgrp = conv[:, 8:12, :]
        qT = projT[:, Z:Z + 8, :]
        pr = flat[:, 0:2048].rearrange("p (t h m) -> p t h m", t=2, h=4)
        pT = flat[:, 2048:4096].rearrange("p (h m t) -> p h m t", h=4, m=2)
        oT = conv[:, 8:16, :]
        junk = projT[:, 0, 0:256]
        scs = projT[:, 1, 0:64]
        sP = projT[0:32, 2, 0:256]
        sPT = projT[:, 3, 0:64].rearrange("p (m c) -> p m c", m=2)
        stok = r1[:, 1000:3048].rearrange("p (g n) -> p g n", g=2)
        sqh = conv[:, 0:8, :]
        moe = projT[:, :, :].rearrange("p a b -> p (a b)")
        at = [0]

        def cut(n):
            at[0] += n
            return moe[:, at[0] - n:at[0]]

        xtok = cut(3 * D).rearrange("p (t n) -> p t n", t=3)
        selT = cut(3 * P).rearrange("p (t n) -> p t n", t=3)
        selG = cut(3 * P).rearrange("p (t n) -> p t n", t=3)
        xg = cut(KB * P).rearrange("p (k n) -> p k n", k=KB)
        gus = cut(4 * 512).rearrange("p (s n) -> p s n", s=4)
        gate, up, sig, act = (cut(KB * P).rearrange("p (k n) -> p k n", k=KB) for _ in range(4))
        ytok = cut(D)
        gtT = cut(T)[0:E, :]
        gT = cut(T)
        moeT = cut(KB * T).rearrange("p (k n) -> p k n", k=KB)
        rkp = cut(3 * (MAXP + 1) * E).rearrange("p (t n) -> p t n", t=3)
        gts = cut(3 * E).rearrange("p (t n) -> p t n", t=3)
        lg = cut(3 * E).rearrange("p (t n) -> p t n", t=3)
        msk = cut(3 * E).rearrange("p (t n) -> p t n", t=3)
        eqm = cut(3 * E).rearrange("p (t n) -> p t n", t=3)
        cum = cut(3 * E).rearrange("p (t n) -> p t n", t=3)
        zer = cut(E)
        top = cut(24).rearrange("p (t n) -> p t n", t=3)
        need = cut(8)
        yout = xtok
        assert at[0] <= 64 * T

        def pcol(i):
            return par[:, i // P, i % P:i % P + 1]

        MW, MB_, SW, NSSM, NMIX, NXA, NMEM, NMOE, NFIN = 0, 64, 80, 104, 112, 120, 128, 136, 144
        bgu = par[:, 2:6, :].rearrange("p a b -> p (a b)")
        bgu = bgu.rearrange("p (e j) -> p e j", j=16)

        bank_filled, act_emptied, dve_emptied = sem("bank_filled"), sem("act_emptied"), sem("dve_emptied")
        act_step, dve_step, pool_step = sem("act_step"), sem("dve_step"), sem("pool_step")
        slot_full = [sem(f"slot_full{i}") for i in range(SLOTS)]
        moe_full = [sem(f"moe_full{i}") for i in range(6)]
        par0_in, par1_in, x_in, mem_in, wdt_in, small_in, conv_in = (sem(n) for n in (
            "par0_in", "par1_in", "x_in", "mem_in", "wdt_in", "small_in", "conv_in"))
        state_in = [sem(f"state_in{u}") for u in range(2)]
        state_out = [sem(f"state_out{u}") for u in range(2)]
        names = ("consts_set", "x_squared", "mem_squared", "x_rms", "mem_rms", "x_normed", "mem_normed",
                 "dt_abs", "dt_exp", "dt_one", "dt_log", "a_exp", "dt_ready", "convolved", "conv_silu",
                 "gated_conv", "gb_sigmoid", "ubr_ready", "raw_used", "cv_ready", "acum_read",
                 "dw_exp", "xdte_ready", "seg_ready", "dcy_ready", "m_ready", "ce_ready",
                 "dec_exp", "dec_ready", "state_new", "z_silu", "ga_sigmoid", "u_ready", "u_squared",
                 "grp_rms", "merged_ready", "h1_ready", "h_squared", "h_rms", "xn_ready",
                 "att_max", "att_exp", "probs_ready", "s_neg", "s_exp", "s_probs", "h2_ready",
                 "lg_ready", "lg_exp", "mask_ready", "rank_ready", "passes_ready",
                 "rows_out", "k_out", "v_out", "fin_out", "y_out", "copy_out",
                 "stage_done", "gu_copied", "turned", "turned_read", "bias_gate", "sig_ready", "h_act",
                 "sel_ready", "xy_full", "xy_copied", "selg_ready", "misc_full", "misc_read",
                 "moe_summed", "final_normed", "state_free", "scratch_free", "sin_ready")
        S = {n: sem(n) for n in names}

        def filled(eng, name, k=0):
            i = JOB[name, k]
            eng.wait_ge(bank_filled, i + 1)
            return bank[i % 8]

        def emptied(eng, name, k=0):
            i = JOB[name, k]
            eng.wait_ge(act_emptied if WHO[i] == A_ else dve_emptied, emptied_before(i + 1, WHO[i]))

        def free_bank(pe, name, k=0):
            i = JOB[name, k]
            if i >= 8:
                w = WHO[i - 8]
                pe.wait_ge(act_emptied if w == A_ else dve_emptied, emptied_before(i - 7, w))
            return bank[i % 8]

        block = ctx.enter_context(nc.Block())

        def wcols(w, c0):
            return w[0].rearrange("(k p) n -> p k n", p=P)[:, :, c0:c0 + CW]

        proj_cols = [1024, 1536, 2048, 2560, 0, 512, 6160, 6672, 4112, 4624, 5136, 5648,
                     3088, 3600, 7184, 7696]
        chunks = [(wcols(a["w_in"], c), ("proj", 4 * i + 3)) for i, c in enumerate(proj_cols)]
        for w, j in (("w_xv", "vp"), ("w_xk", "kp")):
            chunks += [(wcols(a[w], 0), (j, 1)), (wcols(a[w], 512), (j, 3))]
        chunks += [(wcols(a["w_out"], 0), ("wo", 3)), (wcols(a["w_out"], 512), ("wo", 7))]
        chunks += [(wcols(a["w_xq"], 0), ("q", 3)), (wcols(a["w_xq"], 512), ("q", 7))]
        for w, j, per in (("cache_mem_k", "qb", 4), ("cache_mem_v", "so", 0)):
            src = a[w][0].rearrange("b (m p) h d -> p b m (h d)", p=P)
            chunks += [(src[:, 2 * i:2 * i + 2], (j, per * i + per - 1 if per else i // 2 * 2 + 1)) for i in range(4)]
        chunks += [(wcols(a["w_xo"], 0), ("xo", 3)), (wcols(a["w_xo"], 512), ("xo", 7))]
        NCH = len(chunks)
        CH = {"w_xv": 16, "w_xk": 18, "w_out": 20, "w_xq": 22, "k": 24, "v": 28, "w_xo": 32}
        assert NCH == 34

        def slot(i):
            return ring[:, i % SLOTS]

        def chunk_in(eng, i):
            eng.wait_ge(slot_full[i % SLOTS], 16 * (i // SLOTS + 1))
            return slot(i)

        wgu = a["w_gate_up"][0].rearrange("e (k p) n -> e p k n", p=P)
        wdn = a["w_down"][0].rearrange("e (k p) n -> e p k n", p=P)

        mslot = [ring[:, i] for i in range(SLOTS)] + [
            flat[:, 0:4096].rearrange("p (k n) -> p k n", k=8),
            conv[:].rearrange("p a b -> p (a b)")[:, 0:4096].rearrange("p (k n) -> p k n", k=8)]

        def moe_chunk(pair, j):
            w, c = (wgu, j // 2 * CW) if j < 8 else (wdn, (j // 2 - 4) * CW)
            return w[bass.ds(pair * 2 + j % 2, 1), :, :, c:c + CW].rearrange("e p k n -> (e p) k n")

        PARAM_ROWS = [(0, 0, "w_mconv", 64), (0, 64, "b_mconv", 16), (0, 80, "w_sconv", 24), (0, 104, "norm_ssm", 8),
                      (0, 112, "norm_mix", 8), (0, 120, "norm_xattn", 8), (1, 0, "norm_mem", 8),
                      (1, 8, "norm_moe", 8), (1, 16, "norm_final", 8)]

        def param_rows(name):
            src = a[name]
            if len(src.shape) == 3:
                return src.rearrange("l k (b f) -> (l k b) f", f=P)
            if len(src.shape) == 2:
                return src.rearrange("l (b f) -> (l b) f", f=P)
            return src.rearrange("(b f) -> b f", f=P)

        @block.sync
        def _(sp):
            sp.dma_start(xtokin[:, 0:2, :], a["x_prompt"][0].rearrange("(t p) n -> p t n", p=P)).then_inc(x_in, 16)
            sp.dma_start(xtokin[0:TS, 2, :], a["x_sample"].rearrange("b s n -> (b s) n")).then_inc(x_in, 16)
            sp.dma_start(mstate, a["state_mamba_conv"][0].rearrange("b k (c f) -> (b k) c f", f=256)).then_inc(conv_in, 16)
            sp.dma_start(sstate, a["state_short_conv"][0].rearrange("b k (c f) -> (b k) c f", f=256)).then_inc(conv_in, 16)
            for t in range(2):
                sp.dma_start(memv[t], a["mem_prompt"][0, t * P:(t + 1) * P, :].rearrange("p (a n) -> p a n", a=4))\
                    .then_inc(mem_in, 16)
            sp.dma_start(wdt[:], a["w_in"][0].rearrange("(k p) n -> p k n", p=P)[:, :, 3072:3088]).then_inc(wdt_in, 16)
            for i, (src, _) in enumerate(chunks):
                if i == 1:
                    for t, row, name, n in PARAM_ROWS[6:]:
                        sp.dma_start(stage[row:row + n, t, :], param_rows(name)).then_inc(par1_in, 16)
                    sp.dma_start(stage[:, 2:6, :], a["b_gate_up"][0].rearrange("(a e) (b f) -> (e b) a f", a=4, f=P))\
                        .then_inc(par1_in, 16)
                    sp.dma_start(dtb[:], a["dt_bias"][0].partition_broadcast(P)).then_inc(small_in, 16)
                    sp.dma_start(alog[:], a["a_log"][0].partition_broadcast(P)).then_inc(small_in, 16)
                    sp.dma_start(brt[:], a["b_router"][0].partition_broadcast(P)).then_inc(small_in, 16)
                    for y in range(2):
                        sp.dma_start(dsk[64 * y:64 * y + 64, :],
                                     a["d_skip"][0].rearrange("(x y) -> y x", y=2)[y].partition_broadcast(64),
                                     allow_slow_non_contiguous=True).then_inc(small_in, 16)
                    sp.dma_start(wrt[:], a["w_router"][0].rearrange("(k p) n -> p k n", p=P)).then_inc(small_in, 16)
                    sp.dma_start(bdn[:], a["b_down"][0]).then_inc(small_in, 16)
                if i >= SLOTS:
                    name, k = chunks[i - SLOTS][1]
                    if name == "qb":
                        emptied(sp, name, k)
                    else:
                        filled(sp, name, k)
                if 24 <= i < 32:
                    dst = slot(i).rearrange("p (b m n) c -> p b m (n c)", b=2, m=2)
                else:
                    dst = slot(i)
                sp.dma_start(dst, src).then_inc(slot_full[i % SLOTS], 16)
            for j, name, k in ((2, "so", 3), (3, "so", 3), (4, "o", 3), (0, "xo", 3), (1, "xo", 7), (5, "h2ss", 0)):
                filled(sp, name, k)
                sp.dma_start(mslot[j], moe_chunk(0, j)).then_inc(moe_full[j], 16)
            sp.wait_ge(S["passes_ready"], 1)
            n = sp.value_load(npass[0:1, 0:1], min_val=0, max_val=MAXP - 1)
            with sp.Fori(0, n * PAIRS + (PAIRS - 1)) as it:
                for j in range(6, 18):
                    if j % 2 == 0:
                        sp.wait_ge(S["stage_done"], it * 6 + (j // 2 - 2))
                    pair = it % PAIRS if j < 12 else (it + 1) % PAIRS
                    sp.dma_start(mslot[j % 6], moe_chunk(pair, j % 12)).then_inc(moe_full[j % 6], 16)
            for j in range(6, 12):
                if j % 2 == 0:
                    sp.wait_ge(S["stage_done"], n * (6 * PAIRS) + (6 * (PAIRS - 1) + j // 2 - 2))
                src, c = (wgu, j // 2 * CW) if j < 8 else (wdn, (j // 2 - 4) * CW)
                sp.dma_start(mslot[j % 6], src[E - 2 + j % 2, :, :, c:c + CW]).then_inc(moe_full[j % 6], 16)
            for t in range(2):
                emptied(sp, "yT", 2 * t + 1)
                sp.dma_start(outs[0][0, t * P:t * P + P, :], yout[:, t, :]).then_inc(S["y_out"], 16)
            emptied(sp, "yT", 5)
            sp.dma_start(outs[1].rearrange("b s n -> (b s) n"), yout[0:TS, 2, :]).then_inc(S["y_out"], 16)
            sp.wait_ge(S["y_out"], 48)

        @block.gpsimd
        def _(pool):
            st = Steps(pool, pool_step)
            for m in (ident, ones, uinc, ustr):
                st(pool.memset(m[:], 0.0 if m is ident else 1.0))
            st(pool.affine_select(out=ident[:], in_=ident[:], compare_op=ALU.not_equal, fill=1.0, base=0,
                                  pattern=[[-1, P]], channel_multiplier=1))
            for m, op in ((uinc, ALU.is_ge), (ustr, ALU.is_gt)):
                st(pool.affine_select(out=m[:], in_=m[:], compare_op=op, fill=0.0, base=0,
                                      pattern=[[1, P]], channel_multiplier=-1))
            pool.iota(iota[:], pattern=[[1, CAP]], base=0, channel_multiplier=0,
                      allow_small_or_imprecise_dtypes=True).then_inc(S["consts_set"], 1)
            pool.dma_start(outs[8][0, :, 0:2, :], a["state_mamba_conv"][0, :, 1:3, :]).then_inc(S["copy_out"], 16)
            pool.dma_start(outs[9][0, :, 0:1, :], a["state_short_conv"][0, :, 1:2, :]).then_inc(S["copy_out"], 16)
            emptied(pool, "srow", 1)
            pool.dma_start(outs[3][0, 0], mrows[0:3, :]).then_inc(S["rows_out"], 16)
            pool.dma_start(outs[4][0, 0], srows[0:2, :]).then_inc(S["rows_out"], 16)
            pool.dma_start(outs[8][0, :, 2, :], mrows[3:11, :]).then_inc(S["rows_out"], 16)
            pool.dma_start(outs[9][0, :, 1, :], srows[2:10, :]).then_inc(S["rows_out"], 16)
            emptied(pool, "fin", 1)
            pool.dma_start(outs[2][0, 0].rearrange("(x y) p n -> (y p) x n", y=2), finst).then_inc(S["fin_out"], 16)
            sin = a["state_ssm"][0].rearrange("b (x y) p n -> b (y p) x n", y=2)
            sout = outs[7][0].rearrange("b (x y) p n -> b (y p) x n", y=2)
            pool.wait_ge(S["state_free"], 1)
            for b in range(TS + 2):
                if b >= 2:
                    pool.wait_ge(S["state_new"], b - 1)
                    pool.dma_start(sout[b - 2], sst[:, b % 2]).then_inc(state_out[b % 2], 16)
                    pool.wait_ge(state_out[b % 2], 16 * (b // 2))
                if b < TS:
                    if b >= 2:
                        emptied(pool, "bcs", 2 * b - 3)
                    pool.dma_start(sst[:, b % 2], sin[b]).then_inc(state_in[b % 2], 16)
            emptied(pool, "kp", 3)
            pool.dma_start(outs[5][0, 0].rearrange("(m p) h d -> p m (h d)", p=P), ktok).then_inc(S["k_out"], 16)
            emptied(pool, "vp", 3)
            pool.dma_start(outs[6][0, 0].rearrange("(m p) h d -> p m (h d)", p=P), vtok).then_inc(S["v_out"], 16)
            pool.wait_ge(S["k_out"], 16)
            pool.wait_ge(S["v_out"], 16)
            pool.wait_ge(S["fin_out"], 16)
            pool.wait_ge(S["rows_out"], 64)
            pool.wait_ge(S["copy_out"], 32)

        @block.scalar
        def _(s):
            st = Steps(s, act_step)

            def copy(out, in_, scale=1.0):
                return s.activation(out, in_, ACT.Copy, scale=scale)

            def done(ins):
                return ins.then_inc(act_emptied, 1)

            for t, row, name, n in PARAM_ROWS[:6]:
                s.dma_start(stage[row:row + n, t, :], param_rows(name)).then_inc(par0_in, 16)
            for k in range(8):
                b = filled(s, "xT", k)
                done(copy(hT[:, k, :], b[:, 0:T]))
            def root(name, out, n, div=D):
                b = filled(s, name)
                done(s.activation(out, b[:, 0:n], ACT.Sqrt, bias=eps[:, 0:1], scale=1.0 / div))

            s.wait_ge(S["consts_set"], 2)
            root("xss", rinv[:], T)
            b = filled(s, "par0")
            done(copy(par[:, 0, :], b[:, 0:P]))
            b = filled(s, "mst")
            done(copy(msT[:], b[:, 0:384].rearrange("p (b c) -> p b c", b=XB)))
            b = filled(s, "sst")
            done(copy(ssT[:], b[:, 0:128].rearrange("p (b c) -> p b c", b=8)))
            for k in range(4):
                b = filled(s, "memT", k)
                done(copy(mnT[:, 2 * k:2 * k + 2, :], b[:, :].rearrange("p (a n) -> p a n", a=2)))
            emptied(s, "memT", 3)
            s.activation(sqm, mnT[:], ACT.Square).then_inc(S["mem_squared"], 1)
            root("mss", small[:, 0:NM], NM)
            b = filled(s, "par1", 0)
            st(copy(par[:, 1, 0:24], b[:, 0:24]))
            done(copy(par[:, 2, :], b[:, P:2 * P]))
            b = filled(s, "par1", 1)
            done(copy(par[:, 3:6, :], b[:, 0:3 * P].rearrange("p (a n) -> p a n", a=3)))
            s.wait_ge(S["dt_abs"], 1)
            s.activation(dts[:, 1], dts[:, 1], ACT.Exp, scale=-1.0).then_inc(S["dt_exp"], 1)
            s.wait_ge(small_in, 112)
            s.activation(alog[:], alog[:], ACT.Exp).then_inc(S["a_exp"], 1)
            s.wait_ge(S["dt_one"], 1)
            s.activation(dts[:, 3], dts[:, 2], ACT.Ln).then_inc(S["dt_log"], 1)

            def proj_blocks(n0, groups):
                base = JOB["proj", 0] + n0
                with s.Fori(0, groups) as g:
                    for j in range(8):
                        s.wait_ge(bank_filled, g * 8 + (base + j + 1))
                        copy(projT[:, bass.ds(g * 8 + (n0 + j), 1), :].rearrange("p a n -> p (a n)"),
                             bank[(base + j) % 8][:, 0:T]).then_inc(act_emptied, 1)

            proj_blocks(0, 2)
            proj_blocks(16, 2)
            emptied(s, "proj", 31)
            s.wait_ge(S["convolved"], 1)
            s.activation(conv[:], conv[:], ACT.Silu).then_inc(S["conv_silu"], 1)
            s.activation(projT[:, Z:Z + 8, :], projT[:, Z:Z + 8, :], ACT.Silu).then_inc(S["z_silu"], 1)
            s.activation(projT[:, GA:GA + 8, :], projT[:, GA:GA + 8, :], ACT.Sigmoid).then_inc(S["ga_sigmoid"], 1)
            proj_blocks(32, 4)
            emptied(s, "proj", 63)
            s.activation(projT[:, GB:GB + 8, :], projT[:, GB:GB + 8, :], ACT.Sigmoid).then_inc(S["gb_sigmoid"], 1)
            for k in range(4):
                b = filled(s, "mrow", k)
                done(copy(mrows[:, 512 * k:512 * k + 512], b[0:11, :]))
            for k in range(2):
                b = filled(s, "srow", k)
                done(copy(srows[:, 512 * k:512 * k + 512], b[0:10, :]))
            s.wait_ge(S["acum_read"], 1)
            s.activation(small[:, 64:112], small[:, 64:112], ACT.Exp).then_inc(S["dw_exp"], 1)
            for c in range(2):
                b = filled(s, f"btok{c}")
                done(copy(btok[:, c, :], b[:, :]))

            def copy_kv(name, k):
                b = filled(s, name, k)
                dst = ktok if name == "kp" else vtok
                done(copy(dst[:, k % 2, k // 2 * 512:k // 2 * 512 + 512], b[:, :]))

            s.wait_ge(S["ubr_ready"], 1)
            copy_kv("vp", 0)
            copy_kv("vp", 1)
            for k in range(2):
                b = filled(s, "sin", k)
                done(copy(sinT[:, 512 * k:512 * k + 512], b[:, :]))
            for k in range(2):
                b = filled(s, "fin", k)
                done(copy(finst[:, 4 * k:4 * k + 4, :], b[:, :].rearrange("p (h n) -> p h n", h=4)))
            for n in range(2 * G):
                if n == 2:
                    copy_kv("vp", 2)
                b = filled(s, "bc", n)
                s.wait_ge(S["seg_ready"], n + 1)
                ins = s.activation(dcy[:, n % 3], dcy[:, n % 3], ACT.Exp)
                if n < G:
                    done(ins)
                else:
                    ins.then_inc(S["dcy_ready"], 1)
                    filled(s, "y", n - 2)
                    done(s.activation(cexp[:, n % 2], b[:, :].rearrange("p (h l) -> p h l", h=4), ACT.Exp))
            emptied(s, "dec")
            s.activation(dec, dec, ACT.Exp).then_inc(S["dec_ready"], 1)
            copy_kv("vp", 3)
            for k in range(4):
                copy_kv("kp", k)
            for k in range(4):
                b = filled(s, "kT", k)
                done(copy(kT[:, 2 * k:2 * k + 2, :], b[:, :].rearrange("p (a n) -> p a n", a=2)))
            for k in range(KB):
                s.wait_ge(S["u_ready"], k + 1)
                s.activation(sqg[:, k, :], yT[:, k, :], ACT.Square).then_inc(S["u_squared"], 1)
            for g in range(G):
                b = filled(s, "gn", g)
                done(s.activation(rgrp[:, g, :], b[:, 0:T], ACT.Sqrt, bias=eps[:, 0:1], scale=1.0 / 256))

            def square_h(name):
                for k in range(KB):
                    emptied(s, name, k)
                    s.activation(sqh[:, k, :], hT[:, k, :], ACT.Square).then_inc(S["h_squared"], 1)

            square_h("wo")
            root("h1ss", rinv[:], T)
            for k in range(8):
                b = filled(s, "q", k)
                done(copy(qT[:, k, :], b[:, 0:T], 1.0 / 16))
            s.wait_ge(S["k_out"], 16)
            for t in range(2):
                for hh in range(2):
                    n = 2 * t + hh
                    b = filled(s, "att", n)
                    s.wait_ge(S["att_max"], n + 1)
                    for h in range(2):
                        j = 8 * t + 2 * hh + h
                        ins = s.activation(pr[:, t, 2 * hh + h, :], b[:, h * 256:h * 256 + 256], ACT.Exp,
                                           bias=small[:, j:j + 1], accum_out=small[:, 16 + j:17 + j])
                        if h == 0:
                            st(ins)
                    done(ins)
            for h in range(4):
                b = filled(s, "pT", h)
                done(copy(pT[:, h], b[:, :].rearrange("p (m t) -> p m t", m=2)))

            def copy_o(k):
                b = filled(s, "o", k)
                done(copy(oT[:, 2 * k:2 * k + 2, 0:TP], b[:, :].rearrange("p (a t) -> p a t", a=2)))

            copy_o(0)
            copy_o(1)
            emptied(s, "sT")
            s.activation(sP, sP, ACT.Exp, bias=small[0:32, 32:33], accum_out=small[0:32, 33:34]).then_inc(S["s_exp"], 1)
            copy_o(2)
            copy_o(3)
            b = filled(s, "sP")
            done(copy(sPT, b[:, 0:64].rearrange("p (m c) -> p m c", m=2)))
            for i in range(4):
                b = filled(s, "so", i)
                done(copy(stok[:, i // 2, i % 2 * 512:i % 2 * 512 + 512], b[:, :]))
            for i in range(4):
                b = filled(s, "sx", i)
                for j in range(2):
                    h = 2 * (i % 2) + j
                    ins = copy(oT[:, 2 * h:2 * h + 2, TP + i // 2 * 4:TP + i // 2 * 4 + 4],
                               b[:, :].rearrange("p (a c) -> p a c", a=4)
                               [:, 2 * j:2 * j + 2, 16 * (i // 2) + h:16 * (i // 2) + h + 109:36])
                    if j == 0:
                        st(ins)
                done(ins)
            square_h("xo")
            root("h2ss", rinv[:], T)
            s.wait_ge(S["lg_ready"], 1)
            s.activation(gts, gts, ACT.Exp).then_inc(S["lg_exp"], 1)
            for t, (_, n) in enumerate(TILES):
                for k in range(2):
                    b = filled(s, "xtok", 2 * t + k)
                    done(copy(xtok[0:n, t, 512 * k:512 * k + 512], b[0:n, :]))

            for k, name in enumerate(("gu_copied", "gu_copied")):
                s.activation(small[:, 300 + k:301 + k], eps[:], ACT.Copy).then_inc(S[name], 1)

            def gathered(n):
                for k in range(2):
                    s.wait_ge(S["xy_full"], n + (k + 1))
                    copy(xg[:, 4 * k:4 * k + 4, :], bank[4 + k][:, :].rearrange("p (a n) -> p a n", a=4))\
                        .then_inc(S["xy_copied"], 1)

            gathered(0)
            s.wait_ge(S["passes_ready"], 1)
            n = s.value_load(npass[0:1, 0:1], min_val=0, max_val=MAXP - 1)
            with s.Fori(0, n * PAIRS + PAIRS) as it:
                for k in range(4):
                    s.wait_ge(S["stage_done"], it * 6 + (k + 1))
                    copy(gus[:, k], bank[k % 2][:, :]).then_inc(S["gu_copied"], 1)
                    if k in (1, 2):
                        h = k - 1
                        s.wait_ge(S["bias_gate"], it * 2 + (h + 1))
                        s.activation(sig[:, 4 * h:4 * h + 4], gate[:, 4 * h:4 * h + 4], ACT.Sigmoid, scale=ALPHA)\
                            .then_inc(S["sig_ready"], 1)
                gathered(it * 2 + 2)
                for k in range(2):
                    s.wait_ge(S["stage_done"], it * 6 + (k + 5))
                    copy(ytok[:, 512 * k:512 * k + 512], bank[4 + k][:, :]).then_inc(S["xy_copied"], 1)
            s.wait_ge(S["moe_summed"], 1)
            for k in range(KB):
                s.activation(sqh[:, k, :], moeT[:, k, :], ACT.Square).then_inc(S["h_squared"], 1)
            root("fss", rinv[:], T)
            for t, (_, n) in enumerate(TILES):
                for k in range(2):
                    b = filled(s, "yT", 2 * t + k)
                    done(copy(yout[0:n, t, 512 * k:512 * k + 512], b[0:n, :]))

        @block.vector
        def _(v):
            st = Steps(v, dve_step)

            def done(ins):
                return ins.then_inc(dve_emptied, 1)

            def bc(x, n):
                return x.unsqueeze(2).to_broadcast([x.shape[0], x.shape[1], n])

            st(v.memset(small[:], 0.0))
            st(v.memset(dts[:], 0.0))
            v.memset(eps[:], EPS).then_inc(S["consts_set"], 1)

            for k in range(KB):
                emptied(v, "xT", k)
                v.tensor_tensor(out=sqx[:, k, :], in0=hT[:, k, :], in1=hT[:, k, :], op=ALU.mult)\
                    .then_inc(S["x_squared"], 1)

            def norm(name, dst, src, r, n, gain, out):
                emptied(v, name)
                st(v.reciprocal(r, r))
                for k in range(KB):
                    v.scalar_tensor_tensor(out=dst[:, k, 0:n], in0=src[:, k, 0:n], scalar=pcol(gain + k), in1=r,
                                           op0=ALU.mult, op1=ALU.mult).then_inc(S[out], 1)

            emptied(v, "par0")
            norm("xss", xnT, hT, rinv[:], T, NMIX, "x_normed")
            emptied(v, "par1", 0)
            norm("mss", mnT, mnT, small[:, 0:NM], NM, NMEM, "mem_normed")
            v.wait_ge(S["mem_normed"], 8)

            v.wait_ge(small_in, 112)
            b = filled(v, "dt")
            st(v.tensor_tensor(out=dts[:, 0, 0:2], in0=b[:, 0:32].rearrange("p (t h) -> p t h", t=2),
                               in1=dtb[:].unsqueeze(1).to_broadcast([P, 2, H]), op=ALU.add))
            done(v.tensor_tensor(out=dts[0:TS, 0, 2], in0=b[0:TS, 32:48], in1=dtb[0:TS, :], op=ALU.add))
            emptied(v, "dt")
            v.scalar_tensor_tensor(out=dts[:, 1], in0=dts[:, 0], scalar=-1.0, in1=dts[:, 0], op0=ALU.mult, op1=ALU.max).then_inc(S["dt_abs"], 1)
            v.wait_ge(S["dt_exp"], 1)
            v.tensor_scalar(dts[:, 2], dts[:, 1], 1.0, None, ALU.add).then_inc(S["dt_one"], 1)
            v.wait_ge(S["dt_one"], 1)
            st(v.tensor_scalar(dts[:, 4], dts[:, 2], -1.0, None, ALU.add))
            st(v.tensor_scalar(dts[:, 5], dts[:, 4], 0.0, None, ALU.is_equal))
            st(v.tensor_tensor(out=dts[:, 4], in0=dts[:, 4], in1=dts[:, 5], op=ALU.add))
            st(v.reciprocal(dts[:, 4], dts[:, 4]))
            v.wait_ge(S["dt_log"], 1)
            st(v.tensor_tensor(out=dts[:, 3], in0=dts[:, 3], in1=dts[:, 5], op=ALU.add))
            st(v.tensor_tensor(out=dts[:, 3], in0=dts[:, 3], in1=dts[:, 4], op=ALU.mult))
            st(v.tensor_tensor(out=dts[:, 3], in0=dts[:, 3], in1=dts[:, 1], op=ALU.mult))
            st(v.scalar_tensor_tensor(out=dts[:, 0], in0=dts[:, 0], scalar=0.0, in1=dts[:, 3],
                                      op0=ALU.max, op1=ALU.add))
            v.wait_ge(S["a_exp"], 1)
            v.scalar_tensor_tensor(out=dta[:], in0=dts[:, 0], scalar=-1.0,
                                   in1=alog[:].unsqueeze(1).to_broadcast([P, 3, H]),
                                   op0=ALU.mult, op1=ALU.mult).then_inc(S["dt_ready"], 1)

            def blk_of(buf, i, c0, c1):
                return buf[:, bass.ds(i, 1), c0:c1].rearrange("p a n -> p (a n)")

            def weight(i):
                return par[:, 0, bass.ds(i, 1)]

            n0, before = st.n, emptied_before(JOB["proj", 0], A_)
            with v.Fori(0, XB) as blk:
                st.n, st.off = n0, blk * 4
                v.wait_ge(act_emptied, blk + (before + 1))
                st(v.tensor_scalar(blk_of(conv, blk, 0, T), blk_of(projT, blk, 0, T),
                                   weight(blk + 48), weight(blk + MB_), ALU.mult, ALU.add))
                for d in range(1, 4):
                    st(v.scalar_tensor_tensor(out=blk_of(conv, blk, d, TP), in0=blk_of(projT, blk, 0, TP - d),
                                              scalar=weight(blk + 16 * (3 - d)), in1=blk_of(conv, blk, d, TP),
                                              op0=ALU.mult, op1=ALU.add))
            st.n, st.off = n0 + 4 * XB, 0
            emptied(v, "mst")
            old = msT[:].rearrange("p b (s k) -> p b s k", k=3)
            for k in range(3):
                st(v.tensor_tensor(out=tmp, in0=old[:, :, :, k], in1=bc(par[:, 0, 16 * k:16 * k + 16], TS),
                                   op=ALU.mult))
                ins = v.tensor_tensor(out=conv[:, :, TP:T], in0=conv[:, :, TP:T], in1=tmp, op=ALU.add)
                if k < 2:
                    st(ins)
            ins.then_inc(S["convolved"], 1)

            emptied(v, "proj", 47)
            v.tensor_tensor(out=projT[:, SCC:SCC + 8, :], in0=projT[:, SCC:SCC + 8, :],
                            in1=projT[:, SCV:SCV + 8, :], op=ALU.mult).then_inc(S["cv_ready"], 1)
            v.wait_ge(S["cv_ready"], 1)
            n0 = st.n
            with v.Fori(0, KB) as blk:
                st.n, st.off = n0, blk * 3
                st(v.tensor_scalar(blk_of(projT, blk + SCV, 0, T), blk_of(projT, blk + SCC, 0, T),
                                   weight(blk + (SW + 16)), None, ALU.mult))
                for d in range(1, 3):
                    st(v.scalar_tensor_tensor(out=blk_of(projT, blk + SCV, d, TP), in0=blk_of(projT, blk + SCC, 0, TP - d),
                                              scalar=weight(blk + (SW + 8 * (2 - d))), in1=blk_of(projT, blk + SCV, d, TP),
                                              op0=ALU.mult, op1=ALU.add))
            st.n, st.off = n0 + 3 * KB, 0
            u = projT[:, SCV:SCV + 8, :]
            emptied(v, "sst")
            old = ssT[:].rearrange("p b (s k) -> p b s k", k=2)
            v.wait_ge(S["convolved"], 1)
            for k in range(2):
                st(v.tensor_tensor(out=tmp[:, 0:8], in0=old[:, :, :, k],
                                   in1=bc(par[:, 0, SW + 8 * k:SW + 8 * k + 8], TS), op=ALU.mult))
                st(v.tensor_tensor(out=u[:, :, TP:T], in0=u[:, :, TP:T], in1=tmp[:, 0:8], op=ALU.add))
            emptied(v, "proj", 63)
            st(v.tensor_tensor(out=ubr, in0=ubr, in1=u, op=ALU.mult))
            v.wait_ge(S["gb_sigmoid"], 1)
            v.tensor_tensor(out=ubr, in0=ubr, in1=projT[:, GB:GB + 8, :], op=ALU.mult).then_inc(S["ubr_ready"], 1)
            v.wait_ge(S["ubr_ready"], 1)

            b = filled(v, "acum")
            done(v.tensor_copy(small[:, 0:64], b[:, 0:64]))
            emptied(v, "acum")
            st(v.tensor_tensor(out=small[:, 64:80], in0=small[:, 32:48], in1=small[:, 0:16], op=ALU.subtract))
            st(v.tensor_tensor(out=small[:, 80:96], in0=small[:, 64:80], in1=small[:, 48:64], op=ALU.add))
            v.tensor_tensor(out=small[:, 96:112], in0=small[:, 48:64], in1=small[:, 16:32],
                            op=ALU.subtract).then_inc(S["acum_read"], 1)

            def heads(x, n):
                return x.rearrange("p (h n) -> p h n", h=n)

            v.wait_ge(S["rows_out"], 64)
            for c in range(2):
                for k in range(2):
                    b = filled(v, f"xs{c}", k)
                    done(v.tensor_tensor(out=heads(xdt[:, c, 512 * k:512 * k + 512], 8), in0=heads(b[:, :], 8),
                                         in1=bc(dts[:, 0, c, 8 * k:8 * k + 8], HD), op=ALU.mult))
                emptied(v, f"xs{c}", 1)
                v.wait_ge(S["dw_exp"], 1)
                for i in ((0, 1), (2,))[c]:
                    v.tensor_tensor(out=heads(xdte[:, i], H), in0=heads(xdt[:, c], H),
                                    in1=bc(small[:, 64 + 16 * i:80 + 16 * i], HD), op=ALU.mult)\
                        .then_inc(S["xdte_ready"], 1)
            for n in range(2 * G + 2):
                if n < 2 * G:
                    c, g = divmod(n, G)
                    b = filled(v, "sc", n)
                    done(v.tensor_tensor(out=scm[:, n % 3], in0=b[:, 0:P], in1=uinc[:], op=ALU.mult))
                    b = bank[JOB["bc", n] % 8]
                    for i in range(4):
                        j = 16 * c + 4 * g + i
                        ins = v.tensor_scalar(dcy[:, n % 3, i, :], b[:, i * P:i * P + P], small[:, j:j + 1], 0.0,
                                              ALU.subtract, ALU.min)
                    ins.then_inc(S["seg_ready"], 1)
                if 1 <= n <= 2 * G:
                    m, g = n - 1, (n - 1) % G
                    if m < G:
                        emptied(v, "bc", m)
                    else:
                        v.wait_ge(S["dcy_ready"], m - G + 1)
                    emptied(v, "sc", m)
                    v.tensor_tensor(out=dcy[:, m % 3], in0=dcy[:, m % 3],
                                    in1=scm[:, m % 3].unsqueeze(1).to_broadcast([P, 4, P]),
                                    op=ALU.mult).then_inc(S["m_ready"], 1)
                    if m >= G:
                        emptied(v, "bc", m)
                        v.tensor_tensor(out=cexp[:, m % 2], in0=cexp[:, m % 2],
                                        in1=conv[:, 12 + g, P:2 * P].unsqueeze(1).to_broadcast([P, 4, P]),
                                        op=ALU.mult).then_inc(S["ce_ready"], 1)
                if n >= 2:
                    c, g = divmod(n - 2, G)
                    cols = slice(c * P, c * P + P)
                    b = filled(v, "y", n - 2)
                    for i in range(2):
                        ins = v.scalar_tensor_tensor(out=yT[:, 2 * g + i, cols], in0=conv[:, 2 * g + i, cols],
                                                     scalar=dsk[:, 2 * g + i:2 * g + i + 1],
                                                     in1=b[:, i * P:i * P + P], op0=ALU.mult, op1=ALU.add)
                    done(ins)
            emptied(v, "y", 2 * G - 1)
            st(v.memset(tmp[:, 0:8], 0.0))
            v.memset(tmp[:, 8:16], 0.0).then_inc(S["state_free"], 1)

            xs_s = conv[:, 0:8, TP:T]
            b = filled(v, "dec")
            st(v.tensor_tensor(out=dtx, in0=xs_s, in1=b[:, 0:64].rearrange("p (h s) -> p h s", h=8), op=ALU.mult))
            done(v.tensor_copy(dec, b[:, 64:128].rearrange("p (h s) -> p h s", h=8)))
            v.wait_ge(S["dec_ready"], 1)

            def by_group(x):
                return x.rearrange("p (g y) n -> p g y n", y=2)

            def rows_of(b):
                return b[:, :].rearrange("p (g n) -> p g n", g=G).unsqueeze(2).to_broadcast([P, G, 2, P])

            for i in range(TS):
                s_ = sst[:, i % 2]
                v.wait_ge(state_in[i % 2], 16 * (i // 2 + 1))
                st(v.tensor_tensor(out=s_, in0=s_, in1=bc(dec[:, :, i], P), op=ALU.mult))
                b = filled(v, "bcs", 2 * i)
                done(v.tensor_tensor(out=by_group(prod), in0=rows_of(b), in1=by_group(bc(dtx[:, :, i], P)), op=ALU.mult))
                emptied(v, "bcs", 2 * i)
                v.tensor_tensor(out=s_, in0=s_, in1=prod, op=ALU.add).then_inc(S["state_new"], 1)
                v.wait_ge(S["state_new"], i + 1)
                b = filled(v, "bcs", 2 * i + 1)
                done(v.tensor_tensor(out=by_group(prod), in0=rows_of(b), in1=by_group(s_), op=ALU.mult))
                emptied(v, "bcs", 2 * i + 1)
                st(v.tensor_reduce(yT[:, :, TP + i], prod, AX.X, ALU.add))
            st(v.tensor_tensor(out=dtx, in0=xs_s, in1=bc(dsk[:, :], TS), op=ALU.mult))
            v.tensor_tensor(out=yT[:, :, TP:T], in0=yT[:, :, TP:T], in1=dtx, op=ALU.add).then_inc(S["scratch_free"], 1)
            v.wait_ge(S["scratch_free"], 1)
            v.wait_ge(S["z_silu"], 1)
            for k in range(KB):
                v.tensor_tensor(out=yT[:, k, :], in0=yT[:, k, :], in1=projT[:, Z + k, :], op=ALU.mult)\
                    .then_inc(S["u_ready"], 1)
            v.wait_ge(S["ga_sigmoid"], 1)
            for g in range(G):
                emptied(v, "gn", g)
                v.wait_ge(S["u_squared"], 2 * g + 2)
                st(v.reciprocal(rgrp[:, g, :], rgrp[:, g, :]))
                for k in (2 * g, 2 * g + 1):
                    st(v.scalar_tensor_tensor(out=yT[:, k, :], in0=yT[:, k, :], scalar=pcol(NSSM + k),
                                              in1=rgrp[:, g, :], op0=ALU.mult, op1=ALU.mult))
                    st(v.tensor_tensor(out=merged[:, k, :], in0=yT[:, k, :], in1=projT[:, GA + k, :], op=ALU.mult))
                    v.tensor_tensor(out=merged[:, k, :], in0=merged[:, k, :], in1=ubr[:, k, :], op=ALU.add)\
                        .then_inc(S["merged_ready"], 1)

            def add_to_h(name):
                for k in range(KB):
                    b = filled(v, name, k)
                    done(v.tensor_tensor(out=hT[:, k, :], in0=b[:, 0:T], in1=hT[:, k, :], op=ALU.add))
                emptied(v, name, 7)

            add_to_h("wo")
            norm("h1ss", xnT, hT, rinv[:], T, NXA, "xn_ready")
            for n in range(4):
                t, hh = n // 2, n % 2
                j = 8 * t + 2 * hh
                b = filled(v, "att", n)
                v.tensor_reduce(small[:, j:j + 2], b[:, :].rearrange("p (h m) -> p h m", h=2), AX.X, ALU.max,
                                negate=True).then_inc(S["att_max"], 1)
            for u in range(2):
                v.wait_ge(state_out[u], 16 * (TS // 2))
            for i in range(TS):
                if i == 2:
                    for t in range(2):
                        emptied(v, "att", 2 * t + 1)
                        r = small[:, 16 + 8 * t:20 + 8 * t]
                        st(v.reciprocal(r, r))
                        v.tensor_tensor(out=pr[:, t], in0=pr[:, t], in1=bc(r, 256), op=ALU.mult).then_inc(S["probs_ready"], 1)
                keys = chunk_in(v, CH["k"] + i // 2).rearrange("p (b m n) c -> p b m (n c)", b=2, m=2)
                for hh in range(2):
                    b = filled(v, "qb", 2 * i + hh)
                    for h in range(2):
                        for m in range(2):
                            c = m * 32 + i * 4 + 2 * hh + h
                            ins = v.tensor_tensor_reduce(junk, keys[:, i % 2, m, (2 * hh + h) * 256:(2 * hh + h + 1) * 256],
                                                         b[:, h * 256:h * 256 + 256], 1.0, 0.0, ALU.mult, ALU.add,
                                                         scs[:, c:c + 1])
                            if h + m < 2:
                                st(ins)
                    done(ins)
                    emptied(v, "qb", 2 * i + hh)
            b = filled(v, "sT")
            st(v.tensor_reduce(small[0:32, 32:33], b[0:32, 0:256], AX.X, ALU.max, negate=True))
            done(v.tensor_copy(sP, b[0:32, 0:256]))
            v.wait_ge(S["s_exp"], 1)
            st(v.reciprocal(small[0:32, 33:34], small[0:32, 33:34]))
            v.tensor_scalar(sP, sP, small[0:32, 33:34], None, ALU.mult).then_inc(S["s_probs"], 1)
            add_to_h("xo")
            norm("h2ss", xnT, hT, rinv[:], T, NMOE, "xn_ready")

            v.wait_ge(S["v_out"], 16)
            v.wait_ge(S["fin_out"], 16)
            st(v.memset(eqm, 0.0))
            st(v.memset(zer, 0.0))
            st(v.memset(lg, 0.0))
            b = filled(v, "rt")
            for t, (_, n) in enumerate(TILES):
                ins = v.tensor_tensor(out=lg[0:n, t], in0=b[0:n, t * E:t * E + E], in1=brt[0:n, :], op=ALU.add)
            done(ins)
            emptied(v, "rt")
            for t in range(3):
                ins = v.max(top[:, t], lg[:, t])
            st(ins)
            v.tensor_tensor(out=gts, in0=lg, in1=top[:, :, 0:1].to_broadcast([P, 3, E]), op=ALU.subtract)\
                .then_inc(S["lg_ready"], 1)
            fourth = top[:, :, 3:4].to_broadcast([P, 3, E])
            v.tensor_tensor(out=eqm, in0=lg, in1=fourth, op=ALU.is_equal)
            st(v.tensor_tensor(out=msk, in0=lg, in1=fourth, op=ALU.is_gt))
            st(v.tensor_reduce(need[:, 0:3], msk, AX.X, ALU.add))
            st(v.tensor_scalar(need[:, 0:3], need[:, 0:3], -1.0, 4.0, ALU.mult, ALU.add))
            for t in range(3):
                ins = v.tensor_tensor_scan(cum[:, t], eqm[:, t], zer, 0.0, ALU.add, ALU.add)
            st(ins)
            st(v.tensor_tensor(out=cum, in0=cum, in1=bc(need[:, 0:3], E), op=ALU.is_le))
            st(v.tensor_tensor(out=eqm, in0=eqm, in1=cum, op=ALU.mult))
            v.tensor_tensor(out=msk, in0=msk, in1=eqm, op=ALU.add).then_inc(S["mask_ready"], 1)
            v.wait_ge(S["mask_ready"], 1)
            v.wait_ge(S["lg_exp"], 1)
            st(v.tensor_tensor(out=gts, in0=gts, in1=msk, op=ALU.mult))
            st(v.tensor_reduce(need[:, 4:7], gts, AX.X, ALU.add))
            st(v.reciprocal(need[:, 4:7], need[:, 4:7]))
            st(v.tensor_tensor(out=gts, in0=gts, in1=bc(need[:, 4:7], E), op=ALU.mult))
            b = filled(v, "rank")
            for t, (_, n) in enumerate(TILES):
                st(v.scalar_tensor_tensor(out=eqm[0:n, t], in0=b[0:n, t * E:t * E + E], scalar=1.0, in1=msk[0:n, t],
                                          op0=ALU.add, op1=ALU.mult))
            done(v.tensor_reduce(small[0:1, 0:1], b[0:1, 3 * E:4 * E], AX.X, ALU.max))
            for p in range(MAXP + 1):
                st(v.tensor_scalar(rkp[:, :, p * E:p * E + E], eqm, -1.0 - CAP * p, None, ALU.add))
            emptied(v, "rank")
            st(v.tensor_scalar(small[0:1, 1:2], small[0:1, 0:1], float(CAP), None, ALU.is_gt))
            for p in range(2, MAXP):
                st(v.scalar_tensor_tensor(out=small[0:1, 1:2], in0=small[0:1, 0:1], scalar=float(CAP * p),
                                          in1=small[0:1, 1:2], op0=ALU.is_gt, op1=ALU.add))
            v.tensor_copy(npass[0:1, 0:1], small[0:1, 1:2]).then_inc(S["passes_ready"], 1)

            def select(it, gated):
                dst = selG if gated else selT
                for t, (_, n) in enumerate(TILES):
                    for j in range(2):
                        g = gts[0:n, t, bass.ds((it % PAIRS) * 2 + j, 1)] if gated else None
                        ins = v.tensor_scalar(dst[0:n, t, j * CAP:j * CAP + CAP], iota[0:n, :],
                                              rkp[0:n, t, bass.ds(it * 2 + j, 1)], g,
                                              ALU.is_equal, ALU.mult if gated else ALU.bypass)
                ins.then_inc(S["selg_ready" if gated else "sel_ready"], 1)

            b = filled(v, "gtT")
            done(v.tensor_copy(gtT, b[0:E, 0:T]))
            for k in range(KB):
                b = filled(v, "bd", k)
                done(v.tensor_tensor(out=moeT[:, k, :], in0=b[:, 0:T], in1=hT[:, k, :], op=ALU.add))
            for k, name in enumerate(("turned_read", "turned_read", "misc_read", "misc_read")):
                v.memset(small[:, 304 + k:305 + k], 0.0).then_inc(S[name], 1)
            v.wait_ge(S["consts_set"], 2)
            select(0, False)
            v.wait_ge(S["turned_read"], 2)
            v.wait_ge(S["misc_read"], 2)
            emptied(v, "bd", 7)
            v.wait_ge(S["passes_ready"], 1)
            n = v.value_load(npass[0:1, 0:1], min_val=0, max_val=MAXP - 1)
            n0 = st.n

            def biased(dst, h, pair, off, k):
                v.wait_ge(S["turned"], it * 4 + (k + 1))
                v.tensor_tensor(out=dst[:, 4 * h:4 * h + 4, :].rearrange("p b (e c) -> p b e c", e=2),
                                in0=bank[2 + k % 2][:, :].rearrange("p (b e c) -> p b e c", b=4, e=2),
                                in1=bgu[:, bass.ds(pair * 2, 2), off + 4 * h:off + 4 * h + 4]
                                .rearrange("p e b -> p b e").unsqueeze(3).to_broadcast([P, 4, 2, CAP]),
                                op=ALU.add).then_inc(S["turned_read"], 1)
                v.wait_ge(S["turned_read"], it * 4 + (k + 3))
                return dst[:, 4 * h:4 * h + 4]

            with v.Fori(0, n * PAIRS + PAIRS) as it:
                st.n, st.off = n0, it * 4
                pair = it % PAIRS
                for h in range(2):
                    x = biased(gate, h, pair, 0, h)
                    v.tensor_scalar(x, x, LIMIT, None, ALU.min).then_inc(S["bias_gate"], 1)
                v.wait_ge(S["xy_full"], it * 2 + 2)
                select(it + 1, False)
                select(it, True)
                for h in range(2):
                    x = biased(up, h, pair, 8, 2 + h)
                    st(v.tensor_scalar(x, x, LIMIT, -LIMIT, ALU.min, ALU.max))
                    v.wait_ge(S["bias_gate"], it * 2 + (h + 1))
                    st(v.scalar_tensor_tensor(out=x, in0=x, scalar=1.0, in1=gate[:, 4 * h:4 * h + 4],
                                              op0=ALU.add, op1=ALU.mult))
                    v.wait_ge(S["sig_ready"], it * 2 + (h + 1))
                    v.tensor_tensor(out=act[:, 4 * h:4 * h + 4], in0=x, in1=sig[:, 4 * h:4 * h + 4],
                                    op=ALU.mult).then_inc(S["h_act"], 1)
                for k in range(10):
                    b = bank[6 + k % 2]
                    v.wait_ge(S["misc_full"], it * 10 + (k + 1))
                    if k == 0:
                        ins = v.tensor_copy(gT[:, 0:P], b[:, 0:P])
                    elif k == 1:
                        ins = v.tensor_copy(gT[:, P:T], b[:, 0:T - P])
                    else:
                        ins = v.tensor_tensor(out=moeT[:, k - 2, :], in0=b[:, 0:T], in1=moeT[:, k - 2, :], op=ALU.add)
                    ins.then_inc(S["misc_read"], 1)
            v.wait_ge(S["misc_read"], n * (10 * PAIRS) + (10 * PAIRS + 2))
            v.memset(small[:, 310:311], 0.0).then_inc(S["moe_summed"], 1)
            norm("fss", xnT, moeT, rinv[:], T, NFIN, "final_normed")

        @block.tensor
        def _(pe):
            last = [None]

            def mm(out, lhsT, rhs, start=True, stop=True):
                last[0] = pe.matmul(out, lhsT, rhs, start=start, stop=stop)
                return last[0]

            def close():
                last[0].then_inc(bank_filled, 1)

            def turn(out, in_):
                k = in_.shape[0]
                last[0] = pe.transpose(out, in_, ident[0:k, 0:k])

            pe.wait_ge(S["consts_set"], 2)
            pe.wait_ge(x_in, 32)
            for k in range(KB):
                b = free_bank(pe, "xT", k)
                for t, (c, n) in enumerate(TILES):
                    turn(b[:, c:c + n], xtokin[0:n, t, k * P:k * P + P])
                close()

            def sum_squares(name, sq, n, ready, count, rows=range(KB), b=None):
                b = free_bank(pe, name) if b is None else b
                for k in rows:
                    pe.wait_ge(S[ready], count(k))
                    mm(b[:, 0:n], ones[:], sq[:, k, 0:n], k == 0, k == KB - 1)
                if KB - 1 in rows:
                    close()
                return b

            sum_squares("xss", sqx, T, "x_squared", lambda k: k + 1)
            pe.wait_ge(par0_in, 16 * 6)
            b = free_bank(pe, "par0")
            turn(b[:, 0:P], stage[:, 0, :])
            close()
            pe.wait_ge(conv_in, 32)
            b = free_bank(pe, "mst")
            for i in range(XB):
                turn(b[:, i * 24:i * 24 + 24], mstate[:, i // 2, (i % 2) * P:(i % 2) * P + P])
            close()
            b = free_bank(pe, "sst")
            for i in range(KB):
                turn(b[:, i * 16:i * 16 + 16], sstate[:, i // 2, (i % 2) * P:(i % 2) * P + P])
            close()
            pe.wait_ge(mem_in, 32)
            for k in range(4):
                b = free_bank(pe, "memT", k)
                for i in range(2):
                    for t in range(2):
                        turn(b[:, i * 256 + t * P:i * 256 + t * P + P], memv[t][:, k, i * P:i * P + P])
                close()
            pe.wait_ge(S["x_normed"], 8)
            pe.wait_ge(wdt_in, 16)
            b = free_bank(pe, "dt")
            for t, (c, n) in enumerate(TILES):
                for k in range(KB):
                    mm(b[0:n, t * H:t * H + H], xnT[:, k, c:c + n], wdt[:, k, :], k == 0, k == KB - 1)
            close()
            sum_squares("mss", sqm, NM, "mem_squared", lambda k: 1)
            pe.wait_ge(par1_in, 16 * 4)
            b = free_bank(pe, "par1", 0)
            turn(b[:, 0:24], stage[0:24, 1, :])
            turn(b[:, P:2 * P], stage[:, 2, :])
            close()
            b = free_bank(pe, "par1", 1)
            for i in range(3):
                turn(b[:, i * P:i * P + P], stage[:, 3 + i, :])
            close()
            base = JOB["proj", 0]
            before = emptied_before(base, A_)
            with pe.Fori(0, 4) as it:
                for j in range(16):
                    if j % 4 == 0:
                        pe.wait_ge(slot_full[j // 4], it * 16 + 16)
                    if base + j - 8 == JOB["dt", 0]:
                        emptied(pe, "dt")
                    pe.wait_ge(act_emptied, it * 16 + (emptied_before(base + j - 7, A_) if j < 8 else before + j - 7))
                    for k in range(KB):
                        mm(bank[(base + j) % 8][:, 0:T], ring[:, j // 4, k, (j % 4) * P:(j % 4) * P + P], xnT[:, k, :],
                           k == 0, k == KB - 1)
                    close()

            def project(name, chunk, rhs, ready, count, squares=None, squared=0):
                n, sums = rhs.shape[2], None
                for j in range(KB):
                    if j % 4 == 0:
                        w = chunk_in(pe, chunk + j // 4)
                    b = free_bank(pe, name, j)
                    for k in range(KB):
                        if j == 0 and ready:
                            pe.wait_ge(S[ready], count + k + 1)
                        mm(b[:, 0:n], w[:, k, (j % 4) * P:(j % 4) * P + P], rhs[:, k, :], k == 0, k == KB - 1)
                    close()
                    if squares and j >= 2:
                        sums = sum_squares(squares, sqh, T, "h_squared", lambda k: squared + k + 1,
                                           range(j - 2, j - 1), sums)
                if squares:
                    sum_squares(squares, sqh, T, "h_squared", lambda k: squared + k + 1, range(KB - 2, KB), sums)

            emptied(pe, "proj", 63)
            for k in range(4):
                b = free_bank(pe, "mrow", k)
                for i in range(4):
                    turn(b[0:11, i * P:i * P + P], projT[:, 4 * k + i, T - 11:T])
                close()
            pe.wait_ge(S["cv_ready"], 1)
            for k in range(2):
                b = free_bank(pe, "srow", k)
                for i in range(4):
                    turn(b[0:10, i * P:i * P + P], projT[:, SCC + 4 * k + i, T - 10:T])
                close()
            pe.wait_ge(S["dt_ready"], 1)
            b = free_bank(pe, "acum")
            for c in range(2):
                mm(b[:, c * H:c * H + H], uinc[:], dta[:, c, :])
                mm(b[:, 32 + c * H:32 + c * H + H], ones[:], dta[:, c, :])
            close()
            pe.wait_ge(S["conv_silu"], 1)
            for c in range(2):
                cols = slice(c * P, c * P + P)
                for k in range(2):
                    b = free_bank(pe, f"xs{c}", k)
                    for i in range(4):
                        turn(b[:, i * P:i * P + P], conv[:, 4 * k + i, cols])
                    close()
                b = free_bank(pe, f"btok{c}")
                for i in range(4):
                    turn(b[:, i * P:i * P + P], conv[:, 8 + i, cols])
                close()
            def project_kv(name, k):
                w = chunk_in(pe, CH["w_x" + name[0]] + k // 2)
                mt = k % 2
                b = free_bank(pe, name, k)
                for i in range(KB):
                    mm(b[:, :], mnT[:, i, mt * P:mt * P + P], w[:, i, :], i == 0, i == KB - 1)
                close()

            pe.wait_ge(S["mem_normed"], 8)
            project_kv("vp", 0)
            project_kv("vp", 1)
            emptied(pe, "btok1")
            pe.wait_ge(S["xdte_ready"], 3)
            for k in range(2):
                b = free_bank(pe, "sin", k)
                for i in range(2):
                    g = 2 * k + i
                    mm(b[:, i * 256:i * 256 + 256], btok[:, 0, g * P:g * P + P], xdte[:, 0, g * 256:g * 256 + 256])
                close()
            for k in range(2):
                b = free_bank(pe, "fin", k)
                for i in range(4):
                    h = 4 * k + i
                    for c in range(2):
                        mm(b[:, i * P:i * P + P], xdte[:, 1 + c, h * P:h * P + P],
                           btok[:, c, (h // 2) * P:(h // 2) * P + P], c == 0, c == 1)
                close()
            emptied(pe, "sin", 1)
            for n in range(2 * G + 2):
                if n < 2 * G:
                    c, g = divmod(n, G)
                    cols = slice(c * P, c * P + P)
                    b = free_bank(pe, "bc", n)
                    for i in range(4):
                        mm(b[:, i * P:i * P + P], dta[:, c, 4 * g + i:4 * g + i + 1].to_broadcast([P, P]), uinc[:])
                    close()
                    b = free_bank(pe, "sc", n)
                    mm(b[:, 0:P], conv[:, 8 + g, cols], conv[:, 12 + g, cols])
                    close()
                if n == 1:
                    project_kv("vp", 2)
                if n >= 2:
                    m = n - 2
                    c, g = divmod(m, G)
                    b = free_bank(pe, "y", m)
                    pe.wait_ge(S["m_ready"], m + 1)
                    if c == 1:
                        pe.wait_ge(S["ce_ready"], g + 1)
                    for i in range(4):
                        h = 4 * g + i
                        out = b[64 * (i % 2):64 * (i % 2) + 64, (i // 2) * P:(i // 2) * P + P]
                        mm(out, xdt[:, c, h * HD:h * HD + HD], dcy[:, m % 3, i, :], True, c == 0)
                        if c == 1:
                            mm(out, sinT[:, h * HD:h * HD + HD], cexp[:, m % 2, i, :], False, True)
                    close()
            b = free_bank(pe, "dec")
            for i in range(KB):
                for j, src in enumerate((dts[0:TS, 0, 2], dta[0:TS, 2])):
                    for y in range(2):
                        mm(b[HD * y:HD * y + HD, 64 * j + 8 * i:64 * j + 8 * i + 8],
                           src[:, 2 * i + y:2 * i + y + 1].to_broadcast([TS, HD]), ident[0:TS, 0:TS])
            close()
            for i in range(TS):
                for j in range(2):
                    b = free_bank(pe, "bcs", 2 * i + j)
                    for g in range(G):
                        mm(b[:, g * P:g * P + P], conv[:, 8 + 4 * j + g, TP + i:TP + i + 1].to_broadcast([P, P]), ident[:])
                    close()
                if i in FILL:
                    project_kv(FILL[i], sum(1 for j in FILL if j < i and FILL[j] == FILL[i]) + 3 * (FILL[i] == "vp"))
            emptied(pe, "kp", 3)
            for k in range(4):
                b = free_bank(pe, "kT", k)
                for i in range(2):
                    for mt in range(2):
                        turn(b[:, i * 256 + mt * P:i * 256 + mt * P + P],
                             ktok[:, mt, (2 * k + i) * P:(2 * k + i + 1) * P])
                close()
            for g in range(G):
                b = free_bank(pe, "gn", g)
                for k in range(2):
                    pe.wait_ge(S["u_squared"], 2 * g + k + 1)
                    mm(b[:, 0:T], ones[:], sqg[:, 2 * g + k, :], k == 0, k == 1)
                close()
            project("wo", CH["w_out"], merged, "merged_ready", 0, "h1ss", 0)
            project("q", CH["w_xq"], xnT, "xn_ready", 0)
            emptied(pe, "q", 7)
            emptied(pe, "kT", 3)
            for t in range(2):
                for hh in range(2):
                    b = free_bank(pe, "att", 2 * t + hh)
                    for i in range(2):
                        h = 2 * hh + i
                        for k in range(2):
                            mm(b[:, i * 256:i * 256 + 256], qT[:, 2 * h + k, t * P:t * P + P], kT[:, 2 * h + k, :],
                               k == 0, k == 1)
                    close()
            def spread_queries(samples):
                for i in samples:
                    for hh in range(2):
                        b = free_bank(pe, "qb", 2 * i + hh)
                        for k in range(4):
                            mm(b[:, k * P:k * P + P], qT[:, 4 * hh + k, TP + i:TP + i + 1].to_broadcast([P, P]), ident[:])
                        close()

            def weigh_values(blocks):
                for k in blocks:
                    b = free_bank(pe, "o", k)
                    for i in range(2):
                        for mt in range(2):
                            mm(b[:, i * 256:i * 256 + 256], vtok[:, mt, (2 * k + i) * P:(2 * k + i + 1) * P],
                               pT[:, k, mt, :], mt == 0, mt == 1)
                    close()

            spread_queries(range(4))
            pe.wait_ge(S["probs_ready"], 2)
            for h in range(4):
                b = free_bank(pe, "pT", h)
                for mt in range(2):
                    for t in range(2):
                        turn(b[:, mt * 256 + t * P:mt * 256 + t * P + P], pr[:, t, h, mt * P:mt * P + P])
                close()
            spread_queries(range(4, TS))
            emptied(pe, "vp", 3)
            emptied(pe, "pT", 3)
            weigh_values((0, 1))
            emptied(pe, "qb", 15)
            b = free_bank(pe, "sT")
            for m in range(2):
                turn(b[0:32, m * P:m * P + P], scs[:, m * 32:m * 32 + 32])
            close()
            weigh_values((2, 3))
            pe.wait_ge(S["s_probs"], 1)
            b = free_bank(pe, "sP")
            for m in range(2):
                turn(b[:, m * 32:m * 32 + 32], sP[:, m * P:m * P + P])
            close()
            emptied(pe, "sP")
            for grp in range(2):
                vals = [chunk_in(pe, CH["v"] + 2 * grp + i).rearrange("p (b m n) c -> p b m (n c)", b=2, m=2)
                        for i in range(2)]
                for hh in range(2):
                    b = free_bank(pe, "so", 2 * grp + hh)
                    for m in range(2):
                        for q in range(4):
                            mm(b[32 * q:32 * q + 32, :], sPT[:, m, :], vals[q // 2][:, q % 2, m, hh * 512:hh * 512 + 512],
                               m == 0, m == 1)
                    close()
            for i in range(4):
                emptied(pe, "so", i)
                b = free_bank(pe, "sx", i)
                for k in range(4):
                    c = i % 2 * 512 + k * P
                    turn(b[:, k * P:k * P + P], stok[:, i // 2, c:c + P])
                close()
            emptied(pe, "sx", 3)
            project("xo", CH["w_xo"], oT, None, 0, "h2ss", 8)
            pe.wait_ge(S["xn_ready"], 16)
            b = free_bank(pe, "rt")
            for t, (c, n) in enumerate(TILES):
                for k in range(KB):
                    mm(b[0:n, t * E:t * E + E], xnT[:, k, c:c + n], wrt[:, k, :], k == 0, k == KB - 1)
            close()
            for t, (c, n) in enumerate(TILES):
                for k in range(2):
                    b = free_bank(pe, "xtok", 2 * t + k)
                    for i in range(4):
                        turn(b[0:n, i * P:i * P + P], xnT[:, 4 * k + i, c:c + n])
                    close()
            pe.wait_ge(S["mask_ready"], 1)
            b = free_bank(pe, "rank")
            for t, (_, n) in enumerate(TILES):
                for u in range(t):
                    mm(b[0:n, t * E:t * E + E], ones[:, 0:n], msk[:, u], u == 0, False)
                mm(b[0:n, t * E:t * E + E], ustr[0:n, 0:n], msk[0:n, t], t == 0, True)
            for t, (_, n) in enumerate(TILES):
                mm(b[:, 3 * E:4 * E], ones[0:n, :], msk[0:n, t], t == 0, t == 2)
            close()
            emptied(pe, "xtok", 5)
            emptied(pe, "rank")

            b = free_bank(pe, "gtT")
            for t, (c, n) in enumerate(TILES):
                turn(b[0:E, c:c + n], gts[0:n, t, :])
            close()
            emptied(pe, "gtT")
            for k in range(KB):
                b = free_bank(pe, "bd", k)
                mm(b[:, 0:T], bdn[:, k * P:k * P + P], gtT)
                close()
            emptied(pe, "bd", 7)

            def gather(n, m=None):
                pe.wait_ge(S["sel_ready"], n)
                for h in range(2):
                    if m is not None:
                        pe.wait_ge(S["xy_copied"], m + (h + 1))
                    for k in range(4 * h, 4 * h + 4):
                        for t, (_, r) in enumerate(TILES):
                            mm(bank[4 + h][:, (k % 4) * P:(k % 4) * P + P], xtok[0:r, t, k * P:k * P + P],
                               selT[0:r, t, :], t == 0, t == 2)
                    last[0].then_inc(S["xy_full"], 1)

            gather(1)
            pe.wait_ge(S["passes_ready"], 1)
            n = pe.value_load(npass[0:1, 0:1], min_val=0, max_val=MAXP - 1)
            with pe.Fori(0, n * PAIRS + PAIRS) as it:

                def stream(stage, b, stationary, halves=False):
                    for e in range(2):
                        j = 2 * stage + e
                        pe.wait_ge(moe_full[j % 6], it * 32 + 16 * (j // 6 + 1))
                    for k in range(KB):
                        if halves and k % 4 == 0:
                            pe.wait_ge(S["h_act"], it * 2 + (k // 4 + 1))
                        for e in range(2):
                            mm(b[64 * e:64 * e + 64, :], stationary[:, k, 64 * e:64 * e + 64],
                               mslot[(2 * stage + e) % 6][:, k, :], k == 0, k == KB - 1)
                    last[0].then_inc(S["stage_done"], 1)

                def turn_half(k):
                    pe.wait_ge(S["gu_copied"], it * 4 + (k + 3))
                    pe.wait_ge(S["turned_read"], it * 4 + (k + 1))
                    for i in range(4):
                        turn(bank[2 + k % 2][:, i * P:i * P + P], gus[:, k, i * P:i * P + P])
                    last[0].then_inc(S["turned"], 1)

                def misc(k):
                    pe.wait_ge(S["misc_read"], it * 10 + (k + 1))
                    return bank[6 + k % 2]

                pe.wait_ge(S["xy_copied"], it * 4 + 2)
                for k in range(4):
                    pe.wait_ge(S["gu_copied"], it * 4 + (k + 1))
                    stream(k, bank[k % 2], xg)
                    if k:
                        turn_half(k - 1)
                gather(it + 2, it * 4)
                turn_half(3)
                pe.wait_ge(S["selg_ready"], it + 1)
                b = misc(0)
                turn(b[:, 0:P], selG[:, 0, :])
                last[0].then_inc(S["misc_full"], 1)
                b = misc(1)
                turn(b[:, 0:P], selG[:, 1, :])
                turn(b[:, P:P + TS], selG[0:TS, 2, :])
                last[0].then_inc(S["misc_full"], 1)
                for k in range(2):
                    pe.wait_ge(S["xy_copied"], it * 4 + (k + 3))
                    stream(4 + k, bank[4 + k], act, halves=True)
                pe.wait_ge(S["misc_read"], it * 10 + 4)
                for k in range(KB):
                    if k % 4 == 0:
                        pe.wait_ge(S["xy_copied"], it * 4 + (5 + k // 4))
                    b = misc(2 + k)
                    mm(b[:, 0:T], ytok[:, k * P:k * P + P], gT)
                    last[0].then_inc(S["misc_full"], 1)
            sum_squares("fss", sqh, T, "h_squared", lambda k: 16 + k + 1)
            for t, (c, n) in enumerate(TILES):
                for k in range(2):
                    b = free_bank(pe, "yT", 2 * t + k)
                    pe.wait_ge(S["final_normed"], 4 * k + 4)
                    for i in range(4):
                        turn(b[0:n, i * P:i * P + P], xnT[:, 4 * k + i, c:c + n])
                    close()


_INS = ["x_prompt", "x_sample", "mem_prompt", "state_ssm", "state_mamba_conv", "state_short_conv",
        "cache_mem_k", "cache_mem_v", "norm_mix", "w_in", "w_mconv", "b_mconv", "dt_bias", "a_log", "d_skip",
        "norm_ssm", "w_sconv", "w_out", "norm_xattn", "norm_mem", "w_xq", "w_xk", "w_xv", "w_xo", "norm_moe",
        "w_router", "b_router", "w_gate_up", "b_gate_up", "w_down", "b_down", "norm_final"]
_OUTS = [(1, 256, 1024), (8, 1, 1024), (1, 1, 16, 64, 128), (1, 1, 3, 2048), (1, 1, 2, 1024),
         (1, 1, 256, 4, 256), (1, 1, 256, 4, 256), (1, 8, 16, 64, 128), (1, 8, 3, 2048), (1, 8, 2, 1024)]


def kernel(**inputs):
    import numpy as _np
    import concourse.bacc as _bacc
    from concourse import mybir as _mybir
    from concourse.bass_utils import run_bass_kernel_spmd as _run

    nc = _bacc.Bacc("TRN2", target_bir_lowering=False, num_devices=1)
    arrays, args = {}, {}
    for name in _INS:
        x = _np.ascontiguousarray(inputs[name])
        arrays[f"in_{name}"] = x
        args[name] = nc.dram_tensor(f"in_{name}", x.shape, _mybir.dt.from_np(x.dtype), kind="ExternalInput").ap()
    outs = [nc.dram_tensor(f"out_{i}", shape, _mybir.dt.float32, kind="ExternalOutput").ap()
            for i, shape in enumerate(_OUTS)]
    build(nc, args, outs)
    r = _run(nc, [arrays], core_ids=[0])
    return tuple(r.results[0][f"out_{i}"] for i in range(len(_OUTS)))
```
